# Optimizing a Trainium2 kernel written in Bass

```python
import math
import jax, jax.numpy as jnp
from jax import lax
import numpy as np

D_MODEL = 1024
BATCH = 1
SEQ = 512
DEPTH = 1
DEC_BATCH = 8
DEC_SEQ = 8
PAST_LEN = 1024
PAGE_SIZE = 128

H_NSA = 8
DK = 64
G_KV = 2
HPG = H_NSA // G_KV
KV_SLOTS = 4
CMP_STRIDE = 16
CMP_BLOCK = 2 * CMP_STRIDE
SLC_BLOCK = 64
N_SELECT = 16
WINDOW = 512
Q_BLOCK = 128
H_GLA = 4
DK_GLA = 64
DV_GLA = 128
GATE_RANK = 16
GATE_TAU = 16.0
GLA_CHUNK = 64
N_BUCKETS = 32
MAX_DISTANCE = 128
PEER_HEADS = 8
N_KEYS = 128
N_EXPERTS = N_KEYS * N_KEYS
PEER_QDIM = 256
PEER_TOPK = 16
PEER_BLOCK = 128

EPS = 1e-6
NEG = -1e30
FORCE = 1e4
IN_SIZES = (H_NSA * DK,) + (G_KV * DK,) * 6 + (3 * H_NSA, H_GLA * DK_GLA, H_GLA * DK_GLA, H_GLA * DV_GLA, GATE_RANK, H_GLA * DV_GLA)
D_IN = sum(IN_SIZES)
D_MIX = H_NSA * DK + H_GLA * DV_GLA

kernel_name = 'hybrid_nsa_gla_peer_step'

def rmsnorm(x, g):
    xf = x.astype(jnp.float32)
    xf = xf * lax.rsqrt(jnp.mean(xf * xf, axis=-1, keepdims=True) + EPS)
    return (xf * g.astype(jnp.float32)).astype(x.dtype)

def split_cols(a):
    offs = []
    acc = 0
    for s in IN_SIZES[:-1]:
        acc += s
        offs.append(acc)
    return jnp.split(a, offs, axis=-1)

def t5_bucket(d):
    n = jnp.maximum(d, 0)
    max_exact = N_BUCKETS // 2
    nf = jnp.maximum(n, max_exact).astype(jnp.float32)
    large = max_exact + (jnp.log(nf / max_exact) / math.log(MAX_DISTANCE / max_exact) * (N_BUCKETS - max_exact)).astype(jnp.int32)
    return jnp.where(n < max_exact, n, jnp.minimum(large, N_BUCKETS - 1))

def head_bias(rel_bias, d):
    b = rel_bias[t5_bucket(d)].astype(jnp.float32)
    return b.reshape(d.shape + (G_KV, HPG)).transpose(2, 3, 0, 1)

def compress(x_tok, w_pos, proj):
    B, Tk = x_tok.shape[:2]
    n_sub = Tk // CMP_STRIDE
    sub = x_tok[:, :n_sub * CMP_STRIDE].reshape(B, n_sub, CMP_STRIDE, G_KV, DK)
    first = jnp.einsum('bnjgd,gj->bngd', sub, w_pos[:, :CMP_STRIDE])
    second = jnp.einsum('bnjgd,gj->bngd', sub, w_pos[:, CMP_STRIDE:])
    blk = first[:, :-1] + second[:, 1:]
    return jnp.einsum('bngd,gde->bnge', blk, proj)

def nsa_global(q, kc_tok, vc_tok, ks_tok, vs_tok, q_pos, cmp_w_pos, cmp_proj, kn_cmp_g, rel_bias):
    B, Tq = q.shape[:2]
    Tk = ks_tok.shape[1]
    scale = DK ** -0.5
    qg = q.reshape(B, Tq, G_KV, HPG, DK)
    kc = rmsnorm(compress(kc_tok, cmp_w_pos[0], cmp_proj[0]), kn_cmp_g)
    vc = compress(vc_tok, cmp_w_pos[1], cmp_proj[1])
    n_cmp = kc.shape[1]
    blk_end = jnp.arange(n_cmp, dtype=jnp.int32) * CMP_STRIDE + (CMP_BLOCK - 1)
    d_cmp = q_pos[:, None] - blk_end[None, :]
    mask = d_cmp >= 0
    logits = jnp.einsum('btghd,bngd->bghtn', qg, kc).astype(jnp.float32) * scale + head_bias(rel_bias, d_cmp)
    p_cmp = jax.nn.softmax(jnp.where(mask, logits, NEG), axis=-1) * mask
    o_cmp = jnp.einsum('bghtn,bngd->btghd', p_cmp.astype(vc.dtype), vc).reshape(B, Tq, H_NSA, DK)
    n_slc = -(-Tk // SLC_BLOCK)
    ratio = SLC_BLOCK // CMP_STRIDE
    p_grp = p_cmp.sum(axis=2)
    p_ext = jnp.pad(p_grp, ((0, 0), (0, 0), (0, 0), (1, ratio * n_slc + ratio - n_cmp - 1)))
    p_slc = p_ext[..., :ratio * n_slc].reshape(B, G_KV, Tq, n_slc, ratio).sum(-1) + p_ext[..., ratio::ratio]
    j = jnp.arange(n_slc, dtype=jnp.int32)[None, :]
    cur = (q_pos // SLC_BLOCK)[:, None]
    valid = j * SLC_BLOCK <= q_pos[:, None]
    forced = (j == 0) | (j == cur) | (j == cur - 1)
    score = jnp.where(forced, FORCE, jnp.where(valid, p_slc, -FORCE))
    k_sel = min(N_SELECT, n_slc)
    _, sel = lax.top_k(score, k_sel)
    pad_len = n_slc * SLC_BLOCK - Tk
    def to_blocks(a):
        a = jnp.pad(a, ((0, 0), (0, pad_len), (0, 0), (0, 0)))
        return a.reshape(B, n_slc, SLC_BLOCK, G_KV, DK).transpose(0, 3, 1, 2, 4)
    ks_b = to_blocks(ks_tok)
    vs_b = to_blocks(vs_tok)
    rb = rel_bias.reshape(N_BUCKETS, G_KV, HPG).transpose(1, 0, 2)
    bi = jnp.arange(B)[:, None, None, None]
    gi = jnp.arange(G_KV)[None, :, None, None]
    gi5 = jnp.arange(G_KV)[None, :, None, None, None]
    qb_len = math.gcd(Tq, Q_BLOCK)
    nblk = Tq // qb_len
    q_blocks = jnp.moveaxis(qg.reshape(B, nblk, qb_len, G_KV, HPG, DK), 1, 0)
    sel_blocks = jnp.moveaxis(sel.reshape(B, G_KV, nblk, qb_len, k_sel), 2, 0)
    pos_blocks = q_pos.reshape(nblk, qb_len)
    def slc_block(args):
        qb, sb, pb = args
        kg = ks_b[bi, gi, sb]
        vg = vs_b[bi, gi, sb]
        kpos = sb[..., None] * SLC_BLOCK + jnp.arange(SLC_BLOCK, dtype=jnp.int32)
        d = pb[None, None, :, None, None] - kpos
        bias = jnp.moveaxis(rb[gi5, t5_bucket(d)], -1, 2).astype(jnp.float32)
        logits = jnp.einsum('bqghd,bgqkld->bghqkl', qb, kg).astype(jnp.float32) * scale + bias
        logits = jnp.where((d >= 0)[:, :, None], logits, NEG)
        shp = logits.shape
        p = jax.nn.softmax(logits.reshape(shp[:4] + (-1,)), axis=-1).reshape(shp)
        return jnp.einsum('bghqkl,bgqkld->bqghd', p.astype(vg.dtype), vg)
    o_slc = lax.map(slc_block, (q_blocks, sel_blocks, pos_blocks))
    o_slc = jnp.moveaxis(o_slc, 0, 1).reshape(B, Tq, H_NSA, DK)
    return o_cmp, o_slc

def window_attn(q, kw, vw, kbuf, vbuf, q_pos, rel_bias):
    B, Tq = q.shape[:2]
    Pw = kbuf.shape[1]
    n_pad = WINDOW - Pw
    zpad = jnp.zeros((B, n_pad, G_KV, DK), kw.dtype)
    keys = jnp.concatenate([zpad, kbuf.astype(kw.dtype), kw], axis=1)
    vals = jnp.concatenate([zpad, vbuf.astype(vw.dtype), vw], axis=1)
    idx = jnp.arange(WINDOW + Tq, dtype=jnp.int32)
    k_pos = q_pos[0] - WINDOW + idx
    k_ok = idx >= n_pad
    qb_len = math.gcd(Tq, Q_BLOCK)
    nblk = Tq // qb_len
    span = WINDOW + qb_len
    scale = DK ** -0.5
    qg = q.reshape(B, Tq, G_KV, HPG, DK)
    def block(b):
        s = b * qb_len
        kb = lax.dynamic_slice_in_dim(keys, s, span, axis=1)
        vb = lax.dynamic_slice_in_dim(vals, s, span, axis=1)
        kp = lax.dynamic_slice_in_dim(k_pos, s, span)
        ok = lax.dynamic_slice_in_dim(k_ok, s, span)
        qb = lax.dynamic_slice_in_dim(qg, s, qb_len, axis=1)
        qp = lax.dynamic_slice_in_dim(q_pos, s, qb_len)
        d = qp[:, None] - kp[None, :]
        mask = ok[None, :] & (d >= 0) & (d < WINDOW)
        logits = jnp.einsum('bqghd,bsgd->bghqs', qb, kb).astype(jnp.float32) * scale + head_bias(rel_bias, d)
        p = jax.nn.softmax(jnp.where(mask, logits, NEG), axis=-1)
        return jnp.einsum('bghqs,bsgd->bqghd', p.astype(vb.dtype), vb)
    o = lax.map(block, jnp.arange(nblk, dtype=jnp.int32))
    return jnp.moveaxis(o, 0, 1).reshape(B, Tq, H_NSA, DK)

def gla_scan(q, k, v, log_a, s0):
    B, T = q.shape[:2]
    C = math.gcd(T, GLA_CHUNK)
    n = T // C
    def chunks(a):
        return a.astype(jnp.float32).reshape(B, n, C, H_GLA, a.shape[-1]).transpose(1, 0, 3, 2, 4)
    causal = jnp.tril(jnp.ones((C, C), dtype=bool))[:, :, None]
    def step(S, inp):
        qc, kc, vc, ac = inp
        b = jnp.cumsum(ac, axis=2)
        o_inter = jnp.einsum('bhtk,bhkv->bhtv', qc * jnp.exp(b), S)
        diff = b[:, :, :, None, :] - b[:, :, None, :, :]
        decay = jnp.exp(jnp.where(causal, diff, -jnp.inf))
        attn = jnp.einsum('bhtk,bhsk,bhtsk->bhts', qc, kc, decay)
        o_intra = jnp.einsum('bhts,bhsv->bhtv', attn, vc)
        b_last = b[:, :, -1:, :]
        S_new = jnp.exp(b_last[:, :, 0, :])[..., None] * S + jnp.einsum('bhsk,bhsv->bhkv', kc * jnp.exp(b_last - b), vc)
        return S_new, o_inter + o_intra
    S, o = lax.scan(step, s0.astype(jnp.float32), (chunks(q), chunks(k), chunks(v), chunks(log_a)))
    return o.transpose(1, 0, 3, 2, 4).reshape(B, T, H_GLA, v.shape[-1]), S

def peer(h, peer_wq, peer_qn_g, peer_k1, peer_k2, peer_u, peer_v):
    B, T, D = h.shape
    n_tok = B * T
    nb = math.gcd(n_tok, PEER_BLOCK)
    half = PEER_QDIM // 2
    def block(xb):
        q = rmsnorm((xb @ peer_wq).reshape(nb, PEER_HEADS, PEER_QDIM), peer_qn_g)
        s1 = jnp.einsum('nhd,hkd->nhk', q[..., :half], peer_k1).astype(jnp.float32)
        s2 = jnp.einsum('nhd,hkd->nhk', q[..., half:], peer_k2).astype(jnp.float32)
        v1, i1 = lax.top_k(s1, PEER_TOPK)
        v2, i2 = lax.top_k(s2, PEER_TOPK)
        cand = (v1[..., :, None] + v2[..., None, :]).reshape(nb, PEER_HEADS, PEER_TOPK * PEER_TOPK)
        score, ci = lax.top_k(cand, PEER_TOPK)
        expert = jnp.take_along_axis(i1, ci // PEER_TOPK, axis=-1) * N_KEYS + jnp.take_along_axis(i2, ci % PEER_TOPK, axis=-1)
        gate = jax.nn.softmax(score, axis=-1)
        u_e = peer_u[expert]
        v_e = peer_v[expert]
        act = jax.nn.gelu(jnp.einsum('nd,nhkd->nhk', xb, u_e).astype(jnp.float32), approximate=False)
        return jnp.einsum('nhk,nhkd->nd', (gate * act).astype(v_e.dtype), v_e)
    y = lax.map(block, h.reshape(n_tok // nb, nb, D))
    return y.reshape(B, T, D).astype(h.dtype)

def layer(x, past_kv, win_kv, gla_state, p):
    B, T, _ = x.shape
    pos0 = past_kv.shape[1]
    q_pos = pos0 + jnp.arange(T, dtype=jnp.int32)
    h = rmsnorm(x, p['norm1_g'])
    q_n, kc, vc, ks, vs, kw, vw, gate_logit, q_g, k_g, v_g, a_low, r_g = split_cols(h @ p['w_in'])
    kv_shape = (B, T, G_KV, DK)
    q_n = rmsnorm(q_n.reshape(B, T, H_NSA, DK), p['qn_g'])
    ks = rmsnorm(ks.reshape(kv_shape), p['kn_slc_g'])
    kw = rmsnorm(kw.reshape(kv_shape), p['kn_win_g'])
    kc = kc.reshape(kv_shape)
    vc = vc.reshape(kv_shape)
    vs = vs.reshape(kv_shape)
    vw = vw.reshape(kv_shape)
    new_kv = jnp.stack([kc, vc, ks, vs], axis=2)
    full_kv = jnp.concatenate([past_kv.astype(new_kv.dtype), new_kv], axis=1)
    o_cmp, o_slc = nsa_global(q_n, full_kv[:, :, 0], full_kv[:, :, 1], full_kv[:, :, 2], full_kv[:, :, 3], q_pos,
                              p['cmp_w_pos'], p['cmp_proj'], p['kn_cmp_g'], p['rel_bias'])
    o_win = window_attn(q_n, kw, vw, win_kv[:, :, 0], win_kv[:, :, 1], q_pos, p['rel_bias'])
    g = jax.nn.sigmoid(gate_logit.astype(jnp.float32) + p['nsa_gate_b'].astype(jnp.float32)).reshape(B, T, 3, H_NSA, 1)
    o_nsa = g[:, :, 0] * o_cmp + g[:, :, 1] * o_slc + g[:, :, 2] * o_win
    o_nsa = rmsnorm(o_nsa.reshape(B, T, H_NSA * DK).astype(x.dtype), p['nsa_out_g'])
    qg_ = q_g.reshape(B, T, H_GLA, DK_GLA) * (DK_GLA ** -0.5)
    kg_ = k_g.reshape(B, T, H_GLA, DK_GLA)
    vg_ = v_g.reshape(B, T, H_GLA, DV_GLA)
    z = (a_low @ p['gla_a_up']).astype(jnp.float32) + p['gla_a_b'].astype(jnp.float32)
    log_a = (jax.nn.log_sigmoid(z) / GATE_TAU).reshape(B, T, H_GLA, DK_GLA)
    o_g, st = gla_scan(qg_, kg_, vg_, log_a, gla_state)
    o_gla = rmsnorm(o_g.astype(x.dtype), p['gla_out_g']) * jax.nn.silu(r_g.reshape(B, T, H_GLA, DV_GLA))
    mix = jnp.concatenate([o_nsa, o_gla.reshape(B, T, H_GLA * DV_GLA)], axis=-1) @ p['w_out']
    x1 = x + mix
    y = x1 + peer(rmsnorm(x1, p['norm2_g']), p['peer_wq'], p['peer_qn_g'], p['peer_k1'], p['peer_k2'], p['peer_u'], p['peer_v'])
    win_all = jnp.concatenate([win_kv.astype(kw.dtype), jnp.stack([kw, vw], axis=2)], axis=1)
    keep = min(WINDOW, win_all.shape[1])
    return y, new_kv, win_all[:, win_all.shape[1] - keep:], st

def setup_inputs(seed: int = 0) -> dict:
    key = jax.random.key(seed)
    ks = jax.random.split(key, 32)
    n_pages = PAST_LEN // PAGE_SIZE
    n_used = DEC_BATCH * n_pages
    n_pool = n_used + max(1, n_used // 4)
    win_buf = min(WINDOW, PAST_LEN)
    def nrm(k, shape, s):
        return s * jax.random.normal(k, shape, jnp.float32)
    def gain(k, shape):
        return 1.0 + nrm(k, shape, 0.02)
    page_table = jax.random.permutation(ks[5], n_pool)[:n_used].reshape(DEC_BATCH, n_pages).astype(jnp.int32)
    return {
        'x_prompt': nrm(ks[0], (BATCH, SEQ, D_MODEL), 1.0),
        'x_sample': nrm(ks[1], (DEC_BATCH, DEC_SEQ, D_MODEL), 1.0),
        'cache_kv': nrm(ks[2], (n_pool, PAGE_SIZE, KV_SLOTS, G_KV, DK), 1.0),
        'cache_win': nrm(ks[3], (DEC_BATCH, win_buf, 2, G_KV, DK), 1.0),
        'state_gla': nrm(ks[4], (DEC_BATCH, H_GLA, DK_GLA, DV_GLA), 1.0),
        'page_table': page_table,
        'norm1_g': gain(ks[6], (D_MODEL,)),
        'w_in': nrm(ks[7], (D_MODEL, D_IN), D_MODEL ** -0.5),
        'qn_g': gain(ks[8], (DK,)),
        'kn_cmp_g': gain(ks[9], (DK,)),
        'kn_slc_g': gain(ks[10], (DK,)),
        'kn_win_g': gain(ks[11], (DK,)),
        'cmp_w_pos': (1.0 + nrm(ks[12], (2, G_KV, CMP_BLOCK), 0.1)) * CMP_BLOCK ** -0.5,
        'cmp_proj': nrm(ks[13], (2, G_KV, DK, DK), DK ** -0.5),
        'rel_bias': nrm(ks[14], (N_BUCKETS, H_NSA), 0.1),
        'nsa_gate_b': nrm(ks[15], (3 * H_NSA,), 0.1),
        'nsa_out_g': gain(ks[16], (H_NSA * DK,)),
        'gla_a_up': nrm(ks[17], (GATE_RANK, H_GLA * DK_GLA), GATE_RANK ** -0.5),
        'gla_a_b': nrm(ks[18], (H_GLA * DK_GLA,), 0.1),
        'gla_out_g': gain(ks[19], (DV_GLA,)),
        'w_out': nrm(ks[20], (D_MIX, D_MODEL), D_MIX ** -0.5),
        'norm2_g': gain(ks[21], (D_MODEL,)),
        'peer_wq': nrm(ks[22], (D_MODEL, PEER_HEADS * PEER_QDIM), D_MODEL ** -0.5),
        'peer_qn_g': gain(ks[23], (PEER_QDIM,)),
        'peer_k1': nrm(ks[24], (PEER_HEADS, N_KEYS, PEER_QDIM // 2), (PEER_QDIM // 2) ** -0.5),
        'peer_k2': nrm(ks[25], (PEER_HEADS, N_KEYS, PEER_QDIM // 2), (PEER_QDIM // 2) ** -0.5),
        'peer_u': nrm(ks[26], (N_EXPERTS, D_MODEL), D_MODEL ** -0.5),
        'peer_v': nrm(ks[27], (N_EXPERTS, D_MODEL), PEER_HEADS ** -0.5),
    }

def reference(x_prompt, x_sample, cache_kv, cache_win, state_gla, page_table,
              norm1_g, w_in, qn_g, kn_cmp_g, kn_slc_g, kn_win_g, cmp_w_pos, cmp_proj,
              rel_bias, nsa_gate_b, nsa_out_g, gla_a_up, gla_a_b, gla_out_g, w_out,
              norm2_g, peer_wq, peer_qn_g, peer_k1, peer_k2, peer_u, peer_v):
    params = dict(norm1_g=norm1_g, w_in=w_in, qn_g=qn_g, kn_cmp_g=kn_cmp_g, kn_slc_g=kn_slc_g,
                  kn_win_g=kn_win_g, cmp_w_pos=cmp_w_pos, cmp_proj=cmp_proj, rel_bias=rel_bias,
                  nsa_gate_b=nsa_gate_b, nsa_out_g=nsa_out_g, gla_a_up=gla_a_up, gla_a_b=gla_a_b,
                  gla_out_g=gla_out_g, w_out=w_out, norm2_g=norm2_g, peer_wq=peer_wq,
                  peer_qn_g=peer_qn_g, peer_k1=peer_k1, peer_k2=peer_k2, peer_u=peer_u, peer_v=peer_v)
    B = x_prompt.shape[0]
    past_p = jnp.zeros((B, 0, KV_SLOTS, G_KV, DK), x_prompt.dtype)
    win_p = jnp.zeros((B, 0, 2, G_KV, DK), x_prompt.dtype)
    st_p = jnp.zeros((B, H_GLA, DK_GLA, DV_GLA), jnp.float32)
    n_seq, n_pages = page_table.shape
    past_s = cache_kv[page_table].reshape(n_seq, n_pages * PAGE_SIZE, KV_SLOTS, G_KV, DK)
    y_p = x_prompt
    y_s = x_sample
    for layer_idx in range(DEPTH):
        y_p, kv_p, win_new_p, st_new_p = layer(y_p, past_p, win_p, st_p, params)
        y_s, kv_s, win_new_s, st_new_s = layer(y_s, past_s, cache_win, state_gla, params)
    return (y_p, y_s, kv_p, kv_s, win_new_p, win_new_s, st_new_p, st_new_s)


_drawn_inputs = setup_inputs


def setup_inputs(seed=0):
    import zlib

    import numpy as np

    out = dict(_drawn_inputs(seed))
    spreads = {}
    factors = {'qn_g': 3.389,
     'kn_cmp_g': 2.949,
     'kn_slc_g': 5.073,
     'kn_win_g': 3.936,
     'nsa_gate_b': 3.001,
     'nsa_out_g': 30.852,
     'gla_out_g': 53.363,
     'rel_bias': 3.635,
     'norm2_g': 19.234,
     'peer_qn_g': 21.579}
    for name, (base, spread) in spreads.items():
        noise = np.random.default_rng([zlib.crc32(name.encode()), seed]).standard_normal(out[name].shape)
        drawn = base * np.exp(spread * noise) if base else spread * noise
        out[name] = __import__('jax').numpy.asarray(drawn.astype(out[name].dtype))
    for name, factor in factors.items():
        out[name] = (out[name] * factor).astype(out[name].dtype)
    return out
```

```python
from contextlib import ExitStack

import numpy as np

import concourse.bass as bass
from concourse import mybir

ALU = mybir.AluOpType
ACT = mybir.ActivationFunctionType
F32 = mybir.dt.float32
F32R = mybir.dt.float32r
BF16 = mybir.dt.bfloat16
I32 = mybir.dt.int32
U32 = mybir.dt.uint32
X = mybir.AxisListType.X

P = 128
D = 1024
KD = D // P
SEQ = 512
DEC_B, DEC_T = 8, 8
NT = SEQ // P + 1
TOK = NT * P
NTOK = SEQ + DEC_B * DEC_T
PAST, PAGE = 1024, 128
NPAGE = PAST // PAGE
H, DK, G, HPG = 8, 64, 2, 4
STRIDE = 16
NSUB = PAGE // STRIDE
WIN = 512
HG, DKG, DVG, RANK = 4, 64, 128, 16
TAU = 16.0
NB, MAXD = 32, 128
PH, NKEY, PQ, TOPK = 8, 128, 256, 16
EPS = 1e-6
NEG = -1e30
SCALE = DK ** -0.5
SIZES = dict(q=H * DK, kc=G * DK, vc=G * DK, ks=G * DK, vs=G * DK, kw=G * DK, vw=G * DK, gate=3 * H,
             qg=HG * DKG, kg=HG * DKG, vg=HG * DVG, al=RANK, rg=HG * DVG)
D_IN = sum(SIZES.values())
COL = {}
for _n, _s in SIZES.items():
    COL[_n] = sum(SIZES[m] for m in list(SIZES)[:list(SIZES).index(_n)])
PCH = 6
PCW = D_IN // PCH
DMAX = PAST + DEC_T - 1
LVEC = DMAX + P + 1


class Shared:
    pass


def part(S, name, lo=0, hi=NT):
    return S.pj[:, lo:hi, COL[name]:COL[name] + SIZES[name]]


def over(ap, shape):
    return ap.to_broadcast(shape)


def sb(nc, ctx, name, shape, dt=F32):
    return ctx.enter_context(nc.sbuf_tensor(name, shape, dt))


def load_start(nc, S):
    s_in = nc.alloc_semaphore("start_loaded")
    s_zero = nc.alloc_semaphore("sample_padding_zeroed")
    rows = [("g_q", S.qn_g), ("g_ks", S.kn_slc_g), ("g_kw", S.kn_win_g), ("g_kc", S.kn_cmp_g)]
    with nc.Block() as block:
        @block.sync
        def _(sp):
            n = 0
            for i, (_, src) in enumerate(rows):
                sp.dma_start(S.gains[:, i, :], src.partition_broadcast(P)).then_inc(s_in, 16)
            sp.dma_start(S.ident[:], S.c_ident[:, :]).then_inc(s_in, 16)
            sp.dma_start(S.iota[:], S.c_iota[:, :]).then_inc(s_in, 16)
            sp.dma_start(S.x[:, 0:4, :], S.x_prompt[0].rearrange("(t p) d -> p t d", p=P)).then_inc(s_in, 16)
            sp.wait_ge(s_zero, 1)
            sp.dma_start(S.x[0:64, 4, :], S.x_sample.rearrange("b t d -> (b t) d")).then_inc(s_in, 16)
            sp.wait_ge(s_in, 16 * (len(rows) + 4))

        @block.vector
        def _(dve):
            dve.memset(S.x[:, 4, :], 0.0).then_inc(s_zero, 1)
            dve.memset(S.ones[:], 1.0)


def norm_transposed(nc, S, tag, x, xn, gain, out_T):
    with ExitStack() as ctx:
        stat = sb(nc, ctx, f"{tag}_stat", [P, 2, NT])
        gcol = sb(nc, ctx, f"{tag}_gcol", [P, KD])
        s_g = nc.alloc_semaphore(f"{tag}_gain_loaded")
        s_sum = nc.alloc_semaphore(f"{tag}_squares_summed")
        s_ms = nc.alloc_semaphore(f"{tag}_mean_ready")
        s_rs = nc.alloc_semaphore(f"{tag}_rstd_ready")
        s_xn = nc.alloc_semaphore(f"{tag}_tile_scaled")
        s_tr = nc.alloc_semaphore(f"{tag}_chunk_transposed")
        s_ev = nc.alloc_semaphore(f"{tag}_chunk_moved")
        with nc.Block() as block:
            @block.sync
            def _(sp):
                with nc.allow_non_contiguous_dma(reason="1024 gains, one per partition and chunk"):
                    sp.dma_start(gcol[:], gain.rearrange("(k p) -> p k", p=P)).then_inc(s_g, 16)

            @block.scalar
            def _(act):
                for t in range(NT):
                    act.activation(out_T[:].rearrange("p k n -> p (k n)")[:, 0:D], x[:, t, :], ACT.Square, accum_out=stat[:, 0, t:t + 1])
                    act.drain()
                act.drain().then_inc(s_sum, 1)
                act.wait_ge(s_ms, 1)
                act.activation(stat[:, 0, :], stat[:, 1, :], ACT.Sqrt).then_inc(s_rs, 1)
                act.wait_ge(s_g, 16)
                for k in range(KD):
                    act.wait_ge(s_tr, k + 1)
                    act.activation(out_T[:, k, :], S.ps2[:, k % 4, 0:TOK], ACT.Copy,
                                   scale=gcol[:, k:k + 1]).then_inc(s_ev, 1)

            @block.vector
            def _(dve):
                dve.wait_ge(s_sum, 1)
                dve.tensor_scalar(stat[:, 1, :], stat[:, 0, :], 1.0 / D, EPS, ALU.mult, ALU.add)
                dve.drain()
                dve.reciprocal(stat[:, 1, :], stat[:, 1, :]).then_inc(s_ms, 1)
                dve.wait_ge(s_rs, 1)
                for t in range(NT):
                    dve.tensor_scalar(xn[:, t, :], x[:, t, :], stat[:, 0, t:t + 1], None, ALU.mult).then_inc(s_xn, 1)

            @block.tensor
            def _(pe):
                pe.wait_ge(s_xn, NT)
                for k in range(KD):
                    if k >= 4:
                        pe.wait_ge(s_ev, k - 3)
                    for t in range(NT):
                        last = pe.transpose(S.ps2[:, k % 4, t * P:(t + 1) * P], xn[:, t, k * P:(k + 1) * P], S.ident[:])
                    last.then_inc(s_tr, 1)


def project_in(nc, S):
    with ExitStack() as ctx:
        w = sb(nc, ctx, "w_in_sb", [P, KD, D_IN])
        hT = sb(nc, ctx, "hT", [P, KD, TOK])
        s_w = nc.alloc_semaphore("w_in_loaded")
        with nc.Block() as block:
            @block.sync
            def _(sp):
                for k in range(KD):
                    sp.dma_start(w[:, k, :], S.w_in[k * P:(k + 1) * P, :]).then_inc(s_w, 16)
        norm_transposed(nc, S, "norm1", S.x, S.x, S.norm1_g, hT)
        s_mm = nc.alloc_semaphore("proj_bank_ready")
        s_free = nc.alloc_semaphore("proj_bank_free")
        with nc.Block() as block:
            @block.tensor
            def _(pe):
                pe.wait_ge(s_w, 16 * KD)
                with pe.Fori(0, PCH) as c:
                    for t in range(NT):
                        pe.wait_ge(s_free, c * NT + t + 1)
                        for k in range(KD):
                            mm = pe.matmul(S.ps[:, t, 0:PCW], hT[:, k, t * P:(t + 1) * P],
                                           w[:, k, bass.ds(c * PCW, PCW)], start=(k == 0), stop=(k == KD - 1))
                        mm.then_inc(s_mm, 1)

            @block.vector
            def _(dve):
                dve.sem_inc(s_free, NT)
                with dve.Fori(0, PCH) as c:
                    for t in range(NT):
                        dve.wait_ge(s_mm, c * NT + t + 1)
                        dve.tensor_copy(S.pj[:, t, bass.ds(c * PCW, PCW)], S.ps[:, t, 0:PCW]).then_inc(s_free, 1)


def head_norms(nc, S):
    with ExitStack() as ctx:
        sq = sb(nc, ctx, "qk_sq", [P, NT, 12, DK])
        ms = sb(nc, ctx, "qk_ms", [P, NT, 12])
        rs = sb(nc, ctx, "qk_rs", [P, NT, 12])
        gb = sb(nc, ctx, "gate_b", [P, 3 * H])
        s_gb = nc.alloc_semaphore("gate_bias_loaded")
        s_inv = nc.alloc_semaphore("qk_inverse_ready")
        s_rs = nc.alloc_semaphore("qk_rstd_ready")
        s_zg = nc.alloc_semaphore("gate_logits_ready")
        s_out = nc.alloc_semaphore("kv_out_written")
        s_fin = nc.alloc_semaphore("qk_normed")
        q, ks, kw = part(S, "q"), part(S, "ks"), part(S, "kw")
        with nc.Block() as block:
            @block.sync
            def _(sp):
                sp.dma_start(gb[:], S.nsa_gate_b.partition_broadcast(P)).then_inc(s_gb, 16)
                sp.wait_ge(s_fin, 1)
                kv = lambda lo, hi: S.pj[:, lo:hi, COL["kc"]:COL["kc"] + 512]
                wv = lambda lo, hi: S.pj[:, lo:hi, COL["kw"]:COL["kw"] + 256]
                sp.dma_start(S.kv_prompt[0].rearrange("(t p) a g d -> p t (a g d)", p=P), kv(0, 4)).then_inc(s_out, 16)
                sp.dma_start(S.kv_sample.rearrange("b t a g d -> (b t) (a g d)"), kv(4, 5)[0:64, 0, :]).then_inc(s_out, 16)
                sp.dma_start(S.win_prompt[0].rearrange("(t p) a g d -> p t (a g d)", p=P), wv(0, 4)).then_inc(s_out, 16)
                sp.dma_start(S.win_sample[:, 0:WIN - DEC_T].rearrange("b t a g d -> b (t a g d)"),
                             S.cache_win[:, DEC_T:WIN].rearrange("b t a g d -> b (t a g d)")).then_inc(s_out, 16)
                for b in range(DEC_B):
                    sp.dma_start(S.win_sample[b, WIN - DEC_T:WIN].rearrange("t a g d -> t (a g d)"),
                                 wv(4, 5)[b * DEC_T:(b + 1) * DEC_T, 0, :]).then_inc(s_out, 16)
                sp.wait_ge(s_out, 16 * (4 + DEC_B))

            @block.vector
            def _(dve):
                for lo, hi, src in ((0, 8, q), (8, 10, ks), (10, 12, kw)):
                    v = src.rearrange("p t (h d) -> p t h d", d=DK)
                    dve.tensor_tensor(sq[:, :, lo:hi, :], v, v, ALU.mult)
                dve.drain()
                dve.tensor_reduce(ms[:], sq[:], X, ALU.add)
                dve.drain()
                dve.tensor_scalar(ms[:], ms[:], 1.0 / DK, EPS, ALU.mult, ALU.add)
                dve.drain()
                dve.reciprocal(ms[:], ms[:]).then_inc(s_inv, 1)
                dve.wait_ge(s_gb, 16)
                dve.tensor_tensor(S.gates[:], part(S, "gate"),
                                  gb[:].unsqueeze(1).to_broadcast([P, NT, 3 * H]), ALU.add).then_inc(s_zg, 1)
                dve.wait_ge(s_rs, 1)
                for lo, hi, src in ((0, 8, q), (8, 10, ks), (10, 12, kw)):
                    v = src.rearrange("p t (h d) -> p t h d", d=DK)
                    dve.tensor_tensor(sq[:, :, lo:hi, :], v,
                                      rs[:, :, lo:hi].unsqueeze(3).to_broadcast([P, NT, hi - lo, DK]), ALU.mult)
                dve.drain()
                qp = S.qp[:].rearrange("p t (j g d) -> p t j g d", g=G, d=DK)
                for g in range(G):
                    dve.tensor_tensor(qp[:, :, :, g, :], sq[:, :, g * HPG:(g + 1) * HPG, :],
                                      S.gains[:, 0:1, :].unsqueeze(1).to_broadcast([P, NT, HPG, DK]), ALU.mult)
                for i, lo, dst in ((1, 8, ks), (2, 10, kw)):
                    dve.tensor_tensor(dst.rearrange("p t (h d) -> p t h d", d=DK), sq[:, :, lo:lo + 2, :],
                                      S.gains[:, i:i + 1, :].unsqueeze(1).to_broadcast([P, NT, 2, DK]), ALU.mult)
                dve.drain().then_inc(s_fin, 1)

            @block.scalar
            def _(act):
                act.wait_ge(s_inv, 1)
                act.activation(rs[:], ms[:], ACT.Sqrt).then_inc(s_rs, 1)
                act.wait_ge(s_zg, 1)
                act.activation(S.gates[:], S.gates[:], ACT.Sigmoid)




def attention_setup(nc, S):
    with ExitStack() as ctx:
        relb = sb(nc, ctx, "relb", [NB + 1, H])
        onehot = sb(nc, ctx, "bucket_onehot", [NB + 1, LVEC])
        vec = sb(nc, ctx, "bias_vec", [H, LVEC])
        wpos = sb(nc, ctx, "wpos", [P, 4, 2])
        msub = sb(nc, ctx, "msub", [P, NSUB])
        flipped = sb(nc, ctx, "toep_flipped", [P, H, 512])
        sflip = sb(nc, ctx, "sbias_flipped", [P, PAST + DEC_T])
        flips = sb(nc, ctx, "flips", [P, 2, P])
        s_c = nc.alloc_semaphore("bias_inputs_loaded")
        s_neg = nc.alloc_semaphore("mask_row_set")
        s_mm = nc.alloc_semaphore("bias_vec_summed")
        s_vec = nc.alloc_semaphore("bias_vec_ready")
        s_rv = nc.alloc_semaphore("bias_vec_stored")
        s_t = nc.alloc_semaphore("bias_tiles_loaded")
        s_tr = nc.alloc_semaphore("qk_block_transposed")
        s_ea = nc.alloc_semaphore("qk_even_block_moved")
        s_ed = nc.alloc_semaphore("qk_odd_block_moved")
        s_gl = nc.alloc_semaphore("sample_gates_loaded")
        s_gs = nc.alloc_semaphore("sample_gates_stored")
        s_fl = nc.alloc_semaphore("bias_rows_flipped")
        s_fe = nc.alloc_semaphore("bias_rows_moved")
        scuts = [(a, min(a + 512, PAST + DEC_T)) for a in range(0, PAST + DEC_T, 512)]
        NFLIP = H + len(scuts)
        cuts = [(a, min(a + 512, LVEC)) for a in range(0, LVEC, 512)]
        sources = [S.qp[:, :, j * P:(j + 1) * P] for j in range(4)] + [part(S, "ks"), part(S, "kw")]
        targets = [S.qT[:, j, :] for j in range(4)] + [S.ksT[:], S.kwT[:]]
        with nc.Block() as block:
            @block.sync
            def _(sp):
                sp.dma_start(relb[0:NB, :], S.rel_bias[:, :]).then_inc(s_c, 16)
                sp.dma_start(onehot[:], S.c_bucket[:, :]).then_inc(s_c, 16)
                sp.dma_start(msub[:], S.c_sub[:, :]).then_inc(s_c, 16)
                sp.dma_start(S.cproj[:, :, :], S.cmp_proj.rearrange("k g d e -> (g d) k e")).then_inc(s_c, 16)
                sp.dma_start(S.grp[:], S.c_group[:, :]).then_inc(s_c, 16)
                sp.dma_start(S.misc[:], S.c_misc[:, :]).then_inc(s_c, 16)
                sp.dma_start(flips[:], S.c_flips.rearrange("a p n -> p a n")).then_inc(s_c, 16)
                with nc.allow_non_contiguous_dma(reason="position weights, one per partition"):
                    for r in range(NSUB):
                        sp.dma_start(wpos[r * STRIDE:(r + 1) * STRIDE, :, :],
                                     S.cmp_w_pos.rearrange("k g (h j) -> j (k g) h", j=STRIDE)).then_inc(s_c, 16)
                sp.dma_start(S.gate_dram[:, :], S.gates[0:64, 4, :]).then_inc(s_gs, 16)
                sp.wait_ge(s_vec, 1)
                sp.dma_start(S.rv_dram[:, :], vec[:]).then_inc(s_rv, 16)
                sp.wait_ge(s_rv, 16)
                sp.dma_start(flipped[:], bass.AP(S.rv_t, DMAX - 384 - (P - 1), [[1, P], [LVEC, H], [1, 512]])).then_inc(s_t, 16)
                for bb in range(2):
                    for h in range(H):
                        lo = bb * 64 + h * DEC_T
                        sp.dma_start(sflip[lo:lo + DEC_T, :],
                                     bass.AP(S.rv_t, h * LVEC + DMAX - PAST - (DEC_T - 1),
                                             [[1, DEC_T], [1, PAST + DEC_T]])).then_inc(s_t, 16)
                sp.wait_ge(s_gs, 16)
                with nc.allow_non_contiguous_dma(reason="24 gates of each sample token to their rows"):
                    for r in range(4):
                        for bb in range(2):
                            for h in range(H):
                                lo = bb * 64 + h * DEC_T
                                sp.dma_start(S.grow[lo:lo + DEC_T, r, :],
                                             bass.AP(S.gate_t, (2 * r + bb) * DEC_T * 24 + h, [[24, DEC_T], [8, 3]])).then_inc(s_gl, 16)
                sp.wait_ge(s_gl, 16 * 8 * H)

            @block.vector
            def _(dve):
                dve.memset(relb[NB:NB + 1, :], NEG).then_inc(s_neg, 1)
                dve.wait_ge(s_mm, 1)
                for i, (a, b) in enumerate(cuts):
                    dve.tensor_copy(vec[:, a:b], S.ps[0:H, 5 + i, 0:b - a])
                dve.drain().then_inc(s_vec, 1)
                dve.tensor_tensor(S.w16[:].rearrange("p a b n -> p (a b) n"),
                                  wpos[:].rearrange("p a b -> p (a b)").unsqueeze(2).to_broadcast([P, 8, NSUB]),
                                  msub[:].unsqueeze(1).to_broadcast([P, 8, NSUB]), ALU.mult)
                for i in (1, 3, 5):
                    dve.wait_ge(s_tr, i + 1)
                    dve.tensor_copy(targets[i], S.ps2[:, i % 2, 0:TOK]).then_inc(s_ed, 1)
                for i in range(NFLIP):
                    dve.wait_ge(s_fl, i + 1)
                    dst = S.toep[:, i, :] if i < H else S.sbias[:, scuts[i - H][0]:scuts[i - H][1]]
                    dve.tensor_copy(dst, S.ps[:, i % 2, 0:dst.shape[-1]]).then_inc(s_fe, 1)

            @block.scalar
            def _(act):
                for i in (0, 2, 4):
                    act.wait_ge(s_tr, i + 1)
                    act.activation(targets[i], S.ps2[:, i % 2, 0:TOK], ACT.Copy).then_inc(s_ea, 1)

            @block.tensor
            def _(pe):
                pe.wait_ge(s_neg, 1)
                pe.wait_ge(s_c, 16 * (7 + NSUB))
                for i, (a, b) in enumerate(cuts):
                    mm = pe.matmul(S.ps[0:H, 5 + i, 0:b - a], relb[:], onehot[:, a:b], start=True, stop=True)
                mm.then_inc(s_mm, 1)
                for i, src in enumerate(sources):
                    if i >= 2:
                        pe.wait_ge(s_ed if i % 2 else s_ea, i // 2)
                    for t in range(NT):
                        tr = pe.transpose(S.ps2[:, i % 2, t * P:(t + 1) * P], src[:, t, :], S.ident[:])
                    tr.then_inc(s_tr, 1)
                pe.wait_ge(s_t, 16 * (1 + 2 * H))
                pe.wait_ge(s_ea, 3)
                pe.wait_ge(s_ed, 3)
                for i in range(NFLIP):
                    if i >= 2:
                        pe.wait_ge(s_fe, i - 1)
                    src = flipped[:, i, :] if i < H else sflip[:, scuts[i - H][0]:scuts[i - H][1]]
                    pe.matmul(S.ps[:, i % 2, 0:src.shape[-1]], flips[:, 0 if i < H else 1, :], src,
                              start=True, stop=True).then_inc(s_fl, 1)


def prompt_compress(nc, S):
    N, T = 31, 4
    with ExitStack() as ctx:
        halves = sb(nc, ctx, "pc_halves", [P, 2, 2, 32])
        blk = sb(nc, ctx, "pc_blk", [P, 2, N])
        sq = sb(nc, ctx, "pc_sq", [N, G, DK])
        st = sb(nc, ctx, "pc_st", [N, 2, G])
        kc = sb(nc, ctx, "pc_kc", [N, G, DK])
        s_pe = nc.alloc_semaphore("pc_product_ready")
        s_ve = nc.alloc_semaphore("pc_vector_ready")
        s_rt = nc.alloc_semaphore("pc_root_ready")
        cps = S.ps[:, 0, 0:128].rearrange("p (k h n) -> p k h n", k=2, h=2)
        kvc = S.ps[0:N, 1:1 + G, 0:2 * DK].rearrange("p g (k e) -> p g k e", k=2)
        with nc.Block() as block:
            @block.tensor
            def _(pe):
                for kv in range(2):
                    for g in range(G):
                        for t in range(T):
                            c = COL["kc"] + kv * P + g * DK
                            mm = pe.matmul(cps[g * DK:(g + 1) * DK, kv, :, t * NSUB:(t + 1) * NSUB],
                                           S.pj[:, t, c:c + DK], S.w16[:, kv * 2 + g], start=True, stop=True)
                mm.then_inc(s_pe, 1)
                pe.wait_ge(s_ve, 1)
                for kv in range(2):
                    for g in range(G):
                        mm = pe.matmul(kvc[:, g, kv, :], blk[g * DK:(g + 1) * DK, kv, :],
                                       S.cproj[g * DK:(g + 1) * DK, kv, :], start=True, stop=True)
                mm.then_inc(s_pe, 1)
                pe.wait_ge(s_ve, 3)
                pe.transpose(S.ps[:, 3, 0:N], kc[:].rearrange("p g e -> p (g e)"), S.ident[0:N, 0:N]).then_inc(s_pe, 1)

            @block.vector
            def _(dve):
                dve.wait_ge(s_pe, 1)
                dve.tensor_copy(halves[:], cps)
                dve.drain()
                dve.tensor_tensor(blk[:], halves[:, :, 0, 0:N], halves[:, :, 1, 1:N + 1], ALU.add).then_inc(s_ve, 1)
                dve.wait_ge(s_pe, 2)
                dve.tensor_copy(S.vc[0:N, :].rearrange("p (g e) -> p g e", g=G), kvc[:, :, 1])
                dve.tensor_copy(kc[:], kvc[:, :, 0])
                dve.drain()
                dve.tensor_tensor(sq[:], kc[:], kc[:], ALU.mult)
                dve.drain()
                dve.tensor_reduce(st[:, 0, :], sq[:], X, ALU.add)
                dve.drain()
                dve.tensor_scalar(st[:, 0, :], st[:, 0, :], 1.0 / DK, EPS, ALU.mult, ALU.add)
                dve.drain()
                dve.reciprocal(st[:, 0, :], st[:, 0, :]).then_inc(s_ve, 1)
                dve.wait_ge(s_rt, 1)
                dve.tensor_tensor(kc[:], kc[:], st[:, 1, :].unsqueeze(2).to_broadcast([N, G, DK]), ALU.mult)
                dve.drain()
                dve.tensor_tensor(kc[:], kc[:], S.gains[0:N, 3:4, :].to_broadcast([N, G, DK]), ALU.mult).then_inc(s_ve, 1)
                dve.wait_ge(s_pe, 3)
                dve.tensor_copy(S.kcT[:, 0:N], S.ps[:, 3, 0:N])

            @block.scalar
            def _(act):
                act.wait_ge(s_ve, 2)
                act.activation(st[:, 1, :], st[:, 0, :], ACT.Sqrt).then_inc(s_rt, 1)


def prompt_attention(nc, S):
    units = [(t, g, kind) for t in range(4) for g in range(G) for kind in ("slc", "win", "cmp")]
    NU = len(units)
    NCMP = [7 + 8 * t for t in range(4)]
    with ExitStack() as ctx:
        q = sb(nc, ctx, "pa_q", [P, SEQ])
        s = sb(nc, ctx, "pa_s", [P, 2, 512])
        p = sb(nc, ctx, "pa_p", [P, 2, 512])
        pT = sb(nc, ctx, "pa_pT", [P, 2, 512])
        st = sb(nc, ctx, "pa_st", [P, 4, 4])
        s_q = nc.alloc_semaphore("pa_query_ready")
        s_qk = nc.alloc_semaphore("pa_scores_ready")
        s_sc = nc.alloc_semaphore("pa_logits_ready")
        s_p = nc.alloc_semaphore("pa_probs_ready")
        s_tr = nc.alloc_semaphore("pa_probs_transposed")
        s_pt = nc.alloc_semaphore("pa_probsT_ready")
        s_pv = nc.alloc_semaphore("pa_values_ready")
        s_fin = nc.alloc_semaphore("pa_unit_added")

        def width(u):
            t, g, kind = units[u]
            return NCMP[t] if kind == "cmp" else (t + 1) * P

        with nc.Block() as block:
            @block.tensor
            def _(pe):
                def scores(j, u):
                    t, g, kind = units[u]
                    keys = {"slc": S.ksT, "win": S.kwT, "cmp": S.kcT}[kind]
                    if u >= 2:
                        pe.wait_ge(s_sc, j * NU + u - 1)
                    pe.matmul(S.ps[:, u % 2, 0:width(u)], q[g * DK:(g + 1) * DK, t * P:(t + 1) * P],
                              keys[g * DK:(g + 1) * DK, 0:width(u)], start=True, stop=True).then_inc(s_qk, 1)

                def turn(j, u):
                    t, g, kind = units[u]
                    pe.wait_ge(s_p, j * NU + u + 1)
                    if u >= 2:
                        pe.wait_ge(s_pt, j * NU + u - 1)
                    for k0 in range(0, width(u), P):
                        n = min(P, width(u) - k0)
                        tr = pe.transpose(S.ps[0:n, 2 + u % 2, k0:k0 + P], p[:, u % 2, k0:k0 + n], S.ident[:])
                    tr.then_inc(s_tr, 1)

                def values(j, u):
                    t, g, kind = units[u]
                    pe.wait_ge(s_pt, j * NU + u + 1)
                    if u >= 2:
                        pe.wait_ge(s_fin, j * NU + u - 1)
                    out = S.ps[:, 4 + u % 2, 0:DK]
                    if kind == "cmp":
                        n = width(u)
                        mm = pe.matmul(out, pT[0:n, u % 2, 0:P], S.vc[0:n, g * DK:(g + 1) * DK], start=True, stop=True)
                    else:
                        c = COL["vs" if kind == "slc" else "vw"] + g * DK
                        for k in range(t + 1):
                            mm = pe.matmul(out, pT[:, u % 2, k * P:(k + 1) * P], S.pj[:, k, c:c + DK],
                                           start=(k == 0), stop=(k == t))
                    mm.then_inc(s_pv, 1)

                with pe.Fori(0, HPG) as j:
                    pe.wait_ge(s_q, j + 1)
                    for k in range(NU + 2):
                        if k < NU:
                            scores(j, k)
                        if 1 <= k <= NU:
                            turn(j, k - 1)
                        if k >= 2:
                            values(j, k - 2)

            @block.vector
            def _(dve):
                def logits(j, u):
                    t, g, kind = units[u]
                    w = width(u)
                    if kind == "cmp":
                        lo = 415 - P * t
                        bias = S.toep[:, bass.ds(g * HPG + j, 1), lo:lo + 16 * (w - 1) + 1:16]
                    else:
                        bias = S.toep[:, bass.ds(g * HPG + j, 1), 384 - P * t:512]
                    dve.wait_ge(s_qk, j * NU + u + 1)
                    if u >= 2:
                        dve.wait_ge(s_p, j * NU + u - 1)
                    dve.scalar_tensor_tensor(s[:, u % 2:u % 2 + 1, 0:w], S.ps[:, u % 2:u % 2 + 1, 0:w], SCALE, bias,
                                             ALU.mult, ALU.add)
                    dve.drain()
                    dve.tensor_reduce(st[:, u % 4, 0:1], s[:, u % 2, 0:w], X, ALU.max, negate=True).then_inc(s_sc, 1)

                def finish(j, u):
                    t, g, kind = units[u]
                    i = u % 4
                    col = {"cmp": 0, "slc": 1, "win": 2}[kind] * H + g * HPG
                    dve.wait_ge(s_pv, j * NU + u + 1)
                    dve.reciprocal(st[:, i, 2:3], st[:, i, 1:2])
                    dve.drain()
                    dve.tensor_tensor(st[:, i, 2:3], st[:, i, 2:3], S.gates[:, t, bass.ds(col + j, 1)], ALU.mult)
                    dve.drain()
                    if kind == "cmp" and t == 0:
                        dve.tensor_tensor(st[:, i, 2:3], st[:, i, 2:3], S.misc[:, 0:1], ALU.mult)
                        dve.drain()
                    dst = S.onsa[:, t, bass.ds((g * HPG + j) * DK, DK)]
                    if kind == "slc":
                        dve.tensor_scalar(dst, S.ps[:, 4 + u % 2, 0:DK], st[:, i, 2:3], None, ALU.mult).then_inc(s_fin, 1)
                    else:
                        dve.scalar_tensor_tensor(dst, S.ps[:, 4 + u % 2, 0:DK], st[:, i, 2:3], dst,
                                                 ALU.mult, ALU.add).then_inc(s_fin, 1)

                with dve.Fori(0, HPG) as j:
                    dve.tensor_copy(q[:], S.qT[:, bass.ds(j, 1), 0:SEQ].rearrange("p a n -> p (a n)")).then_inc(s_q, 1)
                    for k in range(NU + 2):
                        if k < NU:
                            logits(j, k)
                        if k >= 2:
                            finish(j, k - 2)
                    dve.drain()

            @block.scalar
            def _(act):
                with act.Fori(0, HPG) as j:
                    for k in range(NU + 1):
                        if k < NU:
                            u = k
                            act.wait_ge(s_sc, j * NU + u + 1)
                            if u >= 2:
                                act.wait_ge(s_tr, j * NU + u - 1)
                            act.activation(p[:, u % 2, 0:width(u)], s[:, u % 2, 0:width(u)], ACT.Exp,
                                           bias=st[:, u % 4, 0:1], accum_out=st[:, u % 4, 1:2]).then_inc(s_p, 1)
                        if k >= 1:
                            u = k - 1
                            n = P if units[u][2] != "cmp" else width(u)
                            w = P if units[u][2] == "cmp" else width(u)
                            act.wait_ge(s_tr, j * NU + u + 1)
                            if u >= 2:
                                act.wait_ge(s_pv, j * NU + u - 1)
                            act.activation(pT[0:n, u % 2, 0:w], S.ps[0:n, 2 + u % 2, 0:w], ACT.Copy).then_inc(s_pt, 1)


def settle(pe, S):
    pe.transpose(S.ps[:, 2, 384:512], S.ident[:], S.ident[:])


def sample_attention(nc, S):
    NC, K1, KW = 63, PAST + DEC_T, WIN + DEC_T
    NSLC = 17
    with ExitStack() as ctx:
        pt = sb(nc, ctx, "sa_pages", [1, DEC_B * NPAGE], I32)
        kv = sb(nc, ctx, "sa_kv", [P, 2, 2, NPAGE, 512])
        wn = sb(nc, ctx, "sa_win", [P, 2, 2, 4, 256])
        vn = sb(nc, ctx, "sa_vnew", [DEC_T, 2, 2, 2, P])
        q = sb(nc, ctx, "sa_q", [P, 2, 4, DEC_T])
        kT = sb(nc, ctx, "sa_kT", [P, 2, K1])
        wT = sb(nc, ctx, "sa_wT", [P, 2, KW])
        blk = sb(nc, ctx, "sa_blk", [P, 2, 2, NC])
        kc = sb(nc, ctx, "sa_kc", [NC, 2, G, DK])
        vc = sb(nc, ctx, "sa_vc", [NC, 2, P])
        kst = sb(nc, ctx, "sa_kst", [NC, 2, 2 * G])
        kcT = sb(nc, ctx, "sa_kcT", [P, 2, NC])
        lc = sb(nc, ctx, "sa_lc", [P, NC])
        ls = sb(nc, ctx, "sa_ls", [P, K1])
        lw = sb(nc, ctx, "sa_lw", [P, KW])
        halves = ls[:, 0:512].rearrange("p (b k h n) -> p b k h n", b=2, k=2, h=2)
        sq = lw[0:NC, 0:256].rearrange("p (b g e) -> p b g e", b=2, g=G)
        pext = sb(nc, ctx, "sa_pext", [P, 72])
        sel = sb(nc, ctx, "sa_sel", [P, 4, NSLC])
        st = sb(nc, ctx, "sa_st", [P, 12])
        pTc = sb(nc, ctx, "sa_pTc", [NC, P])
        pTs = kT[:, 0, 0:PAST].rearrange("p (n a) -> p n a", n=NPAGE)
        pTw = wT[:, 0, 0:WIN].rearrange("p (n a) -> p n a", n=4)
        pTn = sb(nc, ctx, "sa_pTn", [DEC_T, 2, P])
        o = sb(nc, ctx, "sa_o", [P, DK])
        names = ["sa_even_loaded", "sa_odd_loaded", "sa_round_read", "sa_halves_summed", "sa_blocks_ready",
                 "sa_kvc_summed", "sa_inverse_ready", "sa_root_ready", "sa_kc_normed", "sa_kc_transposed",
                 "sa_kcT_ready", "sa_bank_transposed", "sa_bank_moved", "sa_copies_ready", "sa_scores_ready",
                 "sa_cmp_logits", "sa_cmp_exp", "sa_cmp_probs", "sa_group_summed", "sa_logits_ready", "sa_exp_ready",
                 "sa_probs_turned", "sa_probsT_ready", "sa_values_ready", "sa_out_ready", "sa_out_stored",
                 "sa_pages_loaded", "sa_cmp_values", "sa_cmp_turned", "sa_turn_bank", "sa_turn_moved", "sa_final_load", "sa_out_free"]
        m = {n[3:]: nc.alloc_semaphore(n) for n in names}
        tail = S.ps[:, 2, 0:8]
        wtail = S.ps[:, 2, 8:16]
        csc = S.ps[:, 2, 64:64 + NC]
        cps = S.ps[:, 6, :].rearrange("p (b k h n) -> p b k h n", b=2, k=2, h=2)
        kvc = S.ps[0:NC, 6:8, 0:256].rearrange("p g (b k e) -> p g b k e", b=2, k=2)
        NLOAD = 2 * (NPAGE + 3)
        combos = [(bb, g) for bb in range(2) for g in range(G)]

        with nc.Block() as block:
            @block.sync
            def _(sp):
                sp.dma_start(pt[:], S.page_table.rearrange("b n -> (b n)").unsqueeze(0)).then_inc(m["pages_loaded"], 16)
                sp.wait_ge(m["pages_loaded"], 16)
                with sp.Fori(0, 2) as rr:
                    for par in range(2):
                        s_ld = m["even_loaded"] if par == 0 else m["odd_loaded"]
                        sp.wait_ge(m["round_read"], rr * 2 + par + 1)
                        for bb in range(2):
                            b = rr * 4 + par * 2 + bb
                            for n in range(NPAGE):
                                page = sp.value_load(pt[0:1, bass.ds(b * NPAGE + n, 1)], min_val=0,
                                                     max_val=S.cache_kv.shape[0] - 1)
                                sp.dma_start(kv[:, par, bb, n, :],
                                             S.cache_kv[bass.ds(page, 1)].rearrange("a p s g d -> p (a s g d)")).then_inc(s_ld, 16)
                            sp.dma_start(wn[:, par, bb, :, :],
                                         S.cache_win[bass.ds(b, 1)].rearrange("a (n p) s g d -> p (a n) (s g d)", p=P)).then_inc(s_ld, 16)
                            sp.dma_start(vn[:, par, bb, 0, :],
                                         S.kv_sample[bass.ds(b, 1), :, 3].rearrange("a t g d -> t (a g d)")).then_inc(s_ld, 16)
                            sp.dma_start(vn[:, par, bb, 1, :],
                                         S.win_sample[bass.ds(b, 1), WIN - DEC_T:WIN, 1].rearrange("a t g d -> t (a g d)")).then_inc(s_ld, 16)

            @block.tensor
            def _(pe):
                with pe.Fori(0, 2) as rr:
                    for par in range(2):
                        r1 = rr * 2 + par + 1
                        pe.wait_ge(m["even_loaded"] if par == 0 else m["odd_loaded"], (rr + 1) * 16 * NLOAD)
                        for bb in range(2):
                            for k in range(2):
                                for g in range(G):
                                    for n in range(NPAGE):
                                        mm = pe.matmul(cps[g * DK:(g + 1) * DK, bb, k, :, n * NSUB:(n + 1) * NSUB],
                                                       kv[:, par, bb, n, k * P + g * DK:k * P + (g + 1) * DK],
                                                       S.w16[:, k * 2 + g], start=True, stop=True)
                        mm.then_inc(m["halves_summed"], 1)
                        for f in range(6):
                            bb, part3 = divmod(f, 3)
                            if f >= 2:
                                pe.wait_ge(m["bank_moved"], (rr * 2 + par) * 6 + f - 1)
                            for i in range(4):
                                src = (kv[:, par, bb, part3 * 4 + i, 2 * P:3 * P] if part3 < 2 else wn[:, par, bb, i, 0:P])
                                tr = pe.transpose(S.ps[:, 4 + f % 2, i * P:(i + 1) * P], src, S.ident[:])
                            tr.then_inc(m["bank_transposed"], 1)
                        pe.wait_ge(m["blocks_ready"], r1)
                        settle(pe, S)
                        for bb in range(2):
                            for k in range(2):
                                for g in range(G):
                                    mm = pe.matmul(kvc[:, g, bb, k, :], blk[g * DK:(g + 1) * DK, bb, k, :],
                                                   S.cproj[g * DK:(g + 1) * DK, k, :], start=True, stop=True)
                        mm.then_inc(m["kvc_summed"], 1)
                        pe.wait_ge(m["kc_normed"], r1)
                        pe.wait_ge(m["bank_moved"], (rr * 2 + par) * 6 + 6)
                        settle(pe, S)
                        for bb in range(2):
                            tr = pe.transpose(S.ps[:, 4, bb * P:bb * P + NC], kc[:, bb].rearrange("p g e -> p (g e)"),
                                              S.ident[0:NC, 0:NC])
                        tr.then_inc(m["kc_transposed"], 1)
                        pe.wait_ge(m["kcT_ready"], r1)
                        pe.wait_ge(m["copies_ready"], r1)
                        settle(pe, S)
                        for c, (bb, g) in enumerate(combos):
                            lhs = q[g * DK:(g + 1) * DK, bb].rearrange("p j t -> p (j t)")
                            rows = slice(32 * c, 32 * c + 32)
                            kr = slice(g * DK, (g + 1) * DK)
                            pe.matmul(csc[rows], lhs, kcT[kr, bb, :], start=True, stop=True)
                            pe.matmul(S.ps[rows, 0, :], lhs, kT[kr, bb, 0:512], start=True, stop=True)
                            pe.matmul(S.ps[rows, 1, :], lhs, kT[kr, bb, 512:1024], start=True, stop=True)
                            pe.matmul(tail[rows], lhs, kT[kr, bb, 1024:K1], start=True, stop=True)
                            pe.matmul(S.ps[rows, 3, :], lhs, wT[kr, bb, 0:512], start=True, stop=True)
                            mm = pe.matmul(wtail[rows], lhs, wT[kr, bb, 512:KW], start=True, stop=True)
                        mm.then_inc(m["scores_ready"], 1)
                        pe.wait_ge(m["cmp_probs"], r1)
                        pe.matmul(S.ps[:, 6, 0:NC], S.grp[:], lc[:], start=True, stop=True).then_inc(m["group_summed"], 1)
                        pe.transpose(S.ps[0:NC, 4, 256:384], lc[:], S.ident[:]).then_inc(m["cmp_turned"], 1)
                        pe.wait_ge(m["exp_ready"], r1)
                        for f in range(4):
                            if f == 0:
                                pe.wait_ge(m["cmp_values"], r1)
                            if f >= 2:
                                pe.wait_ge(m["turn_moved"], (rr * 2 + par) * 4 + f - 1)
                            bank = S.ps[:, 4 + f % 2, :]
                            if f < 3:
                                for i in range(4):
                                    src = ls[:, (4 * f + i) * P:(4 * f + i + 1) * P] if f < 2 else lw[:, i * P:(i + 1) * P]
                                    tr = pe.transpose(bank[:, i * P:(i + 1) * P], src, S.ident[:])
                            else:
                                pe.transpose(bank[0:DEC_T, 0:P], ls[:, PAST:K1], S.ident[:])
                                tr = pe.transpose(bank[0:DEC_T, P:2 * P], lw[:, WIN:KW], S.ident[:])
                            tr.then_inc(m["turn_bank"], 1)
                        pe.wait_ge(m["turn_moved"], (rr * 2 + par) * 4 + 4)
                        settle(pe, S)
                        for c, (bb, g) in enumerate(combos):
                            rows = slice(32 * c, 32 * c + 32)
                            gc = slice(g * DK, (g + 1) * DK)
                            pe.matmul(S.ps[rows, 7, 0:DK], pTc[:, rows], vc[:, bb, gc], start=True, stop=True)
                            for n in range(NPAGE):
                                pe.matmul(S.ps[rows, 0, 0:DK], pTs[:, n, rows],
                                          kv[:, par, bb, n, 3 * P + g * DK:3 * P + (g + 1) * DK], start=(n == 0), stop=False)
                            pe.matmul(S.ps[rows, 0, 0:DK], pTn[:, 0, rows], vn[:, par, bb, 0, gc], start=False, stop=True)
                            for n in range(4):
                                pe.matmul(S.ps[rows, 3, 0:DK], pTw[:, n, rows],
                                          wn[:, par, bb, n, P + g * DK:P + (g + 1) * DK], start=(n == 0), stop=False)
                            mm = pe.matmul(S.ps[rows, 3, 0:DK], pTn[:, 1, rows], vn[:, par, bb, 1, gc], start=False, stop=True)
                        mm.then_inc(m["values_ready"], 1)
                        pe.wait_ge(m["out_ready"], r1)
                        pe.sem_inc(m["round_read"], 1)

            @block.vector
            def _(dve):
                dve.sem_inc(m["round_read"], 2)
                dve.memset(pext[:], 0.0)
                with dve.Fori(0, 2) as rr:
                    for par in range(2):
                        r1 = rr * 2 + par + 1
                        b0 = rr * 4 + par * 2
                        for bb in range(2):
                            at = (b0 + bb) * DEC_T + SEQ
                            dve.tensor_copy(q[:, bb], S.qT[:, :, bass.ds(at, DEC_T)])
                            dve.tensor_copy(kT[:, bb, PAST:K1], S.ksT[:, bass.ds(at, DEC_T)])
                            dve.tensor_copy(wT[:, bb, WIN:KW], S.kwT[:, bass.ds(at, DEC_T)])
                        dve.drain().then_inc(m["copies_ready"], 1)
                        dve.wait_ge(m["halves_summed"], r1)
                        dve.tensor_copy(halves, cps)
                        dve.drain()
                        dve.tensor_tensor(blk[:].rearrange("p b k n -> p (b k) n"),
                                          halves.rearrange("p b k h n -> p (b k) h n")[:, :, 0, 0:NC],
                                          halves.rearrange("p b k h n -> p (b k) h n")[:, :, 1, 1:NC + 1],
                                          ALU.add).then_inc(m["blocks_ready"], 1)
                        dve.wait_ge(m["kvc_summed"], r1)
                        for g in range(G):
                            dve.tensor_copy(vc[:, :, g * DK:(g + 1) * DK], kvc[:, g, :, 1])
                            dve.tensor_copy(kc[:, :, g], kvc[:, g, :, 0])
                        dve.drain()
                        dve.tensor_tensor(sq, kc[:], kc[:], ALU.mult)
                        dve.drain()
                        dve.tensor_reduce(kst[:, 0, :], sq.rearrange("p b g e -> p (b g) e"), X, ALU.add)
                        dve.drain()
                        dve.tensor_scalar(kst[:, 0, :], kst[:, 0, :], 1.0 / DK, EPS, ALU.mult, ALU.add)
                        dve.drain()
                        dve.reciprocal(kst[:, 0, :], kst[:, 0, :]).then_inc(m["inverse_ready"], 1)
                        dve.wait_ge(m["root_ready"], r1)
                        kcv = kc[:].rearrange("p b g e -> p (b g) e")
                        dve.tensor_tensor(kcv, kcv, kst[:, 1, :].unsqueeze(2).to_broadcast([NC, 4, DK]), ALU.mult)
                        dve.drain()
                        dve.tensor_tensor(kcv, kcv, S.gains[0:NC, 3:4, :].to_broadcast([NC, 4, DK]), ALU.mult).then_inc(m["kc_normed"], 1)
                        dve.wait_ge(m["kc_transposed"], r1)
                        dve.tensor_copy(kcT[:], S.ps[:, 4, 0:256].rearrange("p (b n) -> p b n", b=2)[:, :, 0:NC]).then_inc(m["kcT_ready"], 1)
                        dve.wait_ge(m["scores_ready"], r1)
                        dve.scalar_tensor_tensor(lc[:], csc, SCALE, S.sbias[:, 31:1024:16], ALU.mult, ALU.add)
                        dve.scalar_tensor_tensor(ls[:, 0:1024], S.ps[:, 0:2, :].rearrange("p a n -> p (a n)"), SCALE,
                                                 S.sbias[:, 0:1024], ALU.mult, ALU.add)
                        dve.drain()
                        dve.tensor_reduce(st[:, 0:1], lc[:], X, ALU.max, negate=True)
                        dve.drain().then_inc(m["cmp_logits"], 1)
                        dve.scalar_tensor_tensor(ls[:, 1024:K1], tail, SCALE, S.sbias[:, 1024:K1], ALU.mult, ALU.add)
                        dve.scalar_tensor_tensor(lw[:, 0:512], S.ps[:, 3, :], SCALE, S.sbias[:, 512:1024], ALU.mult, ALU.add)
                        dve.scalar_tensor_tensor(lw[:, 512:KW], wtail, SCALE, S.sbias[:, 1024:K1], ALU.mult, ALU.add)
                        dve.drain()
                        dve.tensor_tensor(lw[:, 0:8], lw[:, 0:8], S.misc[:, 1:9], ALU.add)
                        dve.drain()
                        dve.tensor_reduce(st[:, 4:5], lw[:], X, ALU.max, negate=True)
                        dve.wait_ge(m["cmp_exp"], r1)
                        dve.reciprocal(st[:, 2:3], st[:, 1:2])
                        dve.drain()
                        dve.tensor_scalar(lc[:], lc[:], st[:, 2:3], None, ALU.mult).then_inc(m["cmp_probs"], 1)
                        dve.wait_ge(m["group_summed"], r1)
                        dve.tensor_copy(pext[:, 1:1 + NC], S.ps[:, 6, 0:NC])
                        dve.drain()
                        dve.tensor_reduce(sel[:, 0, :], pext[:, 0:68].rearrange("p (j r) -> p j r", r=4), X, ALU.add)
                        dve.drain()
                        dve.tensor_tensor(sel[:, 0, :], sel[:, 0, :], pext[:, 4:69:4], ALU.add)
                        dve.drain()
                        dve.tensor_reduce(st[:, 3:4], sel[:, 0, 1:15], X, ALU.min)
                        dve.drain()
                        dve.scalar_tensor_tensor(sel[:, 1, 1:15], sel[:, 0, 1:15], st[:, 3:4], S.misc[:, 17:31],
                                                 ALU.is_equal, ALU.mult)
                        dve.drain()
                        dve.tensor_reduce(st[:, 3:4], sel[:, 1, 1:15], X, ALU.max)
                        dve.drain()
                        dve.tensor_scalar(sel[:, 2, :], S.misc[:, 16:33], st[:, 3:4], NEG, ALU.is_equal, ALU.mult)
                        dve.drain()
                        lsv = ls[:, 0:1024].rearrange("p (j l) -> p j l", l=64)
                        dve.tensor_tensor(lsv, lsv, sel[:, 2, 0:16].unsqueeze(2).to_broadcast([P, 16, 64]), ALU.add)
                        dve.drain()
                        dve.tensor_reduce(st[:, 6:7], ls[:], X, ALU.max, negate=True).then_inc(m["logits_ready"], 1)
                        dve.wait_ge(m["cmp_turned"], r1)
                        dve.tensor_copy(pTc[:], S.ps[0:NC, 4, 256:384]).then_inc(m["cmp_values"], 1)
                        for f in (1, 3):
                            dve.wait_ge(m["turn_bank"], (rr * 2 + par) * 4 + f + 1)
                            dve.wait_ge(m["turn_moved"], (rr * 2 + par) * 4 + f)
                            if f == 1:
                                dve.tensor_copy(kT[:, 0, 512:PAST], S.ps[:, 5, :]).then_inc(m["turn_moved"], 1)
                            else:
                                dve.tensor_copy(pTn[:].rearrange("p a n -> p (a n)"), S.ps[0:DEC_T, 5, 0:256]).then_inc(m["turn_moved"], 1)
                        dve.reciprocal(st[:, 8:9], st[:, 7:8])
                        dve.reciprocal(st[:, 9:10], st[:, 5:6])
                        dve.drain()
                        dve.tensor_tensor(st[:, 8:10], st[:, 8:10], S.grow[:, bass.ds(rr * 2 + par, 1), 1:3].rearrange("p a n -> p (a n)"), ALU.mult)
                        dve.wait_ge(m["values_ready"], r1)
                        dve.wait_ge(m["out_free"], r1)
                        dve.tensor_tensor(o[:], S.ps[:, 7, 0:DK], S.grow[:, bass.ds(rr * 2 + par, 1), 0:1].rearrange("p a n -> p (a n)").to_broadcast([P, DK]), ALU.mult)
                        dve.drain()
                        dve.scalar_tensor_tensor(o[:], S.ps[:, 0, 0:DK], st[:, 8:9], o[:], ALU.mult, ALU.add)
                        dve.drain()
                        dve.scalar_tensor_tensor(o[:], S.ps[:, 3, 0:DK], st[:, 9:10], o[:], ALU.mult, ALU.add).then_inc(m["out_ready"], 1)

            @block.scalar
            def _(act):
                with act.Fori(0, 2) as rr:
                    for par in range(2):
                        r1 = rr * 2 + par + 1
                        for f in range(6):
                            bb, part3 = divmod(f, 3)
                            act.wait_ge(m["bank_transposed"], (rr * 2 + par) * 6 + f + 1)
                            dst = kT[:, bb, part3 * 512:(part3 + 1) * 512] if part3 < 2 else wT[:, bb, 0:512]
                            act.activation(dst, S.ps[:, 4 + f % 2, :], ACT.Copy).then_inc(m["bank_moved"], 1)
                        act.wait_ge(m["inverse_ready"], r1)
                        act.activation(kst[:, 1, :], kst[:, 0, :], ACT.Sqrt).then_inc(m["root_ready"], 1)
                        act.wait_ge(m["cmp_logits"], r1)
                        act.activation(lc[:], lc[:], ACT.Exp, bias=st[:, 0:1], accum_out=st[:, 1:2]).then_inc(m["cmp_exp"], 1)
                        act.wait_ge(m["logits_ready"], r1)
                        act.activation(ls[:], ls[:], ACT.Exp, bias=st[:, 6:7], accum_out=st[:, 7:8])
                        act.activation(lw[:], lw[:], ACT.Exp, bias=st[:, 4:5], accum_out=st[:, 5:6]).then_inc(m["exp_ready"], 1)
                        for f in (0, 2):
                            act.wait_ge(m["turn_bank"], (rr * 2 + par) * 4 + f + 1)
                            if f == 0:
                                act.activation(kT[:, 0, 0:512], S.ps[:, 4, :], ACT.Copy).then_inc(m["turn_moved"], 1)
                            else:
                                act.wait_ge(m["turn_moved"], (rr * 2 + par) * 4 + f)
                                act.activation(wT[:, 0, 0:WIN], S.ps[:, 4, :], ACT.Copy).then_inc(m["turn_moved"], 1)

            @block.gpsimd
            def _(pool):
                pool.sem_inc(m["out_free"], 1)
                with pool.Fori(0, 4) as r:
                    pool.wait_ge(m["out_ready"], r + 1)
                    for bb in range(2):
                        pool.dma_start(S.osa_dram[bass.ds(r * 2 + bb, 1)].rearrange("a t h d -> (a h) t d"),
                                       o[bb * 64:(bb + 1) * 64, :]).then_inc(m["out_stored"], 16)
                    pool.wait_ge(m["out_stored"], r * 32 + 32)
                    pool.sem_inc(m["out_free"], 1)
                pool.memset(S.onsa[:, 4, :], 0.0).then_inc(m["final_load"], 1)
                pool.wait_ge(m["final_load"], 1)
                pool.dma_start(S.onsa[0:64, 4, :], S.osa_dram.rearrange("b t h d -> (b t) (h d)")).then_inc(m["out_stored"], 16)
                pool.wait_ge(m["out_stored"], 32 * 4 + 16)


def gla_inputs(nc, S):
    with ExitStack() as ctx:
        aup = sb(nc, ctx, "gi_aup", [RANK, HG * DKG])
        ab = sb(nc, ctx, "gi_ab", [P, 2])
        reset = sb(nc, ctx, "gi_reset", [P, TOK])
        alT = sb(nc, ctx, "gi_alT", [RANK, TOK])
        z = sb(nc, ctx, "gi_z", [P, 2, TOK])
        e = sb(nc, ctx, "gi_e", [P, 2, TOK])
        s_ld = nc.alloc_semaphore("gi_loaded")
        s_tr = nc.alloc_semaphore("gi_transposed")
        s_mv = nc.alloc_semaphore("gi_moved")
        s_zm = nc.alloc_semaphore("gi_logit_summed")
        s_z = nc.alloc_semaphore("gi_logit_ready")
        s_ln = nc.alloc_semaphore("gi_log_ready")
        blocks = [(S.gq[:, p, :], COL["qg"] + p * P) for p in range(2)] + [(S.gk[:, p, :], COL["kg"] + p * P) for p in range(2)]
        with nc.Block() as block:
            @block.sync
            def _(sp):
                sp.dma_start(aup[:], S.gla_a_up[:, :]).then_inc(s_ld, 16)
                with nc.allow_non_contiguous_dma(reason="256 decay biases, one per partition"):
                    sp.dma_start(ab[:], S.gla_a_b.rearrange("(a p) -> p a", p=P)).then_inc(s_ld, 16)
                sp.dma_start(reset[:], S.c_reset.partition_broadcast(P)).then_inc(s_ld, 16)
                sp.dma_start(S.gmask[:], S.c_gmask.rearrange("a p n -> p a n")).then_inc(s_ld, 16)
                sp.dma_start(S.seqof[:], S.c_seqof[:, :]).then_inc(s_ld, 16)
                for p in range(2):
                    sp.dma_start(S.gs[:, p], S.state_gla.rearrange("b (a h) k v -> a (h k) b v", a=2)[p]).then_inc(s_ld, 16)

            @block.tensor
            def _(pe):
                for t in range(NT):
                    tr = pe.transpose(S.ps2[0:RANK, 0, t * P:(t + 1) * P],
                                      S.pj[:, t, COL["al"]:COL["al"] + RANK], S.ident[:])
                tr.then_inc(s_tr, 1)
                for i, (_, c) in enumerate(blocks):
                    if i >= 1:
                        pe.wait_ge(s_mv, i + 1)
                    for t in range(NT):
                        tr = pe.transpose(S.ps2[:, 1, t * P:(t + 1) * P], S.pj[:, t, c:c + P], S.ident[:])
                    tr.then_inc(s_tr, 1)
                pe.wait_ge(s_ld, 16 * 7)
                for p in range(2):
                    pe.matmul(S.ps2[:, 2 + p, 0:512], aup[:, p * P:(p + 1) * P], alT[:, 0:512], start=True, stop=True)
                    mm = pe.matmul(S.ps2[:, 2 + p, 512:TOK], aup[:, p * P:(p + 1) * P], alT[:, 512:TOK], start=True, stop=True)
                mm.then_inc(s_zm, 1)

            @block.vector
            def _(dve):
                dve.wait_ge(s_tr, 1)
                dve.tensor_copy(alT[:], S.ps2[0:RANK, 0, 0:TOK]).then_inc(s_mv, 1)
                for i, (dst, _) in enumerate(blocks):
                    dve.wait_ge(s_tr, i + 2)
                    dve.tensor_copy(dst, S.ps2[:, 1, 0:TOK]).then_inc(s_mv, 1)
                dve.wait_ge(s_zm, 1)
                for p in range(2):
                    dve.tensor_scalar(z[:, p, :], S.ps2[:, 2 + p, 0:TOK], ab[:, p:p + 1], None, ALU.add)
                dve.drain().then_inc(s_z, 1)
                dve.wait_ge(s_ln, 1)
                dve.scalar_tensor_tensor(z[:], z[:], 0.0, e[:], ALU.min, ALU.subtract)
                dve.drain()
                dve.tensor_scalar(z[:], z[:], 1.0 / TAU, None, ALU.mult)
                dve.drain()
                for p in range(2):
                    dve.tensor_tensor_scan(S.gb[:, p, :], reset[:], z[:, p, :], 0.0, ALU.mult, ALU.add)

            @block.scalar
            def _(act):
                act.wait_ge(s_z, 1)
                act.activation(e[:], z[:], ACT.Abs)
                act.drain()
                act.activation(e[:], e[:], ACT.Exp, scale=-1.0)
                act.drain()
                act.activation(e[:], e[:], ACT.Ln, bias=S.ones[:, 0:1]).then_inc(s_ln, 1)


def gla_chunks(nc, S):
    GRP, NG, CLAMP, QS = 8, P // 8, 40.0, DKG ** -0.5
    with ExitStack() as ctx:
        bs = sb(nc, ctx, "gc_b", [P, 2, P])
        qs = sb(nc, ctx, "gc_q", [P, 2, P])
        ks = sb(nc, ctx, "gc_k", [P, 2, P])
        dq = sb(nc, ctx, "gc_dq", [P, 2, P])
        de = sb(nc, ctx, "gc_de", [P, 2, P])
        eb = sb(nc, ctx, "gc_eb", [P, 2, P])
        qt = sb(nc, ctx, "gc_qt", [P, 2, P])
        qe = sb(nc, ctx, "gc_qe", [P, 2, P])
        ke = sb(nc, ctx, "gc_ke", [P, 2, P])
        keT = sb(nc, ctx, "gc_keT", [P, 2, P])
        kt = sb(nc, ctx, "gc_kt", [P, 2, NG, P])
        at = sb(nc, ctx, "gc_at", [P, HG, P])
        vs = sb(nc, ctx, "gc_v", [P, HG * DVG])
        st = sb(nc, ctx, "gc_state", [P, 2, DVG])
        qb = sb(nc, ctx, "gc_qb", [P, 2, DEC_B, P])
        vb = sb(nc, ctx, "gc_vb", [P, 2, DEC_B, DVG])
        s_df = nc.alloc_semaphore("gc_exponents_ready")
        s_ex = nc.alloc_semaphore("gc_exps_ready")
        s_fa = nc.alloc_semaphore("gc_factors_ready")
        s_at = nc.alloc_semaphore("gc_attention_summed")
        s_am = nc.alloc_semaphore("gc_attention_masked")
        s_o = nc.alloc_semaphore("gc_outputs_summed")
        s_sv = nc.alloc_semaphore("gc_state_ready")
        s_vb = nc.alloc_semaphore("gc_split_values_ready")
        s_kv = nc.alloc_semaphore("gc_sample_state_summed")
        s_new = nc.alloc_semaphore("gc_sample_state_ready")
        s_out = nc.alloc_semaphore("gc_states_stored")
        CH = SEQ // P
        V = COL["vg"]

        def factors_dve(dve, c, n, sample):
            dve.tensor_copy(bs[:], S.gb[:, :, c])
            dve.tensor_copy(qs[:], S.gq[:, :, c])
            dve.tensor_copy(ks[:], S.gk[:, :, c])
            dve.drain()
            groups = bs[:].rearrange("p a (n e) -> p (a n) e", e=GRP)
            ref = groups[:, :, 3:4]
            dve.tensor_tensor(dq[:].rearrange("p a (n e) -> p (a n) e", e=GRP), groups,
                              ref.to_broadcast([P, 2 * NG, GRP]), ALU.subtract)
            for a in range(2):
                dve.tensor_tensor(kt[:, a], bs[:, a, 3::GRP].unsqueeze(2).to_broadcast([P, NG, P]),
                                  bs[:, a:a + 1, :].to_broadcast([P, NG, P]), ALU.subtract)
            if sample:
                dve.tensor_tensor(de[:].rearrange("p a (n e) -> p (a n) e", e=GRP),
                                  groups[:, :, GRP - 1:GRP].to_broadcast([P, 2 * NG, GRP]), groups, ALU.subtract)
            else:
                dve.tensor_tensor(de[:], bs[:, :, P - 1:P].to_broadcast([P, 2, P]), bs[:], ALU.subtract)
            dve.drain()
            dve.tensor_scalar(dq[:], dq[:], CLAMP, None, ALU.min)
            dve.tensor_scalar(kt[:], kt[:], CLAMP, None, ALU.min)
            dve.drain().then_inc(s_df, 1)
            dve.wait_ge(s_ex, n)
            dve.scalar_tensor_tensor(qt[:], qs[:], QS, dq[:], ALU.mult, ALU.mult)
            dve.scalar_tensor_tensor(qe[:], qs[:], QS, eb[:], ALU.mult, ALU.mult)
            dve.tensor_tensor(ke[:], ks[:], de[:], ALU.mult)
            for a in range(2):
                dve.tensor_tensor(kt[:, a], kt[:, a], ks[:, a:a + 1, :].to_broadcast([P, NG, P]), ALU.mult)
            if sample:
                dve.drain()
                for a in range(2):
                    for b in range(DEC_B):
                        dve.tensor_copy(qb[:, a, b, b * GRP:(b + 1) * GRP], qe[:, a, b * GRP:(b + 1) * GRP])
            dve.drain().then_inc(s_fa, 1)
            dve.wait_ge(s_at, n)
            dve.tensor_tensor(at[:], S.ps[:, 0:4, 0:P], S.gmask[:, int(sample)].unsqueeze(1).to_broadcast([P, HG, P]), ALU.mult)
            dve.tensor_copy(keT[:], S.ps[:, 4, 0:256].rearrange("p (a n) -> p a n", a=2))
            dve.drain().then_inc(s_am, 1)

        def exps_act(act, n):
            act.wait_ge(s_df, n)
            act.activation(dq[:], dq[:], ACT.Exp)
            act.activation(de[:], de[:], ACT.Exp)
            act.activation(eb[:], bs[:], ACT.Exp)
            act.activation(kt[:], kt[:], ACT.Exp)
            act.drain().then_inc(s_ex, 1)

        def attention_pe(pe, n):
            pe.wait_ge(s_fa, n)
            for i in range(NG):
                for h in range(HG):
                    a, r = h // 2, slice(64 * (h % 2), 64 * (h % 2) + 64)
                    mm = pe.matmul(S.ps[:, h, i * GRP:(i + 1) * GRP], kt[r, a, i, :], qt[r, a, i * GRP:(i + 1) * GRP],
                                   start=True, stop=True)
            for a in range(2):
                mm = pe.transpose(S.ps[:, 4, a * P:(a + 1) * P], ke[:, a, :], S.ident[:])
            mm.then_inc(s_at, 1)

        with nc.Block() as block:
            @block.vector
            def _(dve):
                dve.memset(st[:], 0.0)
                dve.memset(qb[:], 0.0)
                dve.drain()
                with dve.Fori(0, CH) as c:
                    dve.tensor_copy(vs[:], S.pj[:, bass.ds(c, 1), V:V + HG * DVG].rearrange("p t v -> p (t v)"))
                    factors_dve(dve, bass.ds(c * P, P), c + 1, False)
                    dve.wait_ge(s_o, c + 1)
                    dve.tensor_copy(S.ogla[:, bass.ds(c, 1), :].rearrange("p t (h v) -> p (t h) v", h=HG), S.ps[:, 0:4, P:2 * P])
                    for a in range(2):
                        dve.scalar_tensor_tensor(st[:, a, :], st[:, a, :], eb[:, a, P - 1:P], S.ps[:, 5 + a, 0:DVG],
                                                 ALU.mult, ALU.add)
                    dve.drain().then_inc(s_sv, 1)
                factors_dve(dve, slice(SEQ, SEQ + P), CH + 1, True)
                dve.wait_ge(s_o, CH + 1)
                dve.tensor_copy(S.ogla[:, CH, :].rearrange("p (h v) -> p h v", h=HG), S.ps[:, 0:4, P:2 * P])
                for a in range(2):
                    if a:
                        dve.wait_ge(s_kv, a)
                    for h in range(2):
                        hv = V + (2 * a + h) * DVG
                        dve.tensor_tensor(vb[:, h], S.pj[:, CH, hv:hv + DVG].unsqueeze(1).to_broadcast([P, DEC_B, DVG]),
                                          S.seqof[:].unsqueeze(2).to_broadcast([P, DEC_B, DVG]), ALU.mult)
                    dve.drain().then_inc(s_vb, 1)
                for a in range(2):
                    dve.tensor_tensor(S.gs[:, a], S.gs[:, a],
                                      eb[:, a, GRP - 1:64:GRP].unsqueeze(2).to_broadcast([P, DEC_B, DVG]), ALU.mult)
                dve.drain()
                dve.wait_ge(s_kv, 2)
                for a in range(2):
                    g2 = S.gs[:, a].rearrange("p b v -> p (b v)")
                    dve.tensor_tensor(g2, g2, S.ps2[:, a, :] if a == 0 else S.ps2[:, 3, :], ALU.add)
                dve.drain().then_inc(s_new, 1)

            @block.scalar
            def _(act):
                with act.Fori(0, CH) as c:
                    exps_act(act, c + 1)
                exps_act(act, CH + 1)

            @block.tensor
            def _(pe):
                with pe.Fori(0, CH) as c:
                    attention_pe(pe, c + 1)
                    pe.wait_ge(s_am, c + 1)
                    for h in range(HG):
                        a, r = h // 2, slice(64 * (h % 2), 64 * (h % 2) + 64)
                        v = vs[:, h * DVG:(h + 1) * DVG]
                        pe.matmul(S.ps[:, h, P:2 * P], at[:, h, :], v, start=True, stop=False)
                        pe.matmul(S.ps[r, 5 + a, 0:DVG], keT[:, a, r], v, start=True, stop=True)
                    for h in range(HG):
                        a, r = h // 2, slice(64 * (h % 2), 64 * (h % 2) + 64)
                        mm = pe.matmul(S.ps[:, h, P:2 * P], qe[r, a, :], st[r, a, :], start=False, stop=True)
                    mm.then_inc(s_o, 1)
                    pe.wait_ge(s_sv, c + 1)
                attention_pe(pe, CH + 1)
                pe.wait_ge(s_am, CH + 1)
                for h in range(HG):
                    a, r = h // 2, slice(64 * (h % 2), 64 * (h % 2) + 64)
                    pe.matmul(S.ps[:, h, P:2 * P], at[:, h, :], S.pj[:, CH, V + h * DVG:V + (h + 1) * DVG], start=True, stop=False)
                    for b in range(DEC_B):
                        mm = pe.matmul(S.ps[:, h, P:2 * P], qb[r, a, b, :], S.gs[r, a, b, :], start=False, stop=(b == DEC_B - 1))
                mm.then_inc(s_o, 1)
                for a in range(2):
                    pe.wait_ge(s_vb, a + 1)
                    out = S.ps2[:, 0, :] if a == 0 else S.ps2[:, 3, :]
                    for h in range(2):
                        for w in range(2):
                            mm = pe.matmul(out[64 * h:64 * h + 64, w * 512:(w + 1) * 512], keT[:, a, 64 * h:64 * h + 64],
                                           vb[:, h, 4 * w:4 * w + 4, :].rearrange("p b v -> p (b v)"), start=True, stop=True)
                    mm.then_inc(s_kv, 1)

            @block.sync
            def _(sp):
                sp.wait_ge(s_sv, CH)
                sp.dma_start(S.gla_prompt[0].rearrange("(a h) k v -> (h k) a v", a=2), st[:]).then_inc(s_out, 16)
                sp.wait_ge(s_new, 1)
                for a in range(2):
                    sp.dma_start(S.gla_sample.rearrange("b (a h) k v -> a (h k) b v", a=2)[a], S.gs[:, a]).then_inc(s_out, 16)
                sp.wait_ge(s_out, 48)


def gla_finish(nc, S):
    with ExitStack() as ctx:
        sq = sb(nc, ctx, "gf_sq", [P, NT, HG * DVG])
        gain = sb(nc, ctx, "gf_gain", [P, DVG])
        st = sb(nc, ctx, "gf_st", [P, 2, NT, HG])
        s_ld = nc.alloc_semaphore("gf_loaded")
        s_inv = nc.alloc_semaphore("gf_inverse_ready")
        s_rt = nc.alloc_semaphore("gf_root_ready")
        o4 = S.ogla.rearrange("p t (h v) -> p t h v", h=HG)
        q4 = sq[:].rearrange("p t (h v) -> p t h v", h=HG)
        with nc.Block() as block:
            @block.sync
            def _(sp):
                sp.dma_start(gain[:], S.gla_out_g.partition_broadcast(P)).then_inc(s_ld, 16)

            @block.vector
            def _(dve):
                dve.tensor_tensor(sq[:], S.ogla, S.ogla, ALU.mult)
                dve.drain()
                dve.tensor_reduce(st[:, 0], q4, X, ALU.add)
                dve.drain()
                dve.tensor_scalar(st[:, 0], st[:, 0], 1.0 / DVG, EPS, ALU.mult, ALU.add)
                dve.drain()
                dve.reciprocal(st[:, 0], st[:, 0]).then_inc(s_inv, 1)
                dve.wait_ge(s_rt, 1)
                dve.tensor_tensor(o4, o4, st[:, 1].unsqueeze(3).to_broadcast([P, NT, HG, DVG]), ALU.mult)
                dve.drain()
                dve.wait_ge(s_ld, 16)
                dve.tensor_tensor(o4, o4, gain[:].unsqueeze(1).unsqueeze(1).to_broadcast([P, NT, HG, DVG]), ALU.mult)
                dve.wait_ge(s_rt, 2)
                dve.drain()
                dve.tensor_tensor(S.ogla, S.ogla, sq[:], ALU.mult)

            @block.scalar
            def _(act):
                act.wait_ge(s_inv, 1)
                act.activation(st[:, 1], st[:, 0], ACT.Sqrt).then_inc(s_rt, 1)
                act.activation(sq[:], part(S, "rg"), ACT.Silu).then_inc(s_rt, 1)


def mix_out(nc, S):
    with ExitStack() as ctx:
        w = sb(nc, ctx, "w_out_sb", [P, KD, D])
        mixT = sb(nc, ctx, "mixT", [P, KD, TOK])
        gcol = sb(nc, ctx, "mo_gain", [P, KD])
        st = sb(nc, ctx, "mo_st", [P, 2, NT])
        junk = sb(nc, ctx, "mo_junk", [P, H * DK])
        s_w = nc.alloc_semaphore("mo_loaded")
        s_g = nc.alloc_semaphore("mo_gains_loaded")
        s_z = nc.alloc_semaphore("mo_zeroed")
        s_sum = nc.alloc_semaphore("mo_squares_summed")
        s_ms = nc.alloc_semaphore("mo_mean_ready")
        s_rs = nc.alloc_semaphore("mo_rstd_ready")
        s_xn = nc.alloc_semaphore("mo_scaled")
        s_tr = nc.alloc_semaphore("mo_chunk_transposed")
        s_ev = nc.alloc_semaphore("mo_chunk_moved")
        s_mm = nc.alloc_semaphore("mo_bank_ready")
        s_free = nc.alloc_semaphore("mo_bank_free")
        with nc.Block() as block:
            @block.sync
            def _(sp):
                with nc.allow_non_contiguous_dma(reason="512 gains, one per partition and chunk"):
                    sp.dma_start(gcol[:, 0:4], S.nsa_out_g.rearrange("(k p) -> p k", p=P)).then_inc(s_g, 16)
                sp.dma_start(S.x1[:, 0:4, :], S.x_prompt[0].rearrange("(t p) d -> p t d", p=P)).then_inc(s_w, 16)
                for k in range(KD):
                    sp.dma_start(w[:, k, :], S.w_out[k * P:(k + 1) * P, :]).then_inc(s_w, 16)
                sp.wait_ge(s_z, 1)
                sp.dma_start(S.x1[0:64, 4, :], S.x_sample.rearrange("b t d -> (b t) d")).then_inc(s_w, 16)

            @block.scalar
            def _(act):
                for t in range(NT):
                    act.activation(junk[:], S.onsa[:, t, :], ACT.Square, accum_out=st[:, 0, t:t + 1])
                    act.drain()
                act.drain().then_inc(s_sum, 1)
                act.wait_ge(s_ms, 1)
                act.activation(st[:, 0, :], st[:, 1, :], ACT.Sqrt).then_inc(s_rs, 1)
                act.wait_ge(s_g, 16)
                for k in range(KD):
                    act.wait_ge(s_tr, k + 1)
                    act.activation(mixT[:, k, :], S.ps2[:, k % 4, 0:TOK], ACT.Copy,
                                   scale=gcol[:, k:k + 1] if k < 4 else 1.0).then_inc(s_ev, 1)

            @block.vector
            def _(dve):
                dve.memset(S.x1[:, 4, :], 0.0).then_inc(s_z, 1)
                dve.sem_inc(s_free, NT)
                dve.wait_ge(s_sum, 1)
                dve.tensor_scalar(st[:, 1, :], st[:, 0, :], 1.0 / (H * DK), EPS, ALU.mult, ALU.add)
                dve.drain()
                dve.reciprocal(st[:, 1, :], st[:, 1, :]).then_inc(s_ms, 1)
                dve.wait_ge(s_rs, 1)
                for t in range(NT):
                    dve.tensor_scalar(S.onsa[:, t, :], S.onsa[:, t, :], st[:, 0, t:t + 1], None, ALU.mult)
                dve.drain().then_inc(s_xn, 1)
                dve.wait_ge(s_w, 16 * (KD + 2))
                with dve.Fori(0, 2) as c:
                    for t in range(NT):
                        dve.wait_ge(s_mm, c * NT + t + 1)
                        x = S.x1[:, t, bass.ds(c * 512, 512)]
                        dve.tensor_tensor(x, S.ps[:, t, :], x, ALU.add).then_inc(s_free, 1)

            @block.tensor
            def _(pe):
                pe.wait_ge(s_xn, 1)
                for k in range(KD):
                    if k >= 4:
                        pe.wait_ge(s_ev, k - 3)
                    for t in range(NT):
                        tr = pe.transpose(S.ps2[:, k % 4, t * P:(t + 1) * P], S.mix[:, t, k * P:(k + 1) * P], S.ident[:])
                    tr.then_inc(s_tr, 1)
                pe.wait_ge(s_ev, KD)
                pe.wait_ge(s_w, 16 * (KD + 2))
                with pe.Fori(0, 2) as c:
                    for t in range(NT):
                        pe.wait_ge(s_free, c * NT + t + 1)
                        for k in range(KD):
                            mm = pe.matmul(S.ps[:, t, :], mixT[:, k, t * P:(t + 1) * P], w[:, k, bass.ds(c * 512, 512)],
                                           start=(k == 0), stop=(k == KD - 1))
                        mm.then_inc(s_mm, 1)


ROWS = [P] * (NT - 1) + [DEC_B * DEC_T]
GONE = -3e38


def peer_select(nc, S):
    HALF = PQ // 2
    with ExitStack() as ctx:
        wq = sb(nc, ctx, "ps_wq", [P, 2, KD, PQ])
        kk = sb(nc, ctx, "ps_keys", [P, 2, 2, HALF])
        kT = sb(nc, ctx, "ps_keysT", [P, 2, NKEY])
        gcol = sb(nc, ctx, "ps_gain", [P, 2])
        qg = sb(nc, ctx, "ps_qg", [P, 2, NTOK])
        sq = sb(nc, ctx, "ps_sq", [P, 2, NTOK])
        rs = sb(nc, ctx, "ps_rs", [P, 2, NT])
        sc = sb(nc, ctx, "ps_scores", [P, NT, 2, NKEY])
        sc2 = sb(nc, ctx, "ps_scores_rest", [P, NT, 2, NKEY])
        val = sb(nc, ctx, "ps_val", [P, NT, 2, TOPK])
        idx = sb(nc, ctx, "ps_idx", [P, NT, 2, TOPK], U32)
        idf = sb(nc, ctx, "ps_idf", [P, NT, 2, TOPK])
        cand = sb(nc, ctx, "ps_cand", [P, NT, TOPK, TOPK])
        cand2 = sb(nc, ctx, "ps_cand_rest", [P, NT, TOPK, TOPK])
        best = sb(nc, ctx, "ps_best", [P, NT, TOPK])
        ci = sb(nc, ctx, "ps_ci", [P, NT, TOPK], U32)
        cab = sb(nc, ctx, "ps_cab", [P, 2, NT, TOPK], U32)
        caf = sb(nc, ctx, "ps_caf", [P, 2, NT, TOPK])
        hot = sb(nc, ctx, "ps_hot", [P, NT * TOPK, TOPK])
        s_g = nc.alloc_semaphore("ps_gain_loaded")
        s_ld = [nc.alloc_semaphore("ps_even_head_loaded"), nc.alloc_semaphore("ps_odd_head_loaded")]
        s_q = nc.alloc_semaphore("ps_query_summed")
        s_qg = nc.alloc_semaphore("ps_query_scaled")
        s_sq = nc.alloc_semaphore("ps_squares_ready")
        s_kt = nc.alloc_semaphore("ps_keys_transposed")
        s_ke = nc.alloc_semaphore("ps_keys_moved")
        s_ss = nc.alloc_semaphore("ps_squares_summed")
        s_iv = nc.alloc_semaphore("ps_inverse_ready")
        s_rt = nc.alloc_semaphore("ps_root_ready")
        s_sc = nc.alloc_semaphore("ps_scores_summed")
        s_sv = nc.alloc_semaphore("ps_scores_moved")
        score = S.ps[:, 4:7, :].rearrange("p a (b n) -> p (a b) n", b=2)
        with nc.Block() as block:
            @block.sync
            def _(sp):
                with nc.allow_non_contiguous_dma(reason="256 gains, one per partition and half"):
                    sp.dma_start(gcol[:], S.peer_qn_g.rearrange("(a p) -> p a", p=P)).then_inc(s_g, 16)
                with sp.Fori(0, PH // 2) as i:
                    for par in range(2):
                        h = i * 2 + par
                        sp.wait_ge(s_sv, h + 1)
                        sp.dma_start(wq[:, par], S.peer_wq[:, bass.ds(h * PQ, PQ)].rearrange("(k p) n -> p k n", p=P)).then_inc(s_ld[par], 16)
                        sp.dma_start(kk[:, par, 0], S.peer_k1[bass.ds(h, 1)].rearrange("a k d -> (a k) d")).then_inc(s_ld[par], 16)
                        sp.dma_start(kk[:, par, 1], S.peer_k2[bass.ds(h, 1)].rearrange("a k d -> (a k) d")).then_inc(s_ld[par], 16)

            @block.tensor
            def _(pe):
                with pe.Fori(0, PH // 2) as i:
                    for par in range(2):
                        n = i * 2 + par + 1
                        pe.wait_ge(s_ld[par], (i + 1) * 48)
                        for a in range(2):
                            for lo, hi in ((0, SEQ), (SEQ, NTOK)):
                                for k in range(KD):
                                    mm = pe.matmul(S.ps2[:, a, lo:hi], wq[:, par, k, a * HALF:(a + 1) * HALF],
                                                   S.h2T[:, k, lo:hi], start=(k == 0), stop=(k == KD - 1))
                        mm.then_inc(s_q, 1)
                        pe.wait_ge(s_sv, n + 1)
                        for a in range(2):
                            tr = pe.transpose(S.ps[:, 7, a * P:(a + 1) * P], kk[:, par, a], S.ident[:])
                        tr.then_inc(s_kt, 1)
                        pe.wait_ge(s_ke, n)
                        pe.wait_ge(s_sq, n)
                        for t, m in enumerate(ROWS):
                            for a in range(2):
                                mm = pe.matmul(S.ps[0:m, 7, 256 + t:257 + t], sq[:, a, t * P:t * P + m], S.ones[:],
                                               start=(a == 0), stop=(a == 1))
                        mm.then_inc(s_ss, 1)
                        pe.wait_ge(s_qg, n)
                        for t, m in enumerate(ROWS):
                            for a in range(2):
                                mm = pe.matmul(score[0:m, t, a * NKEY:(a + 1) * NKEY], qg[:, a, t * P:t * P + m], kT[:, a],
                                               start=True, stop=True)
                        mm.then_inc(s_sc, 1)

            @block.scalar
            def _(act):
                with act.Fori(0, PH) as h:
                    act.wait_ge(s_q, h + 1)
                    act.activation(sq[:], S.ps2[:, 0:2, 0:NTOK], ACT.Square).then_inc(s_sq, 1)
                    act.wait_ge(s_iv, h + 1)
                    act.activation(rs[:, 1, :], rs[:, 0, :], ACT.Sqrt).then_inc(s_rt, 1)

            @block.vector
            def _(dve):
                for buf in (rs, sc, sc2, val, idf, cand, cand2, best):
                    dve.memset(buf[:], 0.0)
                dve.memset(idx[:], 0)
                dve.memset(ci[:], 0)
                dve.drain()
                dve.sem_inc(s_sv, 2)
                dve.wait_ge(s_g, 16)
                def query(h):
                    dve.wait_ge(s_q, h + 1)
                    dve.wait_ge(s_sq, h + 1)
                    for a in range(2):
                        dve.tensor_scalar(qg[:, a, :], S.ps2[:, a, 0:NTOK], gcol[:, a:a + 1], None, ALU.mult)
                    dve.drain().then_inc(s_qg, 1)
                    dve.wait_ge(s_kt, h + 1)
                    dve.tensor_copy(kT[:], S.ps[:, 7, 0:256].rearrange("p (a n) -> p a n", a=2)).then_inc(s_ke, 1)
                    dve.wait_ge(s_ss, h + 1)
                    for rows, t0, t1 in ((P, 0, NT - 1), (ROWS[-1], NT - 1, NT)):
                        dve.tensor_scalar(rs[0:rows, 0, t0:t1], S.ps[0:rows, 7, 256 + t0:256 + t1], 1.0 / PQ, EPS, ALU.mult, ALU.add)
                    dve.drain()
                    dve.reciprocal(rs[:, 0, 0:NT - 1], rs[:, 0, 0:NT - 1])
                    dve.reciprocal(rs[0:ROWS[-1], 0, NT - 1:NT], rs[0:ROWS[-1], 0, NT - 1:NT])
                    dve.drain().then_inc(s_iv, 1)

                def head(h, more):
                    dve.wait_ge(s_sc, h + 1)
                    dve.wait_ge(s_rt, h + 1)
                    for rows, t0, t1 in ((P, 0, NT - 1), (ROWS[-1], NT - 1, NT)):
                        dve.tensor_tensor(sc[0:rows, t0:t1].rearrange("p t a n -> p t (a n)"), score[0:rows, t0:t1, :],
                                          rs[0:rows, 1, t0:t1].unsqueeze(2).to_broadcast([rows, t1 - t0, 2 * NKEY]), ALU.mult)
                    dve.drain().then_inc(s_sv, 1)
                    top16(dve, [(sc[0:m, t, a], sc2[0:m, t, a], val[0:m, t, a], idx[0:m, t, a])
                                for t, m in enumerate(ROWS) for a in range(2)])
                    dve.tensor_copy(idf[:], idx[:])
                    for t in range(NT):
                        dve.tensor_tensor(cand[:, t], val[:, t, 0].unsqueeze(2).to_broadcast([P, TOPK, TOPK]),
                                          val[:, t, 1].unsqueeze(1).to_broadcast([P, TOPK, TOPK]), ALU.add)
                    dve.drain()
                    if more:
                        query(h + 1)
                    top16(dve, [(cand[0:m, t].rearrange("p a b -> p (a b)"), cand2[0:m, t].rearrange("p a b -> p (a b)"),
                                 best[0:m, t], ci[0:m, t]) for t, m in enumerate(ROWS)])
                    dve.tensor_scalar(cab[:, 0], ci[:], 4, None, ALU.logical_shift_right)
                    dve.tensor_scalar(cab[:, 1], ci[:], 15, None, ALU.bitwise_and)
                    dve.tensor_copy(S.best[:, :, bass.ds(h, 1), :].rearrange("p t h k -> p t (h k)"), best[:])
                    dve.drain()
                    dve.tensor_copy(caf[:], cab[:])
                    dve.drain()
                    for a in range(2):
                        dve.tensor_tensor(hot[:], caf[:, a].rearrange("p t k -> p (t k)").unsqueeze(2).to_broadcast([P, NT * TOPK, TOPK]),
                                          S.iota[:, 0:TOPK].unsqueeze(1).to_broadcast([P, NT * TOPK, TOPK]), ALU.is_equal)
                        dve.drain()
                        h4 = hot[:].rearrange("p (t k) r -> p t k r", t=NT)
                        dve.tensor_tensor(h4, h4, idf[:, :, a].unsqueeze(2).to_broadcast([P, NT, TOPK, TOPK]), ALU.mult)
                        dve.drain()
                        dve.tensor_reduce(S.sel[:, a, :, bass.ds(h, 1), :].rearrange("p t h k -> p t (h k)"), h4, X, ALU.add)
                        dve.drain()

                query(0)
                with dve.Fori(0, PH - 1) as h:
                    head(h, True)
                head(PH - 1, False)


def top16(dve, lists):
    for src, rest, val, idx in lists:
        dve.max(val[:, 0:8], src)
    dve.drain()
    for src, rest, val, idx in lists:
        dve.max_index(idx[:, 0:8], val[:, 0:8], src)
        dve.match_replace(rest, val[:, 0:8], src, GONE)
    dve.drain()
    for src, rest, val, idx in lists:
        dve.max(val[:, 8:16], rest)
    dve.drain()
    for src, rest, val, idx in lists:
        dve.max_index(idx[:, 8:16], val[:, 8:16], rest)
    dve.drain()


def peer_gates(nc, S):
    with ExitStack() as ctx:
        s1 = sb(nc, ctx, "pg_sum", [P, NT * PH])
        s_df = nc.alloc_semaphore("pg_shifted")
        s_ex = nc.alloc_semaphore("pg_exp_ready")
        s_gt = nc.alloc_semaphore("pg_gates_ready")
        s_tr = nc.alloc_semaphore("pg_block_transposed")
        s_ev = nc.alloc_semaphore("pg_block_moved")
        b3 = S.best[:].rearrange("p t h k -> p (t h) k")
        srcs = [S.sel[:, 0], S.sel[:, 1], S.best[:]]
        with nc.Block() as block:
            @block.vector
            def _(dve):
                dve.tensor_tensor(S.gate16[:], b3, b3[:, :, 0:1].to_broadcast([P, NT * PH, TOPK]), ALU.subtract).then_inc(s_df, 1)
                dve.wait_ge(s_ex, 1)
                dve.tensor_reduce(s1[:], S.gate16[:], X, ALU.add)
                dve.drain()
                dve.reciprocal(s1[:], s1[:])
                dve.drain()
                dve.tensor_tensor(b3, S.gate16[:], s1[:].unsqueeze(2).to_broadcast([P, NT * PH, TOPK]), ALU.mult).then_inc(s_gt, 1)
                for i in range(3):
                    dve.wait_ge(s_tr, i + 1)
                    dve.tensor_copy(S.selT[:, i, :], S.ps2[:, i, 0:NTOK]).then_inc(s_ev, 1)

            @block.scalar
            def _(act):
                act.wait_ge(s_df, 1)
                act.activation(S.gate16[:], S.gate16[:], ACT.Exp).then_inc(s_ex, 1)

            @block.tensor
            def _(pe):
                pe.wait_ge(s_gt, 1)
                for i, src in enumerate(srcs):
                    for t in range(NT):
                        tr = pe.transpose(S.ps2[:, i, t * P:(t + 1) * P], src[:, t].rearrange("p h k -> p (h k)"), S.ident[:])
                    tr.then_inc(s_tr, 1)


NBLK = 64
BLOCKS = NTOK // NBLK


def peer_gate_matrix(nc, S):
    STEP = 8
    ITS = NBLK // (2 * STEP)
    with ExitStack() as ctx:
        i1 = sb(nc, ctx, "gm_index1", [P, 2, STEP])
        own = sb(nc, ctx, "gm_index1_pool", [P, 2, STEP])
        zero = sb(nc, ctx, "gm_zero", [P, STEP])
        o1 = sb(nc, ctx, "gm_one_hot1", [P, 2, STEP, NKEY])
        o2 = sb(nc, ctx, "gm_gated_hot2", [P, 2, STEP, NKEY])
        gt = sb(nc, ctx, "gm_block", [P, 3, NKEY, NBLK])
        s_i1 = nc.alloc_semaphore("gm_index1_ready")
        s_o1 = nc.alloc_semaphore("gm_one_hot1_ready")
        s_o2 = nc.alloc_semaphore("gm_gated_hot2_ready")
        s_mm = nc.alloc_semaphore("gm_bank_ready")
        s_ev = nc.alloc_semaphore("gm_bank_moved")
        s_st = [nc.alloc_semaphore(f"gm_block{i}_stored") for i in range(3)]
        with nc.Block() as block:
            @block.vector
            def _(dve):
                dve.sem_inc(s_mm, 4)
                with dve.Fori(0, NTOK // (2 * STEP)) as i:
                    for par in range(2):
                        m = i * 2 + par
                        dve.wait_ge(s_mm, m * 2 + 2)
                        dve.tensor_copy(i1[:, par], S.selT[:, 0, bass.ds(m * STEP, STEP)]).then_inc(s_i1, 1)
                        for j in range(STEP):
                            n = m * STEP + j
                            dve.tensor_scalar(o2[:, par, j], S.iota[:], S.selT[:, 1, bass.ds(n, 1)],
                                              S.selT[:, 2, bass.ds(n, 1)], ALU.is_equal, ALU.mult).then_inc(s_o2, 1)

            @block.gpsimd
            def _(pool):
                pool.memset(zero[:], 0.0)
                pool.drain()
                with pool.Fori(0, NTOK // (2 * STEP)) as i:
                    for par in range(2):
                        pool.wait_ge(s_i1, i * 2 + par + 1)
                        pool.tensor_tensor(own[:, par], i1[:, par], zero[:], ALU.add)
                        pool.drain()
                        for j in range(STEP):
                            pool.tensor_scalar(o1[:, par, j], S.iota[:], own[:, par, j:j + 1], None, ALU.is_equal).then_inc(s_o1, 1)

            @block.tensor
            def _(pe):
                with pe.Fori(0, NTOK // (2 * STEP)) as i:
                    for par in range(2):
                        m = i * 2 + par
                        for half in range(2):
                            pe.wait_ge(s_o1, m * STEP + half * 4 + 4)
                            pe.wait_ge(s_o2, m * STEP + half * 4 + 4)
                            pe.wait_ge(s_ev, m * 2 + half + 1)
                            for j in range(4):
                                mm = pe.matmul(S.ps[:, par * 2 + half, j * P:(j + 1) * P], o1[:, par, half * 4 + j],
                                               o2[:, par, half * 4 + j], start=True, stop=True)
                            mm.then_inc(s_mm, 1)

            @block.scalar
            def _(act):
                act.sem_inc(s_ev, 4)
                with act.Fori(0, BLOCKS // 3) as b:
                    for part in range(3):
                        act.wait_ge(s_st[part], b * 16 + 16)
                        with act.Fori(0, ITS) as i:
                            for q in range(4):
                                act.wait_ge(s_mm, (b * 3 + part) * 4 * ITS + i * 4 + q + 5)
                                act.activation(gt[:, part, :, bass.ds(i * 2 * STEP + q * 4, 4)],
                                               S.ps[:, q, :].rearrange("p (j n) -> p n j", j=4), ACT.Copy).then_inc(s_ev, 1)

            @block.sync
            def _(sp):
                for part in range(3):
                    sp.sem_inc(s_st[part], 16)
                with sp.Fori(0, BLOCKS // 3) as b:
                    for part in range(3):
                        sp.wait_ge(s_ev, (b * 3 + part) * 4 * ITS + 4 * ITS + 4)
                        sp.dma_start(S.gm_dram[bass.ds(b * 3 + part, 1)].rearrange("a p i n -> p (a i n)"),
                                     gt[:, part].rearrange("p i n -> p (i n)")).then_inc(s_st[part], 16)
                for part in range(3):
                    sp.wait_ge(s_st[part], 16 * (BLOCKS // 3 + 1))


def peer_experts(nc, S):
    GS = 2
    NG = NKEY // GS
    HALF = NTOK // 2
    PASSES = [(0, 0), (0, 1), (1, 0)]
    with ExitStack() as ctx:
        hs = sb(nc, ctx, "pe_h_parts", [P, 2, KD, NTOK], F32R)
        free = S.mix[:].rearrange("p t d -> p (t d)")
        u = free[:, 0:2 * GS * D].rearrange("p (g s d) -> p g s d", g=2, s=GS)
        w = free[:, 2 * GS * D:2 * GS * D + NTOK]
        v = sb(nc, ctx, "pe_v", [P, 2, GS, D])
        g = sb(nc, ctx, "pe_g", [P, 2, BLOCKS, GS, NBLK])
        uT = sb(nc, ctx, "pe_uT_parts", [P, 2, 2, KD, P], F32R)
        vs = sb(nc, ctx, "pe_v_parts", [P, 2, 2, GS, D], F32R)
        act_ = sb(nc, ctx, "pe_act", [P, 2, NTOK])
        ws = sb(nc, ctx, "pe_w_parts", [P, 2, 2, GS, NTOK], F32R)
        s_u = [nc.alloc_semaphore(f"pe_u_and_gates{i}_loaded") for i in range(2)]
        s_v = [nc.alloc_semaphore(f"pe_v{i}_loaded") for i in range(2)]
        s_hh = nc.alloc_semaphore("pe_h_high_ready")
        s_hl = nc.alloc_semaphore("pe_h_low_ready")
        s_tr = nc.alloc_semaphore("pe_half_turned")
        s_uh = nc.alloc_semaphore("pe_uT_high_ready")
        s_ul = nc.alloc_semaphore("pe_uT_low_ready")
        s_vh = nc.alloc_semaphore("pe_v_high_ready")
        s_vl = nc.alloc_semaphore("pe_v_low_ready")
        s_h = nc.alloc_semaphore("pe_products_summed")
        s_ge = nc.alloc_semaphore("pe_gelu_ready")
        s_wg = nc.alloc_semaphore("pe_gates_applied")
        s_w = nc.alloc_semaphore("pe_weights_ready")
        s_y = nc.alloc_semaphore("pe_output_summed")
        s_ya = nc.alloc_semaphore("pe_output_added")
        s_out = nc.alloc_semaphore("y_stored")
        units = [(t, c) for t in range(NT) for c in range(2)]
        NU = len(units)
        share = [range(0, NU // 2), range(NU // 2, NU)]
        out_bank = lambda i, par: 4 + (i + par * NU) % 4
        u_v = S.peer_u.rearrange("(p s) d -> p s d", p=P)
        v_v = S.peer_v.rearrange("(p s) d -> p s d", p=P)

        with nc.Block() as block:
            @block.sync
            def _(sp):
                def load(gr, par):
                    sp.dma_start(u[:, par], u_v[:, bass.ds(gr * GS, GS), :]).then_inc(s_u[par], 16)
                    sp.dma_start(g[:, par].rearrange("p b s n -> p b (s n)"),
                                 S.gm_dram[:, :, bass.ds(gr * GS, GS), :].rearrange("b p s n -> p b (s n)")).then_inc(s_u[par], 16)
                    sp.dma_start(v[:, par], v_v[:, bass.ds(gr * GS, GS), :]).then_inc(s_v[par], 16)

                def refill(gr, par):
                    sp.wait_ge(s_tr, (gr - 1) * 2 * GS)
                    sp.wait_ge(s_wg, (gr - 1) * GS)
                    sp.wait_ge(s_vl, (gr - 1) * GS)
                    load(gr, par)

                load(0, 0)
                load(1, 1)
                with sp.Fori(0, NG // 2 - 1) as it:
                    refill(it * 2 + 2, 0)
                    refill(it * 2 + 3, 1)
                sp.wait_ge(s_ya, NG * NU + 4)
                sp.dma_start(S.y_prompt[0].rearrange("(t p) d -> p t d", p=P), S.x1[:, 0:NT - 1, :]).then_inc(s_out, 16)
                sp.dma_start(S.y_sample.rearrange("b t d -> (b t) d"), S.x1[0:64, NT - 1, :]).then_inc(s_out, 16)
                sp.wait_ge(s_out, 32)

            @block.tensor
            def _(pe):
                def turn(n, par, s):
                    pe.wait_ge(s_ul, n * 2 + 1)
                    for k in range(KD):
                        tr = pe.transpose(S.ps[:, k // 4, (k % 4) * P:(k % 4 + 1) * P], u[:, par, s, k * P:(k + 1) * P], S.ident[:])
                        if k % 4 == 3:
                            tr.then_inc(s_tr, 1)

                def products(n, s):
                    pe.wait_ge(s_ul, n * 2 + 3)
                    pe.wait_ge(s_ge, n + 1)
                    for half in range(2):
                        out = S.ps[:, 2 + half, 0:HALF]
                        for k in range(KD):
                            for a, b in PASSES:
                                mm = pe.matmul(out, uT[:, s, a, k, :], hs[:, b, k, half * HALF:(half + 1) * HALF],
                                               start=(k == 0 and a == b), stop=(k == KD - 1 and a == 1))
                    mm.then_inc(s_h, 1)

                def output(gr, par, picks):
                    for i in picks:
                        t, c = units[i]
                        m = ROWS[t]
                        pe.wait_ge(s_ya, gr * NU + i + 1)
                        for s in range(GS):
                            for a, b in PASSES:
                                mm = pe.matmul(S.ps[0:m, out_bank(i, par), :], ws[:, par, a, s, t * P:t * P + m],
                                               vs[:, par, b, s, c * 512:(c + 1) * 512],
                                               start=(s == 0 and a == b), stop=(s == GS - 1 and a == 1))
                        mm.then_inc(s_y, 1)

                def group(gr, par, fills, prev, last=False):
                    for s in range(GS):
                        n = gr * GS + s
                        if s < GS - 1:
                            turn(n + 1, par, s + 1)
                        elif not last:
                            pe.wait_ge(s_u[1 - par], fills * 32)
                            turn(n + 1, 1 - par, 0)
                        products(n, s)
                        if prev is not None:
                            if s == 0:
                                pe.wait_ge(s_w, gr * GS)
                                pe.wait_ge(s_vl, gr * GS)
                            output(prev, 1 - par, share[s])

                pe.wait_ge(s_hl, 1)
                pe.wait_ge(s_u[0], 32)
                turn(0, 0, 0)
                group(0, 0, 1, None)
                with pe.Fori(0, NG // 2 - 1) as it:
                    group(it * 2 + 1, 1, it + 2, it * 2)
                    group(it * 2 + 2, 0, it + 2, it * 2 + 1)
                group(NG - 1, 1, 0, NG - 2, last=True)
                pe.wait_ge(s_w, NG * GS)
                pe.wait_ge(s_vl, NG * GS)
                output(NG - 1, 1, range(NU))

            @block.scalar
            def _(act):
                def high(n, slot):
                    for half in range(2):
                        act.wait_ge(s_tr, n * 2 + half + 1)
                        act.activation(uT[:, slot, 0, half * 4:half * 4 + 4, :].rearrange("p k n -> p (k n)"),
                                       S.ps[:, half, :], ACT.Copy).then_inc(s_uh, 1)

                def group(gr, par, fills, free, last=False):
                    for s in range(GS):
                        n = gr * GS + s
                        if not (last and s == GS - 1):
                            high(n + 1, 1 - s)
                        act.wait_ge(s_h, n + 1)
                        if free:
                            act.wait_ge(s_wg, n - 1)
                        act.activation(act_[:, s, :].rearrange("p (h n) -> p h n", h=2),
                                       S.ps[:, 2:4, 0:HALF], ACT.Gelu).then_inc(s_ge, 1)
                        if s == 0:
                            act.wait_ge(s_v[par], fills * 16)
                            if free:
                                act.wait_ge(s_ya, (gr - 1) * NU + 4)
                        act.activation(vs[:, par, 0, s, :], v[:, par, s, :], ACT.Copy).then_inc(s_vh, 1)

                act.sem_inc(s_ge, 1)
                act.activation(hs[:, 0], S.h2T[:, :, 0:NTOK], ACT.Copy).then_inc(s_hh, 1)
                high(0, 0)
                group(0, 0, 1, False)
                with act.Fori(0, NG // 2 - 1) as it:
                    group(it * 2 + 1, 1, it + 1, True)
                    group(it * 2 + 2, 0, it + 2, True)
                group(NG - 1, 1, NG // 2, True, last=True)

            @block.gpsimd
            def _(pool):
                def group(gr, par):
                    for s in range(GS):
                        pool.wait_ge(s_vh, gr * GS + s + 1)
                        pool.tensor_tensor(vs[:, par, 1, s, :], v[:, par, s, :], vs[:, par, 0, s, :].bitcast(F32), ALU.subtract).then_inc(s_vl, 1)

                with pool.Fori(0, NG // 2) as it:
                    group(it * 2, 0)
                    group(it * 2 + 1, 1)

            @block.vector
            def _(dve):
                def low(n, slot):
                    for half in range(2):
                        dve.wait_ge(s_uh, n * 2 + half + 1)
                        dve.tensor_tensor(uT[:, slot, 1, half * 4:half * 4 + 4, :].rearrange("p k n -> p (k n)"), S.ps[:, half, :],
                                          uT[:, slot, 0, half * 4:half * 4 + 4, :].rearrange("p k n -> p (k n)").bitcast(F32),
                                          ALU.subtract).then_inc(s_ul, 1)

                def add(gr, par, picks):
                    for i in picks:
                        t, c = units[i]
                        m = ROWS[t]
                        dve.wait_ge(s_y, gr * NU + i + 1)
                        x = S.x1[0:m, t, c * 512:(c + 1) * 512]
                        dve.tensor_tensor(x, S.ps[0:m, out_bank(i, par), :], x, ALU.add).then_inc(s_ya, 1)

                def group(gr, par, fills, prev, last=False):
                    for s in range(GS):
                        n = gr * GS + s
                        if not (last and s == GS - 1):
                            low(n + 1, 1 - s)
                        if s == 0:
                            dve.wait_ge(s_u[par], fills * 32)
                        dve.wait_ge(s_ge, n + 2)
                        dve.tensor_tensor(w.rearrange("p (b n) -> p b n", b=BLOCKS),
                                          act_[:, s, :].rearrange("p (b n) -> p b n", b=BLOCKS),
                                          g[:, par, :, s, :], ALU.mult)
                        dve.drain().then_inc(s_wg, 1)
                        dve.tensor_copy(ws[:, par, 0, s, :], w)
                        dve.drain()
                        dve.tensor_tensor(ws[:, par, 1, s, :], w, ws[:, par, 0, s, :].bitcast(F32), ALU.subtract)
                        dve.drain().then_inc(s_w, 1)
                        if prev is not None:
                            add(prev, 1 - par, share[s])

                dve.sem_inc(s_ul, 1)
                dve.sem_inc(s_ya, 4)
                dve.wait_ge(s_hh, 1)
                dve.tensor_tensor(hs[:, 1], S.h2T[:, :, 0:NTOK], hs[:, 0].bitcast(F32), ALU.subtract).then_inc(s_hl, 1)
                low(0, 0)
                group(0, 0, 1, None)
                with dve.Fori(0, NG // 2 - 1) as it:
                    group(it * 2 + 1, 1, it + 1, it * 2)
                    group(it * 2 + 2, 0, it + 2, it * 2 + 1)
                group(NG - 1, 1, NG // 2, NG - 2, last=True)
                add(NG - 1, 1, range(NU))


def constants():
    d = DMAX - np.arange(LVEC)
    n = np.maximum(d, 0)
    exact = NB // 2
    nf = np.maximum(n, exact).astype(np.float32)
    large = exact + (np.log(nf / np.float32(exact)) / np.float32(np.log(MAXD / exact)) * np.float32(NB - exact)).astype(np.int32)
    bucket = np.where(n < exact, n, np.minimum(large, NB - 1))
    oh = np.zeros((NB + 1, LVEC), np.float32)
    oh[bucket, np.arange(LVEC)] = 1.0
    oh[:NB, d < 0] = 0.0
    oh[NB, d < 0] = 1.0
    tok = np.arange(P)
    rows = (tok // 32) * 8 + tok % 8
    misc = np.zeros((P, 40), np.float32)
    misc[:, 0] = tok >= 2 * STRIDE - 1
    misc[:, 1:9] = np.where(np.arange(8)[None] <= (tok % 8)[:, None], NEG, 0.0)
    misc[:, 16:33] = np.arange(17)
    at = np.arange(TOK)
    reset = np.where(at < SEQ, at % P, at % DEC_T) > 0
    causal = tok[:, None] <= tok[None]
    gmask = np.stack([causal, causal & (tok[:, None] // DEC_T == tok[None] // DEC_T)])
    seqof = tok[:, None] // DEC_T == np.arange(DEC_B)[None]
    flips = np.stack([np.eye(P)[::-1], np.kron(np.eye(P // 8), np.eye(8)[::-1])]).astype(np.float32)
    return {"c_reset": reset.astype(np.float32), "c_gmask": gmask.astype(np.float32),
            "c_seqof": seqof.astype(np.float32), "c_flips": flips, "c_ident": np.eye(P, dtype=np.float32), "c_bucket": oh,
            "c_sub": (tok[:, None] // STRIDE == np.arange(NSUB)[None]).astype(np.float32),
            "c_group": (rows[:, None] == rows[None]).astype(np.float32), "c_misc": misc,
            "c_iota": np.tile(np.arange(NKEY, dtype=np.float32), (P, 1))}


INPUTS = ["x_prompt", "x_sample", "cache_kv", "cache_win", "state_gla", "page_table", "norm1_g", "w_in", "qn_g",
          "kn_cmp_g", "kn_slc_g", "kn_win_g", "cmp_w_pos", "cmp_proj", "rel_bias", "nsa_gate_b", "nsa_out_g",
          "gla_a_up", "gla_a_b", "gla_out_g", "w_out", "norm2_g", "peer_wq", "peer_qn_g", "peer_k1", "peer_k2",
          "peer_u", "peer_v"]
CONSTANTS = ["c_reset", "c_gmask", "c_seqof", "c_flips", "c_ident", "c_bucket", "c_sub", "c_group", "c_misc", "c_iota"]
OUTPUTS = [("y_prompt", (1, SEQ, D)), ("y_sample", (DEC_B, DEC_T, D)), ("kv_prompt", (1, SEQ, 4, G, DK)),
           ("kv_sample", (DEC_B, DEC_T, 4, G, DK)), ("win_prompt", (1, WIN, 2, G, DK)),
           ("win_sample", (DEC_B, WIN, 2, G, DK)), ("gla_prompt", (1, HG, DKG, DVG)),
           ("gla_sample", (DEC_B, HG, DKG, DVG))]
SCRATCH = [("rv", (H, LVEC)), ("gate", (DEC_B * DEC_T, 3 * H)), ("gm", (BLOCKS, P, NKEY, NBLK)), ("osa", (DEC_B, DEC_T, H, DK))]


def program(nc, S):
    with ExitStack() as ctx:
        S.ident = sb(nc, ctx, "ident", [P, P])
        S.ones = sb(nc, ctx, "ones", [P, 1])
        S.gains = sb(nc, ctx, "gains", [P, 4, DK])
        S.gates = sb(nc, ctx, "gates", [P, NT, 3 * H])
        S.ps = ctx.enter_context(nc.psum_tensor("ps", [P, 8, 512], F32))
        S.ps2 = S.ps[:].rearrange("p (a b) n -> p a (b n)", b=2)
        S.iota = sb(nc, ctx, "iota", [P, NKEY])
        S.mix = sb(nc, ctx, "mix", [P, NT, D])
        S.onsa, S.ogla = S.mix[:, :, 0:H * DK], S.mix[:, :, H * DK:D]
        S.x = S.mix
        with ExitStack() as c0:
            token_mixers(nc, S, c0)
        S.x1 = sb(nc, ctx, "x1", [P, NT, D])
        mix_out(nc, S)
        S.h2T = sb(nc, ctx, "h2T", [P, KD, TOK])
        norm_transposed(nc, S, "norm2", S.x1, S.mix, S.norm2_g, S.h2T)
        with ExitStack() as c0:
            S.selT = sb(nc, c0, "selT", [P, 3, NTOK])
            with ExitStack() as c1:
                S.best = sb(nc, c1, "best", [P, NT, PH, TOPK])
                S.sel = sb(nc, c1, "sel", [P, 2, NT, PH, TOPK])
                S.gate16 = sb(nc, c1, "gate16", [P, NT * PH, TOPK])
                peer_select(nc, S)
                peer_gates(nc, S)
            peer_gate_matrix(nc, S)
        peer_experts(nc, S)


def token_mixers(nc, S, ctx):
    S.pj = sb(nc, ctx, "pj", [P, NT, D_IN])
    load_start(nc, S)
    project_in(nc, S)
    with ExitStack() as c2:
        S.qT = sb(nc, c2, "qT", [P, 4, TOK])
        S.ksT = sb(nc, c2, "ksT", [P, TOK])
        S.kwT = sb(nc, c2, "kwT", [P, TOK])
        S.cproj = sb(nc, c2, "cproj", [P, 2, DK])
        S.grp = sb(nc, c2, "grp", [P, P])
        S.misc = sb(nc, c2, "misc", [P, 40])
        S.w16 = sb(nc, c2, "w16", [P, 4, 2, NSUB])
        S.sbias = sb(nc, c2, "sbias", [P, PAST + DEC_T])
        S.grow = sb(nc, c2, "grow", [P, 4, 3])
        with ExitStack() as c3:
            S.toep = sb(nc, c3, "toep", [P, H, 512])
            S.vc = sb(nc, c3, "vc", [32, P])
            S.kcT = sb(nc, c3, "kcT", [P, 32])
            with ExitStack() as c4:
                S.qp = sb(nc, c4, "qp", [P, NT, H * DK])
                head_norms(nc, S)
                attention_setup(nc, S)
            prompt_compress(nc, S)
            prompt_attention(nc, S)
        sample_attention(nc, S)
    with ExitStack() as c2:
        S.gq = sb(nc, c2, "gq", [P, 2, TOK])
        S.gk = sb(nc, c2, "gk", [P, 2, TOK])
        S.gb = sb(nc, c2, "gb", [P, 2, TOK])
        S.gs = sb(nc, c2, "gs", [P, 2, DEC_B, DVG])
        S.gmask = sb(nc, c2, "gmask", [P, 2, P])
        S.seqof = sb(nc, c2, "seqof", [P, DEC_B])
        gla_inputs(nc, S)
        gla_chunks(nc, S)
    gla_finish(nc, S)


def kernel(**inputs):
    import numpy as _np
    import concourse.bacc as _bacc
    from concourse.bass_utils import run_bass_kernel_spmd as _run

    nc = _bacc.Bacc("TRN2", target_bir_lowering=False, num_devices=1)
    arrays = {name: _np.ascontiguousarray(inputs[name]) for name in INPUTS}
    arrays.update(constants())
    dram = {name: nc.dram_tensor("in_" + name, a.shape, mybir.dt.from_np(a.dtype), kind="ExternalInput").ap()
            for name, a in arrays.items()}
    S = Shared()
    (S.x_prompt, S.x_sample, S.cache_kv, S.cache_win, S.state_gla, S.page_table, S.norm1_g, S.w_in, S.qn_g,
     S.kn_cmp_g, S.kn_slc_g, S.kn_win_g, S.cmp_w_pos, S.cmp_proj, S.rel_bias, S.nsa_gate_b, S.nsa_out_g,
     S.gla_a_up, S.gla_a_b, S.gla_out_g, S.w_out, S.norm2_g, S.peer_wq, S.peer_qn_g, S.peer_k1, S.peer_k2,
     S.peer_u, S.peer_v) = (dram[n] for n in INPUTS)
    (S.c_reset, S.c_gmask, S.c_seqof, S.c_flips, S.c_ident, S.c_bucket, S.c_sub, S.c_group, S.c_misc, S.c_iota) = (dram[n] for n in CONSTANTS)
    (S.y_prompt, S.y_sample, S.kv_prompt, S.kv_sample, S.win_prompt, S.win_sample, S.gla_prompt, S.gla_sample) = (nc.dram_tensor("out_" + n, shape, F32, kind="ExternalOutput").ap() for n, shape in OUTPUTS)
    (S.rv_t, S.gate_t, S.gm_t, S.osa_t) = (nc.dram_tensor(n, shape, F32, kind="Internal") for n, shape in SCRATCH)
    S.rv_dram = S.rv_t.ap()
    S.gate_dram = S.gate_t.ap()
    S.gm_dram = S.gm_t.ap()
    S.osa_dram = S.osa_t.ap()
    program(nc, S)
    r = _run(nc, [{"in_" + name: a for name, a in arrays.items()}], core_ids=[0])
    return tuple(r.results[0]["out_" + name] for name, _ in OUTPUTS)
```

```python
from contextlib import ExitStack

import numpy as np

import concourse.bass as bass
from concourse import mybir

ALU = mybir.AluOpType
ACT = mybir.ActivationFunctionType
F32 = mybir.dt.float32
F32R = mybir.dt.float32r
I32 = mybir.dt.int32
U32 = mybir.dt.uint32
X = mybir.AxisListType.X

P = 128
D = 1024
KD = D // P
SEQ = 512
DEC_B, DEC_T = 8, 8
NT = SEQ // P + 1
TOK = NT * P
NTOK = SEQ + DEC_B * DEC_T
PAST, PAGE = 1024, 128
NPAGE = PAST // PAGE
H, DK, G, HPG = 8, 64, 2, 4
STRIDE = 16
NSUB = PAGE // STRIDE
WIN = 512
HG, DKG, DVG, RANK = 4, 64, 128, 16
TAU = 16.0
NB, MAXD = 32, 128
PH, NKEY, PQ, TOPK = 8, 128, 256, 16
EPS = 1e-6
NEG = -1e30
SCALE = DK ** -0.5
SIZES = dict(q=H * DK, kc=G * DK, vc=G * DK, ks=G * DK, vs=G * DK, kw=G * DK, vw=G * DK, gate=3 * H,
             qg=HG * DKG, kg=HG * DKG, vg=HG * DVG, al=RANK, rg=HG * DVG)
D_IN = sum(SIZES.values())
COL = {}
for _n, _s in SIZES.items():
    COL[_n] = sum(SIZES[m] for m in list(SIZES)[:list(SIZES).index(_n)])
PCH = 6
PCW = D_IN // PCH
DMAX = PAST + DEC_T - 1
LVEC = DMAX + P + 1


class Shared:
    pass


def part(S, name, lo=0, hi=NT):
    return S.pj[:, lo:hi, COL[name]:COL[name] + SIZES[name]]


def over(ap, shape):
    return ap.to_broadcast(shape)


def sb(nc, ctx, name, shape, dt=F32):
    return ctx.enter_context(nc.sbuf_tensor(name, shape, dt))


def load_start(nc, S):
    s_in = nc.alloc_semaphore("start_loaded")
    s_zero = nc.alloc_semaphore("sample_padding_zeroed")
    rows = [S.qn_g, S.kn_slc_g, S.kn_win_g, S.kn_cmp_g]
    with nc.Block() as block:
        @block.sync
        def _(sp):
            for i, src in enumerate(rows):
                sp.dma_start(S.gains[:, i, :], src.partition_broadcast(P)).then_inc(s_in, 16)
            sp.dma_start(S.ident[:], S.c_ident[:, :]).then_inc(s_in, 16)
            sp.dma_start(S.x[:, 0:4, :], S.x_prompt[0].rearrange("(t p) d -> p t d", p=P)).then_inc(s_in, 16)
            sp.wait_ge(s_zero, 1)
            sp.dma_start(S.x[0:64, 4, :], S.x_sample.rearrange("b t d -> (b t) d")).then_inc(s_in, 16)
            sp.wait_ge(s_in, 16 * (len(rows) + 3))

        @block.vector
        def _(dve):
            dve.memset(S.x[:, 4, :], 0.0).then_inc(s_zero, 1)
            dve.memset(S.ones[:], 1.0)


def norm_transposed(nc, S, tag, x, xn, gain, out_T):
    with ExitStack() as ctx:
        stat = sb(nc, ctx, f"{tag}_stat", [P, 2, NT])
        gcol = sb(nc, ctx, f"{tag}_gcol", [P, KD])
        s_g = nc.alloc_semaphore(f"{tag}_gain_loaded")
        s_sum = nc.alloc_semaphore(f"{tag}_squares_summed")
        s_ms = nc.alloc_semaphore(f"{tag}_mean_ready")
        s_rs = nc.alloc_semaphore(f"{tag}_rstd_ready")
        s_xn = nc.alloc_semaphore(f"{tag}_tile_scaled")
        s_tr = nc.alloc_semaphore(f"{tag}_chunk_transposed")
        s_ev = nc.alloc_semaphore(f"{tag}_chunk_moved")
        with nc.Block() as block:
            @block.sync
            def _(sp):
                with nc.allow_non_contiguous_dma(reason="1024 gains, one per partition and chunk"):
                    sp.dma_start(gcol[:], gain.rearrange("(k p) -> p k", p=P)).then_inc(s_g, 16)

            @block.scalar
            def _(act):
                for t in range(NT):
                    act.activation(out_T[:].rearrange("p k n -> p (k n)")[:, 0:D], x[:, t, :], ACT.Square, accum_out=stat[:, 0, t:t + 1])
                    act.drain()
                act.drain().then_inc(s_sum, 1)
                act.wait_ge(s_ms, 1)
                act.activation(stat[:, 0, :], stat[:, 1, :], ACT.Sqrt).then_inc(s_rs, 1)
                act.wait_ge(s_g, 16)
                for k in range(KD):
                    act.wait_ge(s_tr, k + 1)
                    act.activation(out_T[:, k, :], S.ps2[:, k % 4, 0:TOK], ACT.Copy,
                                   scale=gcol[:, k:k + 1]).then_inc(s_ev, 1)

            @block.vector
            def _(dve):
                dve.wait_ge(s_sum, 1)
                dve.tensor_scalar(stat[:, 1, :], stat[:, 0, :], 1.0 / D, EPS, ALU.mult, ALU.add)
                dve.drain()
                dve.reciprocal(stat[:, 1, :], stat[:, 1, :]).then_inc(s_ms, 1)
                dve.wait_ge(s_rs, 1)
                for t in range(NT):
                    dve.tensor_scalar(xn[:, t, :], x[:, t, :], stat[:, 0, t:t + 1], None, ALU.mult).then_inc(s_xn, 1)

            @block.tensor
            def _(pe):
                pe.wait_ge(s_xn, NT)
                for k in range(KD):
                    if k >= 4:
                        pe.wait_ge(s_ev, k - 3)
                    for t in range(NT):
                        last = pe.transpose(S.ps2[:, k % 4, t * P:(t + 1) * P], xn[:, t, k * P:(k + 1) * P], S.ident[:])
                    last.then_inc(s_tr, 1)


def project_in(nc, S):
    with ExitStack() as ctx:
        w = sb(nc, ctx, "w_in_sb", [P, KD, D_IN])
        hT = sb(nc, ctx, "hT", [P, KD, TOK])
        s_w0 = nc.alloc_semaphore("w_in_first_columns_loaded")
        s_w = nc.alloc_semaphore("w_in_other_columns_loaded")
        with nc.Block() as block:
            @block.sync
            def _(sp):
                rows = S.w_in.rearrange("(k p) n -> p k n", p=P)
                sp.dma_start(w[:, :, 0:PCW], rows[:, :, 0:PCW]).then_inc(s_w0, 16)
                for c in range(1, PCH):
                    sp.dma_start(w[:, :, c * PCW:(c + 1) * PCW], rows[:, :, c * PCW:(c + 1) * PCW]).then_inc(s_w, 16)
        norm_transposed(nc, S, "norm1", S.x, S.x, S.norm1_g, hT)
        s_mm = nc.alloc_semaphore("proj_bank_ready")
        s_free = nc.alloc_semaphore("proj_bank_free")
        with nc.Block() as block:
            @block.tensor
            def _(pe):
                def columns(c):
                    for t in range(NT):
                        pe.wait_ge(s_free, c * NT + t + 1)
                        for k in range(KD):
                            mm = pe.matmul(S.ps[:, t, 0:PCW], hT[:, k, t * P:(t + 1) * P],
                                           w[:, k, bass.ds(c * PCW, PCW)], start=(k == 0), stop=(k == KD - 1))
                        mm.then_inc(s_mm, 1)

                pe.wait_ge(s_w0, 16)
                columns(0)
                pe.wait_ge(s_w, 16 * (PCH - 1))
                with pe.Fori(1, PCH) as c:
                    columns(c)

            @block.vector
            def _(dve):
                dve.sem_inc(s_free, NT)
                with dve.Fori(0, PCH) as c:
                    for t in range(NT):
                        dve.wait_ge(s_mm, c * NT + t + 1)
                        dve.tensor_copy(S.pj[:, t, bass.ds(c * PCW, PCW)], S.ps[:, t, 0:PCW]).then_inc(s_free, 1)


def head_norms(nc, S):
    with ExitStack() as ctx:
        sq = sb(nc, ctx, "qk_sq", [P, NT, 12, DK])
        ms = sb(nc, ctx, "qk_ms", [P, NT, 12])
        rs = sb(nc, ctx, "qk_rs", [P, NT, 12])
        gb = sb(nc, ctx, "gate_b", [P, 3 * H])
        s_gb = nc.alloc_semaphore("gate_bias_loaded")
        s_inv = nc.alloc_semaphore("qk_inverse_ready")
        s_rs = nc.alloc_semaphore("qk_rstd_ready")
        s_zg = nc.alloc_semaphore("gate_logits_ready")
        s_out = S.s_out = nc.alloc_semaphore("outputs_written")
        S.n_out = 4 + DEC_B
        s_fin = nc.alloc_semaphore("qk_normed")
        q, ks, kw = part(S, "q"), part(S, "ks"), part(S, "kw")
        with nc.Block() as block:
            @block.sync
            def _(sp):
                sp.dma_start(gb[:], S.nsa_gate_b.partition_broadcast(P)).then_inc(s_gb, 16)
                setup_loads(nc, S, sp)
                sp.wait_ge(s_fin, 1)
                kv = lambda lo, hi: S.pj[:, lo:hi, COL["kc"]:COL["kc"] + 512]
                wv = lambda lo, hi: S.pj[:, lo:hi, COL["kw"]:COL["kw"] + 256]
                sp.dma_start(S.kv_prompt[0].rearrange("(t p) a g d -> p t (a g d)", p=P), kv(0, 4)).then_inc(s_out, 16)
                sp.dma_start(S.kv_sample.rearrange("b t a g d -> (b t) (a g d)"), kv(4, 5)[0:64, 0, :]).then_inc(s_out, 16)
                sp.dma_start(S.win_prompt[0].rearrange("(t p) a g d -> p t (a g d)", p=P), wv(0, 4)).then_inc(s_out, 16)
                sp.dma_start(S.win_sample[:, 0:WIN - DEC_T].rearrange("b t a g d -> b (t a g d)"),
                             S.cache_win[:, DEC_T:WIN].rearrange("b t a g d -> b (t a g d)")).then_inc(s_out, 16)
                for b in range(DEC_B):
                    sp.dma_start(S.win_sample[b, WIN - DEC_T:WIN].rearrange("t a g d -> t (a g d)"),
                                 wv(4, 5)[b * DEC_T:(b + 1) * DEC_T, 0, :]).then_inc(s_out, 16)

            @block.vector
            def _(dve):
                for lo, hi, src in ((0, 8, q), (8, 10, ks), (10, 12, kw)):
                    v = src.rearrange("p t (h d) -> p t h d", d=DK)
                    dve.tensor_tensor(sq[:, :, lo:hi, :], v, v, ALU.mult)
                dve.drain()
                dve.tensor_reduce(ms[:], sq[:], X, ALU.add)
                dve.drain()
                dve.tensor_scalar(ms[:], ms[:], 1.0 / DK, EPS, ALU.mult, ALU.add)
                dve.drain()
                dve.reciprocal(ms[:], ms[:]).then_inc(s_inv, 1)
                dve.wait_ge(s_gb, 16)
                dve.tensor_tensor(S.gates[:], part(S, "gate"),
                                  gb[:].unsqueeze(1).to_broadcast([P, NT, 3 * H]), ALU.add).then_inc(s_zg, 1)
                dve.wait_ge(s_rs, 1)
                for lo, hi, src in ((0, 8, q), (8, 10, ks), (10, 12, kw)):
                    v = src.rearrange("p t (h d) -> p t h d", d=DK)
                    dve.tensor_tensor(sq[:, :, lo:hi, :], v,
                                      rs[:, :, lo:hi].unsqueeze(3).to_broadcast([P, NT, hi - lo, DK]), ALU.mult)
                dve.drain()
                qp = S.qp[:].rearrange("p t (j g d) -> p t j g d", g=G, d=DK)
                for g in range(G):
                    dve.tensor_tensor(qp[:, :, :, g, :], sq[:, :, g * HPG:(g + 1) * HPG, :],
                                      S.gains[:, 0:1, :].unsqueeze(1).to_broadcast([P, NT, HPG, DK]), ALU.mult)
                for i, lo, dst in ((1, 8, ks), (2, 10, kw)):
                    dve.tensor_tensor(dst.rearrange("p t (h d) -> p t h d", d=DK), sq[:, :, lo:lo + 2, :],
                                      S.gains[:, i:i + 1, :].unsqueeze(1).to_broadcast([P, NT, 2, DK]), ALU.mult)
                dve.drain().then_inc(s_fin, 1)

            @block.scalar
            def _(act):
                act.wait_ge(s_inv, 1)
                act.activation(rs[:], ms[:], ACT.Sqrt).then_inc(s_rs, 1)
                act.wait_ge(s_zg, 1)
                act.activation(S.gate_hj[:].rearrange("p (h j) -> p j h", j=3),
                               S.gates[:, NT - 1, :].rearrange("p (j h) -> p j h", j=3), ACT.Sigmoid)
                act.drain()
                act.activation(S.gates[:], S.gates[:], ACT.Sigmoid)




def setup_buffers(nc, S, ctx):
    S.relb = sb(nc, ctx, "relb", [NB + 1, H])
    S.onehot = sb(nc, ctx, "bucket_onehot", [NB + 1, LVEC])
    S.wpos = sb(nc, ctx, "wpos", [P, 4, 2])
    S.msub = sb(nc, ctx, "msub", [P, NSUB])
    S.flips = sb(nc, ctx, "flips", [P, 2, P])
    S.s_bias_in = nc.alloc_semaphore("bias_inputs_loaded")


def setup_loads(nc, S, sp):
    sp.dma_start(S.relb[0:NB, :], S.rel_bias[:, :]).then_inc(S.s_bias_in, 16)
    sp.dma_start(S.onehot[:], S.c_bucket[:, :]).then_inc(S.s_bias_in, 16)
    sp.dma_start(S.msub[:], S.c_sub[:, :]).then_inc(S.s_bias_in, 16)
    sp.dma_start(S.cproj[:, :, :], S.cmp_proj.rearrange("k g d e -> (g d) k e")).then_inc(S.s_bias_in, 16)
    sp.dma_start(S.grp[:], S.c_group[:, :]).then_inc(S.s_bias_in, 16)
    sp.dma_start(S.misc[:], S.c_misc[:, :]).then_inc(S.s_bias_in, 16)
    sp.dma_start(S.flips[:], S.c_flips.rearrange("a p n -> p a n")).then_inc(S.s_bias_in, 16)
    with nc.allow_non_contiguous_dma(reason="position weights, one per partition"):
        for r in range(NSUB):
            sp.dma_start(S.wpos[r * STRIDE:(r + 1) * STRIDE, :, :],
                         S.cmp_w_pos.rearrange("k g (h j) -> j (k g) h", j=STRIDE)).then_inc(S.s_bias_in, 16)


def attention_setup(nc, S):
    with ExitStack() as ctx:
        vec = sb(nc, ctx, "bias_vec", [H, LVEC])
        flipped = sb(nc, ctx, "toep_flipped", [P, H, 512])
        sflip = sb(nc, ctx, "sbias_flipped", [P, PAST + DEC_T])
        relb, onehot, wpos, msub, flips, s_c = S.relb, S.onehot, S.wpos, S.msub, S.flips, S.s_bias_in
        s_neg = nc.alloc_semaphore("mask_row_set")
        s_mm = nc.alloc_semaphore("bias_vec_summed")
        s_vec = nc.alloc_semaphore("bias_vec_ready")
        s_rv = nc.alloc_semaphore("bias_vec_stored")
        s_t = nc.alloc_semaphore("bias_tiles_loaded")
        s_tr = nc.alloc_semaphore("qk_block_transposed")
        s_ea = nc.alloc_semaphore("qk_even_block_moved")
        s_ed = nc.alloc_semaphore("qk_odd_block_moved")
        s_gl = nc.alloc_semaphore("sample_gates_loaded")
        s_gs = nc.alloc_semaphore("sample_gates_stored")
        s_fl = nc.alloc_semaphore("bias_rows_flipped")
        s_fe = nc.alloc_semaphore("bias_rows_moved")
        scuts = [(a, min(a + 512, PAST + DEC_T)) for a in range(0, PAST + DEC_T, 512)]
        NFLIP = H + len(scuts)
        cuts = [(a, min(a + 512, LVEC)) for a in range(0, LVEC, 512)]
        sources = [S.qp[:, :, j * P:(j + 1) * P] for j in range(4)] + [part(S, "ks"), part(S, "kw")]
        targets = [S.qT[:, j, :] for j in range(4)] + [S.ksT[:], S.kwT[:]]
        with nc.Block() as block:
            @block.sync
            def _(sp):
                sp.dma_start(S.gate_dram[:, :], S.gate_hj[0:64, :]).then_inc(s_gs, 16)
                sp.wait_ge(s_vec, 1)
                sp.dma_start(S.rv_dram[:, :], vec[:]).then_inc(s_rv, 16)
                sp.wait_ge(s_rv, 16)
                sp.dma_start(flipped[:], bass.AP(S.rv_t, DMAX - 384 - (P - 1), [[1, P], [LVEC, H], [1, 512]])).then_inc(s_t, 16)
                for bb in range(2):
                    for h in range(H):
                        lo = bb * 64 + h * DEC_T
                        sp.dma_start(sflip[lo:lo + DEC_T, :],
                                     bass.AP(S.rv_t, h * LVEC + DMAX - PAST - (DEC_T - 1),
                                             [[1, DEC_T], [1, PAST + DEC_T]])).then_inc(s_t, 16)
                sp.wait_ge(s_gs, 16)
                with nc.allow_non_contiguous_dma(reason="24 gates of each sample token to their rows"):
                    for bb in range(2):
                        for h in range(H):
                            lo = bb * 64 + h * DEC_T
                            sp.dma_start(S.grow[lo:lo + DEC_T, :, :],
                                         bass.AP(S.gate_t, bb * DEC_T * 24 + 3 * h,
                                                 [[24, DEC_T], [2 * DEC_T * 24, 4], [1, 3]])).then_inc(s_gl, 16)
                sp.wait_ge(s_gl, 16 * 2 * H)

            @block.vector
            def _(dve):
                dve.memset(relb[NB:NB + 1, :], NEG).then_inc(s_neg, 1)
                dve.wait_ge(s_mm, 1)
                for i, (a, b) in enumerate(cuts):
                    dve.tensor_copy(vec[:, a:b], S.ps[0:H, 5 + i, 0:b - a])
                dve.drain().then_inc(s_vec, 1)
                dve.tensor_tensor(S.w16[:].rearrange("p a b n -> p (a b) n"),
                                  wpos[:].rearrange("p a b -> p (a b)").unsqueeze(2).to_broadcast([P, 8, NSUB]),
                                  msub[:].unsqueeze(1).to_broadcast([P, 8, NSUB]), ALU.mult)
                for i in (1, 3, 5):
                    dve.wait_ge(s_tr, i + 1)
                    dve.tensor_copy(targets[i], S.ps2[:, i % 2, 0:TOK]).then_inc(s_ed, 1)
                for i in range(NFLIP):
                    dve.wait_ge(s_fl, i + 1)
                    dst = S.toep[:, i, :] if i < H else S.sbias[:, scuts[i - H][0]:scuts[i - H][1]]
                    dve.tensor_copy(dst, S.ps[:, i % 2, 0:dst.shape[-1]]).then_inc(s_fe, 1)

            @block.scalar
            def _(act):
                for i in (0, 2, 4):
                    act.wait_ge(s_tr, i + 1)
                    act.activation(targets[i], S.ps2[:, i % 2, 0:TOK], ACT.Copy).then_inc(s_ea, 1)

            @block.tensor
            def _(pe):
                pe.wait_ge(s_neg, 1)
                pe.wait_ge(s_c, 16 * (7 + NSUB))
                for i, (a, b) in enumerate(cuts):
                    mm = pe.matmul(S.ps[0:H, 5 + i, 0:b - a], relb[:], onehot[:, a:b], start=True, stop=True)
                mm.then_inc(s_mm, 1)
                for i, src in enumerate(sources):
                    if i >= 2:
                        pe.wait_ge(s_ed if i % 2 else s_ea, i // 2)
                    for t in range(NT):
                        tr = pe.transpose(S.ps2[:, i % 2, t * P:(t + 1) * P], src[:, t, :], S.ident[:])
                    tr.then_inc(s_tr, 1)
                pe.wait_ge(s_t, 16 * (1 + 2 * H))
                pe.wait_ge(s_ea, 3)
                pe.wait_ge(s_ed, 3)
                for i in range(NFLIP):
                    if i >= 2:
                        pe.wait_ge(s_fe, i - 1)
                    src = flipped[:, i, :] if i < H else sflip[:, scuts[i - H][0]:scuts[i - H][1]]
                    pe.matmul(S.ps[:, i % 2, 0:src.shape[-1]], flips[:, 0 if i < H else 1, :], src,
                              start=True, stop=True).then_inc(s_fl, 1)


def prompt_compress(nc, S):
    N, T = 31, 4
    with ExitStack() as ctx:
        halves = sb(nc, ctx, "pc_halves", [P, 2, 2, 32])
        blk = sb(nc, ctx, "pc_blk", [P, 2, N])
        sq = sb(nc, ctx, "pc_sq", [N, G, DK])
        st = sb(nc, ctx, "pc_st", [N, 2, G])
        kc = sb(nc, ctx, "pc_kc", [N, G, DK])
        s_pe = nc.alloc_semaphore("pc_product_ready")
        s_ve = nc.alloc_semaphore("pc_vector_ready")
        s_rt = nc.alloc_semaphore("pc_root_ready")
        cps = S.ps[:, 0, 0:128].rearrange("p (k h n) -> p k h n", k=2, h=2)
        kvc = S.ps[0:N, 1:1 + G, 0:2 * DK].rearrange("p g (k e) -> p g k e", k=2)
        with nc.Block() as block:
            @block.tensor
            def _(pe):
                for kv in range(2):
                    for g in range(G):
                        for t in range(T):
                            c = COL["kc"] + kv * P + g * DK
                            mm = pe.matmul(cps[g * DK:(g + 1) * DK, kv, :, t * NSUB:(t + 1) * NSUB],
                                           S.pj[:, t, c:c + DK], S.w16[:, kv * 2 + g], start=True, stop=True)
                mm.then_inc(s_pe, 1)
                pe.wait_ge(s_ve, 1)
                for kv in range(2):
                    for g in range(G):
                        mm = pe.matmul(kvc[:, g, kv, :], blk[g * DK:(g + 1) * DK, kv, :],
                                       S.cproj[g * DK:(g + 1) * DK, kv, :], start=True, stop=True)
                mm.then_inc(s_pe, 1)
                pe.wait_ge(s_ve, 3)
                pe.transpose(S.ps[:, 3, 0:N], kc[:].rearrange("p g e -> p (g e)"), S.ident[0:N, 0:N]).then_inc(s_pe, 1)

            @block.vector
            def _(dve):
                dve.wait_ge(s_pe, 1)
                dve.tensor_copy(halves[:], cps)
                dve.drain()
                dve.tensor_tensor(blk[:], halves[:, :, 0, 0:N], halves[:, :, 1, 1:N + 1], ALU.add).then_inc(s_ve, 1)
                dve.wait_ge(s_pe, 2)
                dve.tensor_copy(S.vc[0:N, :].rearrange("p (g e) -> p g e", g=G), kvc[:, :, 1])
                dve.tensor_copy(kc[:], kvc[:, :, 0])
                dve.drain()
                dve.tensor_tensor(sq[:], kc[:], kc[:], ALU.mult)
                dve.drain()
                dve.tensor_reduce(st[:, 0, :], sq[:], X, ALU.add)
                dve.drain()
                dve.tensor_scalar(st[:, 0, :], st[:, 0, :], 1.0 / DK, EPS, ALU.mult, ALU.add)
                dve.drain()
                dve.reciprocal(st[:, 0, :], st[:, 0, :]).then_inc(s_ve, 1)
                dve.wait_ge(s_rt, 1)
                dve.tensor_tensor(kc[:], kc[:], st[:, 1, :].unsqueeze(2).to_broadcast([N, G, DK]), ALU.mult)
                dve.drain()
                dve.tensor_tensor(kc[:], kc[:], S.gains[0:N, 3:4, :].to_broadcast([N, G, DK]), ALU.mult).then_inc(s_ve, 1)
                dve.wait_ge(s_pe, 3)
                dve.tensor_copy(S.kcT[:, 0:N], S.ps[:, 3, 0:N])

            @block.scalar
            def _(act):
                act.wait_ge(s_ve, 2)
                act.activation(st[:, 1, :], st[:, 0, :], ACT.Sqrt).then_inc(s_rt, 1)


def prompt_attention(nc, S):
    units = [(t, g, kind) for t in range(4) for g in range(G) for kind in ("slc", "win", "cmp")]
    NU = len(units)
    NCMP = [7 + 8 * t for t in range(4)]
    with ExitStack() as ctx:
        lent = S.kv[:, 1].rearrange("p b n d -> p (b n d)")
        q = lent[:, 0:SEQ]
        s, p, pT = (lent[:, SEQ + i * 1024:SEQ + (i + 1) * 1024].rearrange("p (a n) -> p a n", a=2) for i in range(3))
        st = sb(nc, ctx, "pa_st", [P, 4, 4])
        s_q = nc.alloc_semaphore("pa_query_ready")
        s_qk = nc.alloc_semaphore("pa_scores_ready")
        s_sc = nc.alloc_semaphore("pa_logits_ready")
        s_p = nc.alloc_semaphore("pa_probs_ready")
        s_tr = nc.alloc_semaphore("pa_probs_transposed")
        s_pt = nc.alloc_semaphore("pa_probsT_ready")
        s_pv = nc.alloc_semaphore("pa_values_ready")
        s_fin = nc.alloc_semaphore("pa_unit_added")

        def width(u):
            t, g, kind = units[u]
            return NCMP[t] if kind == "cmp" else (t + 1) * P

        with nc.Block() as block:
            @block.sync
            def _(sp):
                sp.dma_start(S.pt[:], S.page_table.rearrange("b n -> (b n)").unsqueeze(0)).then_inc(S.s_pages, 16)
                sp.wait_ge(S.s_pages, 16)
                sp.wait_ge(S.s_out, 16 * S.n_out)
                load_round(S, sp, 0)

            @block.tensor
            def _(pe):
                def scores(j, u):
                    t, g, kind = units[u]
                    keys = {"slc": S.ksT, "win": S.kwT, "cmp": S.kcT}[kind]
                    if u >= 2:
                        pe.wait_ge(s_sc, j * NU + u - 1)
                    pe.matmul(S.ps[:, u % 2, 0:width(u)], q[g * DK:(g + 1) * DK, t * P:(t + 1) * P],
                              keys[g * DK:(g + 1) * DK, 0:width(u)], start=True, stop=True).then_inc(s_qk, 1)

                def turn(j, u):
                    t, g, kind = units[u]
                    pe.wait_ge(s_p, j * NU + u + 1)
                    if u >= 2:
                        pe.wait_ge(s_pt, j * NU + u - 1)
                    for k0 in range(0, width(u), P):
                        n = min(P, width(u) - k0)
                        tr = pe.transpose(S.ps[0:n, 2 + u % 2, k0:k0 + P], p[:, u % 2, k0:k0 + n], S.ident[:])
                    tr.then_inc(s_tr, 1)

                def values(j, u):
                    t, g, kind = units[u]
                    pe.wait_ge(s_pt, j * NU + u + 1)
                    if u >= 2:
                        pe.wait_ge(s_fin, j * NU + u - 1)
                    out = S.ps[:, 4 + u % 2, 0:DK]
                    if kind == "cmp":
                        n = width(u)
                        mm = pe.matmul(out, pT[0:n, u % 2, 0:P], S.vc[0:n, g * DK:(g + 1) * DK], start=True, stop=True)
                    else:
                        c = COL["vs" if kind == "slc" else "vw"] + g * DK
                        for k in range(t + 1):
                            mm = pe.matmul(out, pT[:, u % 2, k * P:(k + 1) * P], S.pj[:, k, c:c + DK],
                                           start=(k == 0), stop=(k == t))
                    mm.then_inc(s_pv, 1)

                with pe.Fori(0, HPG) as j:
                    pe.wait_ge(s_q, j + 1)
                    for k in range(NU + 2):
                        if k < NU:
                            scores(j, k)
                        if 1 <= k <= NU:
                            turn(j, k - 1)
                        if k >= 2:
                            values(j, k - 2)

            @block.vector
            def _(dve):
                def logits(j, u):
                    t, g, kind = units[u]
                    w = width(u)
                    if kind == "cmp":
                        lo = 415 - P * t
                        bias = S.toep[:, bass.ds(g * HPG + j, 1), lo:lo + 16 * (w - 1) + 1:16]
                    else:
                        bias = S.toep[:, bass.ds(g * HPG + j, 1), 384 - P * t:512]
                    dve.wait_ge(s_qk, j * NU + u + 1)
                    if u >= 2:
                        dve.wait_ge(s_p, j * NU + u - 1)
                    dve.scalar_tensor_tensor(s[:, u % 2:u % 2 + 1, 0:w], S.ps[:, u % 2:u % 2 + 1, 0:w], SCALE, bias,
                                             ALU.mult, ALU.add)
                    dve.drain()
                    dve.tensor_reduce(st[:, u % 4, 0:1], s[:, u % 2, 0:w], X, ALU.max, negate=True).then_inc(s_sc, 1)

                def finish(j, u):
                    t, g, kind = units[u]
                    i = u % 4
                    col = {"cmp": 0, "slc": 1, "win": 2}[kind] * H + g * HPG
                    dve.wait_ge(s_pv, j * NU + u + 1)
                    dve.reciprocal(st[:, i, 2:3], st[:, i, 1:2])
                    dve.drain()
                    dve.tensor_tensor(st[:, i, 2:3], st[:, i, 2:3], S.gates[:, t, bass.ds(col + j, 1)], ALU.mult)
                    dve.drain()
                    if kind == "cmp" and t == 0:
                        dve.tensor_tensor(st[:, i, 2:3], st[:, i, 2:3], S.misc[:, 0:1], ALU.mult)
                        dve.drain()
                    dst = S.onsa[:, t, bass.ds((g * HPG + j) * DK, DK)]
                    if kind == "slc":
                        dve.tensor_scalar(dst, S.ps[:, 4 + u % 2, 0:DK], st[:, i, 2:3], None, ALU.mult).then_inc(s_fin, 1)
                    else:
                        dve.scalar_tensor_tensor(dst, S.ps[:, 4 + u % 2, 0:DK], st[:, i, 2:3], dst,
                                                 ALU.mult, ALU.add).then_inc(s_fin, 1)

                with dve.Fori(0, HPG) as j:
                    dve.tensor_copy(q, S.qT[:, bass.ds(j, 1), 0:SEQ].rearrange("p a n -> p (a n)")).then_inc(s_q, 1)
                    for k in range(NU + 2):
                        if k < NU:
                            logits(j, k)
                        if k >= 2:
                            finish(j, k - 2)
                    dve.drain()

            @block.scalar
            def _(act):
                with act.Fori(0, HPG) as j:
                    for k in range(NU + 1):
                        if k < NU:
                            u = k
                            act.wait_ge(s_sc, j * NU + u + 1)
                            if u >= 2:
                                act.wait_ge(s_tr, j * NU + u - 1)
                            act.activation(p[:, u % 2, 0:width(u)], s[:, u % 2, 0:width(u)], ACT.Exp,
                                           bias=st[:, u % 4, 0:1], accum_out=st[:, u % 4, 1:2]).then_inc(s_p, 1)
                        if k >= 1:
                            u = k - 1
                            n = P if units[u][2] != "cmp" else width(u)
                            w = P if units[u][2] == "cmp" else width(u)
                            act.wait_ge(s_tr, j * NU + u + 1)
                            if u >= 2:
                                act.wait_ge(s_pv, j * NU + u - 1)
                            act.activation(pT[0:n, u % 2, 0:w], S.ps[0:n, 2 + u % 2, 0:w], ACT.Copy).then_inc(s_pt, 1)


def settle(pe, S):
    pe.transpose(S.ps[:, 2, 384:512], S.ident[:], S.ident[:])


def load_pages(nc, S, ctx):
    S.pt = sb(nc, ctx, "sa_pages", [1, DEC_B * NPAGE], I32)
    S.kv = sb(nc, ctx, "sa_kv", [P, 2, 2, NPAGE, 512])
    S.wn = sb(nc, ctx, "sa_win", [P, 2, 2, 4, 256])
    S.vn = sb(nc, ctx, "sa_vnew", [DEC_T, 2, 2, 2, P])
    S.s_pages = nc.alloc_semaphore("sa_pages_loaded")
    S.s_round = [nc.alloc_semaphore("sa_even_loaded"), nc.alloc_semaphore("sa_odd_loaded")]


def load_round(S, sp, r):
    par = r % 2
    for bb in range(2):
        b = r * 2 + bb
        for n in range(NPAGE):
            page = sp.value_load(S.pt[0:1, b * NPAGE + n:b * NPAGE + n + 1], min_val=0, max_val=S.cache_kv.shape[0] - 1)
            sp.dma_start(S.kv[:, par, bb, n, :],
                         S.cache_kv[bass.ds(page, 1)].rearrange("a p s g d -> p (a s g d)")).then_inc(S.s_round[par], 16)
        sp.dma_start(S.wn[:, par, bb, :, :],
                     S.cache_win[b].rearrange("(n p) s g d -> p n (s g d)", p=P)).then_inc(S.s_round[par], 16)
        sp.dma_start(S.vn[:, par, bb, 0, :], S.kv_sample[b, :, 3].rearrange("t g d -> t (g d)")).then_inc(S.s_round[par], 16)
        sp.dma_start(S.vn[:, par, bb, 1, :],
                     S.win_sample[b, WIN - DEC_T:WIN, 1].rearrange("t g d -> t (g d)")).then_inc(S.s_round[par], 16)


def sample_attention(nc, S):
    NC, K1, KW = 63, PAST + DEC_T, WIN + DEC_T
    NSLC = 17
    with ExitStack() as ctx:
        kv, wn, vn = S.kv, S.wn, S.vn
        q = sb(nc, ctx, "sa_q", [P, 2, 4, DEC_T])
        lent = S.toep[:].rearrange("p h n -> p (h n)")
        kT = lent[:, 0:2 * K1].rearrange("p (a k) -> p a k", a=2)
        wT = lent[:, 2 * K1:2 * K1 + 2 * KW].rearrange("p (a k) -> p a k", a=2)
        lw = lent[:, 2 * K1 + 2 * KW:2 * K1 + 3 * KW]
        end = 2 * K1 + 3 * KW
        blk = lent[:, end:end + 4 * NC].rearrange("p (b k n) -> p b k n", b=2, k=2)
        o = lent[:, end + 4 * NC:end + 4 * NC + DK]
        kc = sb(nc, ctx, "sa_kc", [NC, 2, G, DK])
        vc = sb(nc, ctx, "sa_vc", [NC, 2, P])
        kst = sb(nc, ctx, "sa_kst", [NC, 2, 2 * G])
        kcT = sb(nc, ctx, "sa_kcT", [P, 2, NC])
        lc = sb(nc, ctx, "sa_lc", [P, NC])
        ls = sb(nc, ctx, "sa_ls", [P, K1])
        halves = ls[:, 0:512].rearrange("p (b k h n) -> p b k h n", b=2, k=2, h=2)
        sq = lw[0:NC, 0:256].rearrange("p (b g e) -> p b g e", b=2, g=G)
        pext = lent[:, end + 4 * NC + DK:end + 4 * NC + DK + 72]
        end += 4 * NC + DK + 72
        sel = lent[:, end:end + 4 * NSLC].rearrange("p (a n) -> p a n", a=4)
        st = sb(nc, ctx, "sa_st", [P, 12])
        pTc = sb(nc, ctx, "sa_pTc", [NC, P])
        pTs = kT[:, 0, 0:PAST].rearrange("p (n a) -> p n a", n=NPAGE)
        pTw = wT[:, 0, 0:WIN].rearrange("p (n a) -> p n a", n=4)
        pTn = sb(nc, ctx, "sa_pTn", [DEC_T, 2, P])
        names = ["sa_round_read", "sa_halves_summed", "sa_blocks_ready",
                 "sa_kvc_summed", "sa_inverse_ready", "sa_root_ready", "sa_kc_normed", "sa_kc_transposed",
                 "sa_kcT_ready", "sa_bank_transposed", "sa_bank_moved", "sa_copies_ready", "sa_scores_ready",
                 "sa_cmp_logits", "sa_cmp_exp", "sa_cmp_probs", "sa_group_summed", "sa_logits_ready", "sa_exp_ready",
                 "sa_probs_turned", "sa_probsT_ready", "sa_values_ready", "sa_out_ready", "sa_out_stored",
                 "sa_cmp_values", "sa_cmp_turned", "sa_turn_bank", "sa_turn_moved", "sa_final_load", "sa_out_free"]
        m = {n[3:]: nc.alloc_semaphore(n) for n in names}
        m["even_loaded"], m["odd_loaded"] = S.s_round
        tail = S.ps[:, 2, 0:8]
        wtail = S.ps[:, 2, 8:16]
        csc = S.ps[:, 2, 64:64 + NC]
        cps = S.ps[:, 6, :].rearrange("p (b k h n) -> p b k h n", b=2, k=2, h=2)
        kvc = S.ps[0:NC, 6:8, 0:256].rearrange("p g (b k e) -> p g b k e", b=2, k=2)
        NLOAD = 2 * (NPAGE + 3)
        combos = [(bb, g) for bb in range(2) for g in range(G)]

        with nc.Block() as block:
            @block.sync
            def _(sp):
                load_round(S, sp, 1)
                for r in (2, 3):
                    sp.wait_ge(m["round_read"], r + 1)
                    load_round(S, sp, r)

            @block.tensor
            def _(pe):
                with pe.Fori(0, 2) as rr:
                    for par in range(2):
                        r1 = rr * 2 + par + 1
                        pe.wait_ge(m["even_loaded"] if par == 0 else m["odd_loaded"], (rr + 1) * 16 * NLOAD)
                        for bb in range(2):
                            for k in range(2):
                                for g in range(G):
                                    for n in range(NPAGE):
                                        mm = pe.matmul(cps[g * DK:(g + 1) * DK, bb, k, :, n * NSUB:(n + 1) * NSUB],
                                                       kv[:, par, bb, n, k * P + g * DK:k * P + (g + 1) * DK],
                                                       S.w16[:, k * 2 + g], start=True, stop=True)
                        mm.then_inc(m["halves_summed"], 1)
                        for f in range(6):
                            bb, part3 = divmod(f, 3)
                            if f >= 2:
                                pe.wait_ge(m["bank_moved"], (rr * 2 + par) * 6 + f - 1)
                            for i in range(4):
                                src = (kv[:, par, bb, part3 * 4 + i, 2 * P:3 * P] if part3 < 2 else wn[:, par, bb, i, 0:P])
                                tr = pe.transpose(S.ps[:, 4 + f % 2, i * P:(i + 1) * P], src, S.ident[:])
                            tr.then_inc(m["bank_transposed"], 1)
                        pe.wait_ge(m["blocks_ready"], r1)
                        settle(pe, S)
                        for bb in range(2):
                            for k in range(2):
                                for g in range(G):
                                    mm = pe.matmul(kvc[:, g, bb, k, :], blk[g * DK:(g + 1) * DK, bb, k, :],
                                                   S.cproj[g * DK:(g + 1) * DK, k, :], start=True, stop=True)
                        mm.then_inc(m["kvc_summed"], 1)
                        pe.wait_ge(m["kc_normed"], r1)
                        pe.wait_ge(m["bank_moved"], (rr * 2 + par) * 6 + 6)
                        settle(pe, S)
                        for bb in range(2):
                            tr = pe.transpose(S.ps[:, 4, bb * P:bb * P + NC], kc[:, bb].rearrange("p g e -> p (g e)"),
                                              S.ident[0:NC, 0:NC])
                        tr.then_inc(m["kc_transposed"], 1)
                        pe.wait_ge(m["kcT_ready"], r1)
                        pe.wait_ge(m["copies_ready"], r1)
                        settle(pe, S)
                        for c, (bb, g) in enumerate(combos):
                            lhs = q[g * DK:(g + 1) * DK, bb].rearrange("p j t -> p (j t)")
                            rows = slice(32 * c, 32 * c + 32)
                            kr = slice(g * DK, (g + 1) * DK)
                            pe.matmul(csc[rows], lhs, kcT[kr, bb, :], start=True, stop=True)
                            pe.matmul(S.ps[rows, 0, :], lhs, kT[kr, bb, 0:512], start=True, stop=True)
                            pe.matmul(S.ps[rows, 1, :], lhs, kT[kr, bb, 512:1024], start=True, stop=True)
                            pe.matmul(tail[rows], lhs, kT[kr, bb, 1024:K1], start=True, stop=True)
                            pe.matmul(S.ps[rows, 3, :], lhs, wT[kr, bb, 0:512], start=True, stop=True)
                            mm = pe.matmul(wtail[rows], lhs, wT[kr, bb, 512:KW], start=True, stop=True)
                        mm.then_inc(m["scores_ready"], 1)
                        pe.wait_ge(m["cmp_probs"], r1)
                        pe.matmul(S.ps[:, 6, 0:NC], S.grp[:], lc[:], start=True, stop=True).then_inc(m["group_summed"], 1)
                        pe.transpose(S.ps[0:NC, 4, 256:384], lc[:], S.ident[:]).then_inc(m["cmp_turned"], 1)
                        pe.wait_ge(m["exp_ready"], r1)
                        for f in range(4):
                            if f == 0:
                                pe.wait_ge(m["cmp_values"], r1)
                            if f >= 2:
                                pe.wait_ge(m["turn_moved"], (rr * 2 + par) * 4 + f - 1)
                            bank = S.ps[:, 4 + f % 2, :]
                            if f < 3:
                                for i in range(4):
                                    src = ls[:, (4 * f + i) * P:(4 * f + i + 1) * P] if f < 2 else lw[:, i * P:(i + 1) * P]
                                    tr = pe.transpose(bank[:, i * P:(i + 1) * P], src, S.ident[:])
                            else:
                                pe.transpose(bank[0:DEC_T, 0:P], ls[:, PAST:K1], S.ident[:])
                                tr = pe.transpose(bank[0:DEC_T, P:2 * P], lw[:, WIN:KW], S.ident[:])
                            tr.then_inc(m["turn_bank"], 1)
                        pe.wait_ge(m["turn_moved"], (rr * 2 + par) * 4 + 4)
                        settle(pe, S)
                        for c, (bb, g) in enumerate(combos):
                            rows = slice(32 * c, 32 * c + 32)
                            gc = slice(g * DK, (g + 1) * DK)
                            pe.matmul(S.ps[rows, 7, 0:DK], pTc[:, rows], vc[:, bb, gc], start=True, stop=True)
                            for n in range(NPAGE):
                                pe.matmul(S.ps[rows, 0, 0:DK], pTs[:, n, rows],
                                          kv[:, par, bb, n, 3 * P + g * DK:3 * P + (g + 1) * DK], start=(n == 0), stop=False)
                            pe.matmul(S.ps[rows, 0, 0:DK], pTn[:, 0, rows], vn[:, par, bb, 0, gc], start=False, stop=True)
                            for n in range(4):
                                pe.matmul(S.ps[rows, 3, 0:DK], pTw[:, n, rows],
                                          wn[:, par, bb, n, P + g * DK:P + (g + 1) * DK], start=(n == 0), stop=False)
                            mm = pe.matmul(S.ps[rows, 3, 0:DK], pTn[:, 1, rows], vn[:, par, bb, 1, gc], start=False, stop=True)
                        mm.then_inc(m["values_ready"], 1)
                        pe.wait_ge(m["out_ready"], r1)
                        pe.sem_inc(m["round_read"], 1)

            @block.vector
            def _(dve):
                dve.sem_inc(m["round_read"], 2)
                dve.memset(pext, 0.0)
                with dve.Fori(0, 2) as rr:
                    for par in range(2):
                        r1 = rr * 2 + par + 1
                        b0 = rr * 4 + par * 2
                        for bb in range(2):
                            at = (b0 + bb) * DEC_T + SEQ
                            dve.tensor_copy(q[:, bb], S.qT[:, :, bass.ds(at, DEC_T)])
                            dve.tensor_copy(kT[:, bb, PAST:K1], S.ksT[:, bass.ds(at, DEC_T)])
                            dve.tensor_copy(wT[:, bb, WIN:KW], S.kwT[:, bass.ds(at, DEC_T)])
                        dve.drain().then_inc(m["copies_ready"], 1)
                        dve.wait_ge(m["halves_summed"], r1)
                        dve.tensor_copy(halves, cps)
                        dve.drain()
                        dve.tensor_tensor(blk.rearrange("p b k n -> p (b k) n"),
                                          halves.rearrange("p b k h n -> p (b k) h n")[:, :, 0, 0:NC],
                                          halves.rearrange("p b k h n -> p (b k) h n")[:, :, 1, 1:NC + 1],
                                          ALU.add).then_inc(m["blocks_ready"], 1)
                        dve.wait_ge(m["kvc_summed"], r1)
                        for g in range(G):
                            dve.tensor_copy(vc[:, :, g * DK:(g + 1) * DK], kvc[:, g, :, 1])
                            dve.tensor_copy(kc[:, :, g], kvc[:, g, :, 0])
                        dve.drain()
                        dve.tensor_tensor(sq, kc[:], kc[:], ALU.mult)
                        dve.drain()
                        dve.tensor_reduce(kst[:, 0, :], sq.rearrange("p b g e -> p (b g) e"), X, ALU.add)
                        dve.drain()
                        dve.tensor_scalar(kst[:, 0, :], kst[:, 0, :], 1.0 / DK, EPS, ALU.mult, ALU.add)
                        dve.drain()
                        dve.reciprocal(kst[:, 0, :], kst[:, 0, :]).then_inc(m["inverse_ready"], 1)
                        dve.wait_ge(m["root_ready"], r1)
                        kcv = kc[:].rearrange("p b g e -> p (b g) e")
                        dve.tensor_tensor(kcv, kcv, kst[:, 1, :].unsqueeze(2).to_broadcast([NC, 4, DK]), ALU.mult)
                        dve.drain()
                        dve.tensor_tensor(kcv, kcv, S.gains[0:NC, 3:4, :].to_broadcast([NC, 4, DK]), ALU.mult).then_inc(m["kc_normed"], 1)
                        dve.wait_ge(m["kc_transposed"], r1)
                        dve.tensor_copy(kcT[:], S.ps[:, 4, 0:256].rearrange("p (b n) -> p b n", b=2)[:, :, 0:NC]).then_inc(m["kcT_ready"], 1)
                        dve.wait_ge(m["scores_ready"], r1)
                        dve.scalar_tensor_tensor(lc[:], csc, SCALE, S.sbias[:, 31:1024:16], ALU.mult, ALU.add)
                        dve.scalar_tensor_tensor(ls[:, 0:1024], S.ps[:, 0:2, :].rearrange("p a n -> p (a n)"), SCALE,
                                                 S.sbias[:, 0:1024], ALU.mult, ALU.add)
                        dve.drain()
                        dve.tensor_reduce(st[:, 0:1], lc[:], X, ALU.max, negate=True)
                        dve.drain().then_inc(m["cmp_logits"], 1)
                        dve.scalar_tensor_tensor(ls[:, 1024:K1], tail, SCALE, S.sbias[:, 1024:K1], ALU.mult, ALU.add)
                        dve.scalar_tensor_tensor(lw[:, 0:512], S.ps[:, 3, :], SCALE, S.sbias[:, 512:1024], ALU.mult, ALU.add)
                        dve.scalar_tensor_tensor(lw[:, 512:KW], wtail, SCALE, S.sbias[:, 1024:K1], ALU.mult, ALU.add)
                        dve.drain()
                        dve.tensor_tensor(lw[:, 0:8], lw[:, 0:8], S.misc[:, 1:9], ALU.add)
                        dve.drain()
                        dve.tensor_reduce(st[:, 4:5], lw, X, ALU.max, negate=True)
                        dve.wait_ge(m["cmp_exp"], r1)
                        dve.reciprocal(st[:, 2:3], st[:, 1:2])
                        dve.drain()
                        dve.tensor_scalar(lc[:], lc[:], st[:, 2:3], None, ALU.mult).then_inc(m["cmp_probs"], 1)
                        dve.wait_ge(m["group_summed"], r1)
                        dve.tensor_copy(pext[:, 1:1 + NC], S.ps[:, 6, 0:NC])
                        dve.drain()
                        dve.tensor_reduce(sel[:, 0, :], pext[:, 0:68].rearrange("p (j r) -> p j r", r=4), X, ALU.add)
                        dve.drain()
                        dve.tensor_tensor(sel[:, 0, :], sel[:, 0, :], pext[:, 4:69:4], ALU.add)
                        dve.drain()
                        dve.tensor_reduce(st[:, 3:4], sel[:, 0, 1:15], X, ALU.min)
                        dve.drain()
                        dve.scalar_tensor_tensor(sel[:, 1, 1:15], sel[:, 0, 1:15], st[:, 3:4], S.misc[:, 17:31],
                                                 ALU.is_equal, ALU.mult)
                        dve.drain()
                        dve.tensor_reduce(st[:, 3:4], sel[:, 1, 1:15], X, ALU.max)
                        dve.drain()
                        dve.tensor_scalar(sel[:, 2, :], S.misc[:, 16:33], st[:, 3:4], NEG, ALU.is_equal, ALU.mult)
                        dve.drain()
                        lsv = ls[:, 0:1024].rearrange("p (j l) -> p j l", l=64)
                        dve.tensor_tensor(lsv, lsv, sel[:, 2, 0:16].unsqueeze(2).to_broadcast([P, 16, 64]), ALU.add)
                        dve.drain()
                        dve.tensor_reduce(st[:, 6:7], ls[:], X, ALU.max, negate=True).then_inc(m["logits_ready"], 1)
                        dve.wait_ge(m["cmp_turned"], r1)
                        dve.tensor_copy(pTc[:], S.ps[0:NC, 4, 256:384]).then_inc(m["cmp_values"], 1)
                        for f in (1, 3):
                            dve.wait_ge(m["turn_bank"], (rr * 2 + par) * 4 + f + 1)
                            dve.wait_ge(m["turn_moved"], (rr * 2 + par) * 4 + f)
                            if f == 1:
                                dve.tensor_copy(kT[:, 0, 512:PAST], S.ps[:, 5, :]).then_inc(m["turn_moved"], 1)
                            else:
                                dve.tensor_copy(pTn[:].rearrange("p a n -> p (a n)"), S.ps[0:DEC_T, 5, 0:256]).then_inc(m["turn_moved"], 1)
                        dve.reciprocal(st[:, 8:9], st[:, 7:8])
                        dve.reciprocal(st[:, 9:10], st[:, 5:6])
                        dve.drain()
                        dve.tensor_tensor(st[:, 8:10], st[:, 8:10], S.grow[:, bass.ds(rr * 2 + par, 1), 1:3].rearrange("p a n -> p (a n)"), ALU.mult)
                        dve.wait_ge(m["values_ready"], r1)
                        dve.wait_ge(m["out_free"], r1)
                        dve.tensor_tensor(o, S.ps[:, 7, 0:DK], S.grow[:, bass.ds(rr * 2 + par, 1), 0:1].rearrange("p a n -> p (a n)").to_broadcast([P, DK]), ALU.mult)
                        dve.drain()
                        dve.scalar_tensor_tensor(o, S.ps[:, 0, 0:DK], st[:, 8:9], o, ALU.mult, ALU.add)
                        dve.drain()
                        dve.scalar_tensor_tensor(o, S.ps[:, 3, 0:DK], st[:, 9:10], o, ALU.mult, ALU.add).then_inc(m["out_ready"], 1)

            @block.scalar
            def _(act):
                with act.Fori(0, 2) as rr:
                    for par in range(2):
                        r1 = rr * 2 + par + 1
                        for f in range(6):
                            bb, part3 = divmod(f, 3)
                            act.wait_ge(m["bank_transposed"], (rr * 2 + par) * 6 + f + 1)
                            dst = kT[:, bb, part3 * 512:(part3 + 1) * 512] if part3 < 2 else wT[:, bb, 0:512]
                            act.activation(dst, S.ps[:, 4 + f % 2, :], ACT.Copy).then_inc(m["bank_moved"], 1)
                        act.wait_ge(m["inverse_ready"], r1)
                        act.activation(kst[:, 1, :], kst[:, 0, :], ACT.Sqrt).then_inc(m["root_ready"], 1)
                        act.wait_ge(m["cmp_logits"], r1)
                        act.activation(lc[:], lc[:], ACT.Exp, bias=st[:, 0:1], accum_out=st[:, 1:2]).then_inc(m["cmp_exp"], 1)
                        act.wait_ge(m["logits_ready"], r1)
                        act.activation(ls[:], ls[:], ACT.Exp, bias=st[:, 6:7], accum_out=st[:, 7:8])
                        act.activation(lw, lw, ACT.Exp, bias=st[:, 4:5], accum_out=st[:, 5:6]).then_inc(m["exp_ready"], 1)
                        for f in (0, 2):
                            act.wait_ge(m["turn_bank"], (rr * 2 + par) * 4 + f + 1)
                            if f == 0:
                                act.activation(kT[:, 0, 0:512], S.ps[:, 4, :], ACT.Copy).then_inc(m["turn_moved"], 1)
                            else:
                                act.wait_ge(m["turn_moved"], (rr * 2 + par) * 4 + f)
                                act.activation(wT[:, 0, 0:WIN], S.ps[:, 4, :], ACT.Copy).then_inc(m["turn_moved"], 1)

            @block.gpsimd
            def _(pool):
                pool.sem_inc(m["out_free"], 1)
                with pool.Fori(0, 4) as r:
                    pool.wait_ge(m["out_ready"], r + 1)
                    for bb in range(2):
                        pool.dma_start(S.osa_dram[bass.ds(r * 2 + bb, 1)].rearrange("a t h d -> (a h) t d"),
                                       o[bb * 64:(bb + 1) * 64, :]).then_inc(m["out_stored"], 16)
                    pool.wait_ge(m["out_stored"], r * 32 + 32)
                    pool.sem_inc(m["out_free"], 1)
                pool.memset(S.onsa[:, 4, :], 0.0).then_inc(m["final_load"], 1)
                pool.wait_ge(m["final_load"], 1)
                pool.dma_start(S.onsa[0:64, 4, :], S.osa_dram.rearrange("b t h d -> (b t) (h d)")).then_inc(m["out_stored"], 16)
                pool.wait_ge(m["out_stored"], 32 * 4 + 16)


def gla_inputs(nc, S):
    with ExitStack() as ctx:
        aup = sb(nc, ctx, "gi_aup", [RANK, HG * DKG])
        ab = sb(nc, ctx, "gi_ab", [P, 2])
        reset = sb(nc, ctx, "gi_reset", [P, TOK])
        alT = sb(nc, ctx, "gi_alT", [RANK, TOK])
        z = sb(nc, ctx, "gi_z", [P, 2, TOK])
        e = sb(nc, ctx, "gi_e", [P, 2, TOK])
        s_ld = nc.alloc_semaphore("gi_loaded")
        s_tr = nc.alloc_semaphore("gi_transposed")
        s_mv = nc.alloc_semaphore("gi_moved")
        s_zm = nc.alloc_semaphore("gi_logit_summed")
        s_z = nc.alloc_semaphore("gi_logit_ready")
        s_ln = nc.alloc_semaphore("gi_log_ready")
        blocks = [(S.gq[:, p, :], COL["qg"] + p * P) for p in range(2)] + [(S.gk[:, p, :], COL["kg"] + p * P) for p in range(2)]
        with nc.Block() as block:
            @block.sync
            def _(sp):
                sp.dma_start(aup[:], S.gla_a_up[:, :]).then_inc(s_ld, 16)
                with nc.allow_non_contiguous_dma(reason="256 decay biases, one per partition"):
                    sp.dma_start(ab[:], S.gla_a_b.rearrange("(a p) -> p a", p=P)).then_inc(s_ld, 16)
                sp.dma_start(reset[:], S.c_reset.partition_broadcast(P)).then_inc(s_ld, 16)
                sp.dma_start(S.gmask[:], S.c_gmask.rearrange("a p n -> p a n")).then_inc(s_ld, 16)
                sp.dma_start(S.seqof[:], S.c_seqof[:, :]).then_inc(s_ld, 16)
                for p in range(2):
                    sp.dma_start(S.gs[:, p], S.state_gla.rearrange("b (a h) k v -> a (h k) b v", a=2)[p]).then_inc(s_ld, 16)

            @block.tensor
            def _(pe):
                for t in range(NT):
                    tr = pe.transpose(S.ps2[0:RANK, 0, t * P:(t + 1) * P],
                                      S.pj[:, t, COL["al"]:COL["al"] + RANK], S.ident[:])
                tr.then_inc(s_tr, 1)
                for i, (_, c) in enumerate(blocks):
                    if i >= 1:
                        pe.wait_ge(s_mv, i + 1)
                    for t in range(NT):
                        tr = pe.transpose(S.ps2[:, 1, t * P:(t + 1) * P], S.pj[:, t, c:c + P], S.ident[:])
                    tr.then_inc(s_tr, 1)
                pe.wait_ge(s_ld, 16 * 7)
                for p in range(2):
                    pe.matmul(S.ps2[:, 2 + p, 0:512], aup[:, p * P:(p + 1) * P], alT[:, 0:512], start=True, stop=True)
                    mm = pe.matmul(S.ps2[:, 2 + p, 512:TOK], aup[:, p * P:(p + 1) * P], alT[:, 512:TOK], start=True, stop=True)
                mm.then_inc(s_zm, 1)

            @block.vector
            def _(dve):
                dve.wait_ge(s_tr, 1)
                dve.tensor_copy(alT[:], S.ps2[0:RANK, 0, 0:TOK]).then_inc(s_mv, 1)
                for i, (dst, _) in enumerate(blocks):
                    dve.wait_ge(s_tr, i + 2)
                    dve.tensor_copy(dst, S.ps2[:, 1, 0:TOK]).then_inc(s_mv, 1)
                dve.wait_ge(s_zm, 1)
                for p in range(2):
                    dve.tensor_scalar(z[:, p, :], S.ps2[:, 2 + p, 0:TOK], ab[:, p:p + 1], None, ALU.add)
                dve.drain().then_inc(s_z, 1)
                dve.wait_ge(s_ln, 1)
                dve.scalar_tensor_tensor(z[:], z[:], 0.0, e[:], ALU.min, ALU.subtract)
                dve.drain()
                dve.tensor_scalar(z[:], z[:], 1.0 / TAU, None, ALU.mult)
                dve.drain()
                for p in range(2):
                    dve.tensor_tensor_scan(S.gb[:, p, :], reset[:], z[:, p, :], 0.0, ALU.mult, ALU.add)

            @block.scalar
            def _(act):
                act.wait_ge(s_z, 1)
                act.activation(e[:], z[:], ACT.Abs)
                act.drain()
                act.activation(e[:], e[:], ACT.Exp, scale=-1.0)
                act.drain()
                act.activation(e[:], e[:], ACT.Ln, bias=S.ones[:, 0:1]).then_inc(s_ln, 1)


def gla_chunks(nc, S):
    GRP, NG, CLAMP, QS = 8, P // 8, 40.0, DKG ** -0.5
    CH = SEQ // P
    V = COL["vg"]
    with ExitStack() as ctx:
        dq = sb(nc, ctx, "gc_dq", [P, 2, P])
        de = sb(nc, ctx, "gc_de", [P, 2, P])
        eb = sb(nc, ctx, "gc_eb", [P, 2, 2, P])
        qt = sb(nc, ctx, "gc_qt", [P, 2, 2, NG, 2, GRP])
        qe = sb(nc, ctx, "gc_qe", [P, 2, 2, P])
        ke = sb(nc, ctx, "gc_ke", [P, 2, 2, P])
        kt = sb(nc, ctx, "gc_kt", [P, 2, 2, NG, P])
        keT = sb(nc, ctx, "gc_keT", [P, 2, P])
        at = sb(nc, ctx, "gc_at", [P, HG, P])
        st = sb(nc, ctx, "gc_state", [P, 2, DVG])
        qb = sb(nc, ctx, "gc_qb", [P, 2, DEC_B, P])
        vb = sb(nc, ctx, "gc_vb", [P, 2, DEC_B, DVG])
        s_df = nc.alloc_semaphore("gc_exponents_ready")
        s_ex = nc.alloc_semaphore("gc_exps_ready")
        s_fa = nc.alloc_semaphore("gc_factors_ready")
        s_fb = nc.alloc_semaphore("gc_second_pair_keys_ready")
        s_at = nc.alloc_semaphore("gc_attention_summed")
        s_am = nc.alloc_semaphore("gc_attention_masked")
        s_o = nc.alloc_semaphore("gc_outputs_summed")
        s_sv = nc.alloc_semaphore("gc_state_ready")
        s_vb = nc.alloc_semaphore("gc_split_values_ready")
        s_kv = nc.alloc_semaphore("gc_sample_state_summed")
        s_new = nc.alloc_semaphore("gc_sample_state_ready")
        attn = S.ps[:, 0:2, 0:2 * P].rearrange("p a (n h e) -> p a n h e", h=2, e=GRP)
        outs = S.ps[:, 2:4, 0:2 * DVG]
        span = [slice(c * P, (c + 1) * P) for c in range(CH + 1)]
        groups = lambda x: x.rearrange("p a (n e) -> p a n e", e=GRP)

        with nc.Block() as block:
            @block.vector
            def _(dve):
                def factors(c):
                    p = c % 2
                    b = S.gb[:, :, span[c]]
                    b4 = groups(b)
                    dve.tensor_tensor(groups(dq[:]), b4, b4[:, :, :, 3:4].to_broadcast([P, 2, NG, GRP]), ALU.subtract)
                    for a in range(2):
                        dve.tensor_tensor(kt[:, p, a], b[:, a, 3::GRP].unsqueeze(2).to_broadcast([P, NG, P]),
                                          b[:, a:a + 1, :].to_broadcast([P, NG, P]), ALU.subtract)
                    if c == CH:
                        dve.tensor_tensor(groups(de[:]), b4[:, :, :, GRP - 1:GRP].to_broadcast([P, 2, NG, GRP]), b4, ALU.subtract)
                    else:
                        dve.tensor_tensor(de[:], b[:, :, P - 1:P].to_broadcast([P, 2, P]), b, ALU.subtract)
                    dve.drain()
                    dve.tensor_scalar(dq[:], dq[:], CLAMP, None, ALU.min)
                    dve.tensor_scalar(kt[:, p], kt[:, p], CLAMP, None, ALU.min)
                    dve.drain().then_inc(s_df, 1)
                    dve.wait_ge(s_ex, c + 1)
                    for h in range(2):
                        r = slice(64 * h, 64 * h + 64)
                        for a in range(2):
                            dve.scalar_tensor_tensor(qt[r, p, a, :, h, :], S.gq[r, a, span[c]].rearrange("p (n e) -> p n e", e=GRP), QS,
                                                     dq[r, a, :].rearrange("p (n e) -> p n e", e=GRP), ALU.mult, ALU.mult)
                    dve.scalar_tensor_tensor(qe[:, p], S.gq[:, :, span[c]], QS, eb[:, p], ALU.mult, ALU.mult)
                    dve.tensor_tensor(ke[:, p], S.gk[:, :, span[c]], de[:], ALU.mult)
                    dve.tensor_tensor(kt[:, p, 0], kt[:, p, 0], S.gk[:, 0:1, span[c]].to_broadcast([P, NG, P]), ALU.mult)
                    if c == CH:
                        dve.drain()
                        for a in range(2):
                            for b in range(DEC_B):
                                dve.tensor_copy(qb[:, a, b, b * GRP:(b + 1) * GRP], qe[:, p, a, b * GRP:(b + 1) * GRP])
                    dve.drain().then_inc(s_fa, 1)

                def mask(c):
                    dve.wait_ge(s_at, c + 1)
                    for h in range(HG):
                        dve.tensor_tensor(at[:, h, :].rearrange("p (n e) -> p n e", e=GRP), attn[:, h // 2, :, h % 2, :],
                                          S.gmask[:, int(c == CH)].rearrange("p (n e) -> p n e", e=GRP), ALU.mult)
                    dve.tensor_copy(keT[:], S.ps[:, 4, 0:256].rearrange("p (a n) -> p a n", a=2))
                    dve.drain().then_inc(s_am, 1)
                    dve.wait_ge(s_o, c + 1)
                    dve.tensor_copy(S.ogla[:, c, :].rearrange("p (a b v) -> p b a v", a=2, b=2),
                                    outs.rearrange("p b (a v) -> p b a v", a=2))

                dve.memset(st[:], 0.0)
                dve.memset(qb[:], 0.0)
                dve.memset(qt[:], 0.0)
                dve.drain()
                factors(0)
                for c in range(CH):
                    factors(c + 1)
                    mask(c)
                    for a in range(2):
                        dve.scalar_tensor_tensor(st[:, a, :], st[:, a, :], eb[:, c % 2, a, P - 1:P], S.ps[:, 5 + a, 0:DVG],
                                                 ALU.mult, ALU.add)
                    dve.drain().then_inc(s_sv, 1)
                mask(CH)
                for a in range(2):
                    if a:
                        dve.wait_ge(s_kv, a)
                    for h in range(2):
                        hv = V + (2 * a + h) * DVG
                        dve.tensor_tensor(vb[:, h], S.pj[:, CH, hv:hv + DVG].unsqueeze(1).to_broadcast([P, DEC_B, DVG]),
                                          S.seqof[:].unsqueeze(2).to_broadcast([P, DEC_B, DVG]), ALU.mult)
                    dve.drain().then_inc(s_vb, 1)
                for a in range(2):
                    dve.tensor_tensor(S.gs[:, a], S.gs[:, a],
                                      eb[:, CH % 2, a, GRP - 1:64:GRP].unsqueeze(2).to_broadcast([P, DEC_B, DVG]), ALU.mult)
                dve.drain()
                dve.wait_ge(s_kv, 2)
                for a in range(2):
                    g2 = S.gs[:, a].rearrange("p b v -> p (b v)")
                    dve.tensor_tensor(g2, g2, S.ps2[:, a, :] if a == 0 else S.ps2[:, 3, :], ALU.add)
                dve.drain().then_inc(s_new, 1)

            @block.gpsimd
            def _(pool):
                for c in range(CH + 1):
                    pool.wait_ge(s_ex, c + 1)
                    pool.tensor_tensor(kt[:, c % 2, 1], kt[:, c % 2, 1], S.gk[:, 1:2, span[c]].to_broadcast([P, NG, P]), ALU.mult)
                    pool.drain().then_inc(s_fb, 1)

            @block.scalar
            def _(act):
                for c in range(CH + 1):
                    act.wait_ge(s_df, c + 1)
                    act.activation(dq[:], dq[:], ACT.Exp)
                    act.activation(de[:], de[:], ACT.Exp)
                    act.activation(eb[:, c % 2], S.gb[:, :, span[c]], ACT.Exp)
                    act.activation(kt[:, c % 2], kt[:, c % 2], ACT.Exp)
                    act.drain().then_inc(s_ex, 1)

            @block.tensor
            def _(pe):
                for c in range(CH + 1):
                    p = c % 2
                    pe.wait_ge(s_fa, c + 1)
                    for a in range(2):
                        if a:
                            pe.wait_ge(s_fb, c + 1)
                        for i in range(NG):
                            pe.matmul(attn[:, a, i, :, :].rearrange("p h e -> p (h e)"), kt[:, p, a, i, :],
                                      qt[:, p, a, i, :, :].rearrange("p h e -> p (h e)"), start=True, stop=True)
                    for a in range(2):
                        mm = pe.transpose(S.ps[:, 4, a * P:(a + 1) * P], ke[:, p, a, :], S.ident[:])
                    mm.then_inc(s_at, 1)
                    pe.wait_ge(s_am, c + 1)
                    if c > 0:
                        pe.wait_ge(s_sv, min(c, CH))
                    for h in range(HG):
                        a, r = h // 2, slice(64 * (h % 2), 64 * (h % 2) + 64)
                        v = S.pj[:, c, V + h * DVG:V + (h + 1) * DVG]
                        out = outs[:, h % 2, a * DVG:(a + 1) * DVG]
                        pe.matmul(out, at[:, h, :], v, start=True, stop=False)
                        if c < CH:
                            mm = pe.matmul(out, qe[r, p, a, :], st[r, a, :], start=False, stop=True)
                            pe.matmul(S.ps[r, 5 + a, 0:DVG], keT[:, a, r], v, start=True, stop=True)
                        else:
                            for b in range(DEC_B):
                                mm = pe.matmul(out, qb[r, a, b, :], S.gs[r, a, b, :], start=False, stop=(b == DEC_B - 1))
                    pe.drain().then_inc(s_o, 1)
                for a in range(2):
                    pe.wait_ge(s_vb, a + 1)
                    out = S.ps2[:, 0, :] if a == 0 else S.ps2[:, 3, :]
                    for h in range(2):
                        for w in range(2):
                            mm = pe.matmul(out[64 * h:64 * h + 64, w * 512:(w + 1) * 512], keT[:, a, 64 * h:64 * h + 64],
                                           vb[:, h, 4 * w:4 * w + 4, :].rearrange("p b v -> p (b v)"), start=True, stop=True)
                    mm.then_inc(s_kv, 1)

            @block.sync
            def _(sp):
                sp.wait_ge(s_sv, CH)
                sp.dma_start(S.gla_prompt[0].rearrange("(a h) k v -> (h k) a v", a=2), st[:]).then_inc(S.s_out, 16)
                sp.wait_ge(s_new, 1)
                for a in range(2):
                    sp.dma_start(S.gla_sample.rearrange("b (a h) k v -> a (h k) b v", a=2)[a], S.gs[:, a]).then_inc(S.s_out, 16)
                S.n_out += 3
                sp.wait_ge(S.s_out, 16 * S.n_out)


def gla_finish(nc, S):
    with ExitStack() as ctx:
        sq = sb(nc, ctx, "gf_sq", [P, NT, HG * DVG])
        gain = sb(nc, ctx, "gf_gain", [P, DVG])
        st = sb(nc, ctx, "gf_st", [P, 2, NT, HG])
        s_ld = nc.alloc_semaphore("gf_loaded")
        s_inv = nc.alloc_semaphore("gf_inverse_ready")
        s_rt = nc.alloc_semaphore("gf_root_ready")
        o4 = S.ogla.rearrange("p t (h v) -> p t h v", h=HG)
        q4 = sq[:].rearrange("p t (h v) -> p t h v", h=HG)
        with nc.Block() as block:
            @block.sync
            def _(sp):
                sp.dma_start(gain[:], S.gla_out_g.partition_broadcast(P)).then_inc(s_ld, 16)

            @block.vector
            def _(dve):
                dve.tensor_tensor(sq[:], S.ogla, S.ogla, ALU.mult)
                dve.drain()
                dve.tensor_reduce(st[:, 0], q4, X, ALU.add)
                dve.drain()
                dve.tensor_scalar(st[:, 0], st[:, 0], 1.0 / DVG, EPS, ALU.mult, ALU.add)
                dve.drain()
                dve.reciprocal(st[:, 0], st[:, 0]).then_inc(s_inv, 1)
                dve.wait_ge(s_rt, 1)
                dve.tensor_tensor(o4, o4, st[:, 1].unsqueeze(3).to_broadcast([P, NT, HG, DVG]), ALU.mult)
                dve.drain()
                dve.wait_ge(s_ld, 16)
                dve.tensor_tensor(o4, o4, gain[:].unsqueeze(1).unsqueeze(1).to_broadcast([P, NT, HG, DVG]), ALU.mult)
                dve.wait_ge(s_rt, 2)
                dve.drain()
                dve.tensor_tensor(S.ogla, S.ogla, sq[:], ALU.mult)

            @block.scalar
            def _(act):
                act.wait_ge(s_inv, 1)
                act.activation(st[:, 1], st[:, 0], ACT.Sqrt).then_inc(s_rt, 1)
                act.activation(sq[:], part(S, "rg"), ACT.Silu).then_inc(s_rt, 1)


def mix_out(nc, S):
    with ExitStack() as ctx:
        w = sb(nc, ctx, "w_out_sb", [P, KD, D])
        mixT = sb(nc, ctx, "mixT", [P, KD, TOK])
        gcol = sb(nc, ctx, "mo_gain", [P, KD])
        st = sb(nc, ctx, "mo_st", [P, 2, NT])
        junk = sb(nc, ctx, "mo_junk", [P, H * DK])
        s_w = nc.alloc_semaphore("mo_loaded")
        s_g = nc.alloc_semaphore("mo_gains_loaded")
        s_z = nc.alloc_semaphore("mo_zeroed")
        s_sum = nc.alloc_semaphore("mo_squares_summed")
        s_ms = nc.alloc_semaphore("mo_mean_ready")
        s_rs = nc.alloc_semaphore("mo_rstd_ready")
        s_xn = nc.alloc_semaphore("mo_scaled")
        s_tr = nc.alloc_semaphore("mo_chunk_transposed")
        s_ev = nc.alloc_semaphore("mo_chunk_moved")
        s_mm = nc.alloc_semaphore("mo_bank_ready")
        s_free = nc.alloc_semaphore("mo_bank_free")
        with nc.Block() as block:
            @block.sync
            def _(sp):
                with nc.allow_non_contiguous_dma(reason="512 gains, one per partition and chunk"):
                    sp.dma_start(gcol[:, 0:4], S.nsa_out_g.rearrange("(k p) -> p k", p=P)).then_inc(s_g, 16)
                sp.dma_start(S.x1[:, 0:4, :], S.x_prompt[0].rearrange("(t p) d -> p t d", p=P)).then_inc(s_w, 16)
                sp.dma_start(S.iota[:], S.c_iota[:, :]).then_inc(s_w, 16)
                for k in range(KD):
                    sp.dma_start(w[:, k, :], S.w_out[k * P:(k + 1) * P, :]).then_inc(s_w, 16)
                sp.wait_ge(s_z, 1)
                sp.dma_start(S.x1[0:64, 4, :], S.x_sample.rearrange("b t d -> (b t) d")).then_inc(s_w, 16)

            @block.scalar
            def _(act):
                for t in range(NT):
                    act.activation(junk[:], S.onsa[:, t, :], ACT.Square, accum_out=st[:, 0, t:t + 1])
                    act.drain()
                act.drain().then_inc(s_sum, 1)
                act.wait_ge(s_ms, 1)
                act.activation(st[:, 0, :], st[:, 1, :], ACT.Sqrt).then_inc(s_rs, 1)
                act.wait_ge(s_g, 16)
                for k in range(KD):
                    act.wait_ge(s_tr, k + 1)
                    act.activation(mixT[:, k, :], S.ps2[:, k % 4, 0:TOK], ACT.Copy,
                                   scale=gcol[:, k:k + 1] if k < 4 else 1.0).then_inc(s_ev, 1)

            @block.vector
            def _(dve):
                dve.memset(S.x1[:, 4, :], 0.0).then_inc(s_z, 1)
                dve.sem_inc(s_free, NT)
                dve.wait_ge(s_sum, 1)
                dve.tensor_scalar(st[:, 1, :], st[:, 0, :], 1.0 / (H * DK), EPS, ALU.mult, ALU.add)
                dve.drain()
                dve.reciprocal(st[:, 1, :], st[:, 1, :]).then_inc(s_ms, 1)
                dve.wait_ge(s_rs, 1)
                for t in range(NT):
                    dve.tensor_scalar(S.onsa[:, t, :], S.onsa[:, t, :], st[:, 0, t:t + 1], None, ALU.mult)
                dve.drain().then_inc(s_xn, 1)
                dve.wait_ge(s_w, 16 * (KD + 3))
                with dve.Fori(0, 2) as c:
                    for t in range(NT):
                        dve.wait_ge(s_mm, c * NT + t + 1)
                        x = S.x1[:, t, bass.ds(c * 512, 512)]
                        dve.tensor_tensor(x, S.ps[:, t, :], x, ALU.add).then_inc(s_free, 1)

            @block.tensor
            def _(pe):
                pe.wait_ge(s_xn, 1)
                for k in range(KD):
                    if k >= 4:
                        pe.wait_ge(s_ev, k - 3)
                    for t in range(NT):
                        tr = pe.transpose(S.ps2[:, k % 4, t * P:(t + 1) * P], S.mix[:, t, k * P:(k + 1) * P], S.ident[:])
                    tr.then_inc(s_tr, 1)
                pe.wait_ge(s_ev, KD)
                pe.wait_ge(s_w, 16 * (KD + 3))
                with pe.Fori(0, 2) as c:
                    for t in range(NT):
                        pe.wait_ge(s_free, c * NT + t + 1)
                        for k in range(KD):
                            mm = pe.matmul(S.ps[:, t, :], mixT[:, k, t * P:(t + 1) * P], w[:, k, bass.ds(c * 512, 512)],
                                           start=(k == 0), stop=(k == KD - 1))
                        mm.then_inc(s_mm, 1)


ROWS = [P] * (NT - 1) + [DEC_B * DEC_T]
GONE = -3e38


def peer_select(nc, S):
    HALF = PQ // 2
    with ExitStack() as ctx:
        wq = sb(nc, ctx, "ps_wq", [P, 2, KD, PQ])
        kk = sb(nc, ctx, "ps_keys", [P, 2, 2, HALF])
        kT = sb(nc, ctx, "ps_keysT", [P, 2, NKEY])
        gcol = sb(nc, ctx, "ps_gain", [P, 2])
        qg = sb(nc, ctx, "ps_qg", [P, 2, NTOK])
        sq = sb(nc, ctx, "ps_sq", [P, 2, NTOK])
        rs = sb(nc, ctx, "ps_rs", [P, 2, NT])
        sc = sb(nc, ctx, "ps_scores", [P, NT, 2, NKEY])
        sc2 = sb(nc, ctx, "ps_scores_rest", [P, NT, 2, NKEY])
        val = sb(nc, ctx, "ps_val", [P, NT, 2, TOPK])
        idx = sb(nc, ctx, "ps_idx", [P, NT, 2, TOPK], U32)
        idf = sb(nc, ctx, "ps_idf", [P, NT, 2, TOPK])
        cand = sb(nc, ctx, "ps_cand", [P, NT, TOPK, TOPK])
        cand2 = sb(nc, ctx, "ps_cand_rest", [P, NT, TOPK, TOPK])
        best = sb(nc, ctx, "ps_best", [P, NT, TOPK])
        ci = sb(nc, ctx, "ps_ci", [P, NT, TOPK], U32)
        cab = sb(nc, ctx, "ps_cab", [P, 2, NT, TOPK], U32)
        caf = sb(nc, ctx, "ps_caf", [P, 2, NT, TOPK])
        hot = sb(nc, ctx, "ps_hot", [P, NT * TOPK, TOPK])
        s_g = nc.alloc_semaphore("ps_gain_loaded")
        s_ld = [nc.alloc_semaphore("ps_even_head_loaded"), nc.alloc_semaphore("ps_odd_head_loaded")]
        s_q = nc.alloc_semaphore("ps_query_summed")
        s_qg = nc.alloc_semaphore("ps_query_scaled")
        s_sq = nc.alloc_semaphore("ps_squares_ready")
        s_ke = nc.alloc_semaphore("ps_keys_moved")
        s_ss = nc.alloc_semaphore("ps_squares_summed")
        s_iv = nc.alloc_semaphore("ps_inverse_ready")
        s_rt = nc.alloc_semaphore("ps_root_ready")
        s_sc = nc.alloc_semaphore("ps_scores_summed")
        s_sv = nc.alloc_semaphore("ps_scores_moved")
        score = S.ps[:, 4:7, :].rearrange("p a (b n) -> p (a b) n", b=2)
        with nc.Block() as block:
            @block.sync
            def _(sp):
                with nc.allow_non_contiguous_dma(reason="256 gains, one per partition and half"):
                    sp.dma_start(gcol[:], S.peer_qn_g.rearrange("(a p) -> p a", p=P)).then_inc(s_g, 16)
                with sp.Fori(0, PH // 2) as i:
                    for par in range(2):
                        h = i * 2 + par
                        sp.wait_ge(s_sv, h + 1)
                        sp.dma_start(wq[:, par], S.peer_wq[:, bass.ds(h * PQ, PQ)].rearrange("(k p) n -> p k n", p=P)).then_inc(s_ld[par], 16)
                        sp.dma_start(kk[:, par, 0], S.peer_k1[bass.ds(h, 1)].rearrange("a k d -> (a k) d")).then_inc(s_ld[par], 16)
                        sp.dma_start(kk[:, par, 1], S.peer_k2[bass.ds(h, 1)].rearrange("a k d -> (a k) d")).then_inc(s_ld[par], 16)

            @block.tensor
            def _(pe):
                with pe.Fori(0, PH // 2) as i:
                    for par in range(2):
                        n = i * 2 + par + 1
                        pe.wait_ge(s_ld[par], (i + 1) * 48)
                        for a in range(2):
                            for lo, hi in ((0, SEQ), (SEQ, NTOK)):
                                for k in range(KD):
                                    mm = pe.matmul(S.ps2[:, a, lo:hi], wq[:, par, k, a * HALF:(a + 1) * HALF],
                                                   S.h2T[:, k, lo:hi], start=(k == 0), stop=(k == KD - 1))
                        for a in range(2):
                            tr = pe.transpose(S.ps[:, 1, (a + 2) * P:(a + 3) * P], kk[:, par, a], S.ident[:])
                        tr.then_inc(s_q, 1)
                        pe.wait_ge(s_sv, n + 1)
                        pe.wait_ge(s_sq, n)
                        for t, m in enumerate(ROWS):
                            for a in range(2):
                                mm = pe.matmul(S.ps[0:m, 7, 256 + t:257 + t], sq[:, a, t * P:t * P + m], S.ones[:],
                                               start=(a == 0), stop=(a == 1))
                        mm.then_inc(s_ss, 1)
                        pe.wait_ge(s_ke, n)
                        pe.wait_ge(s_qg, n)
                        for t, m in enumerate(ROWS):
                            for a in range(2):
                                mm = pe.matmul(score[0:m, t, a * NKEY:(a + 1) * NKEY], qg[:, a, t * P:t * P + m], kT[:, a],
                                               start=True, stop=True)
                        mm.then_inc(s_sc, 1)

            @block.scalar
            def _(act):
                act.wait_ge(s_g, 16)
                with act.Fori(0, PH) as h:
                    act.wait_ge(s_q, h + 1)
                    act.activation(sq[:], S.ps2[:, 0:2, 0:NTOK], ACT.Square).then_inc(s_sq, 1)
                    for a in range(2):
                        act.activation(qg[:, a, :], S.ps2[:, a, 0:NTOK], ACT.Copy, scale=gcol[:, a:a + 1])
                    act.drain().then_inc(s_qg, 1)
                    act.activation(kT[:], S.ps[:, 1, 256:512].rearrange("p (a n) -> p a n", a=2), ACT.Copy).then_inc(s_ke, 1)
                    act.wait_ge(s_iv, h + 1)
                    act.activation(rs[:, 1, :], rs[:, 0, :], ACT.Sqrt).then_inc(s_rt, 1)

            @block.vector
            def _(dve):
                for buf in (rs, sc, sc2, val, idf, cand, cand2, best):
                    dve.memset(buf[:], 0.0)
                dve.memset(idx[:], 0)
                dve.memset(ci[:], 0)
                dve.drain()
                dve.sem_inc(s_sv, 2)
                def query(h):
                    dve.wait_ge(s_ss, h + 1)
                    for rows, t0, t1 in ((P, 0, NT - 1), (ROWS[-1], NT - 1, NT)):
                        dve.tensor_scalar(rs[0:rows, 0, t0:t1], S.ps[0:rows, 7, 256 + t0:256 + t1], 1.0 / PQ, EPS, ALU.mult, ALU.add)
                    dve.drain()
                    dve.reciprocal(rs[:, 0, 0:NT - 1], rs[:, 0, 0:NT - 1])
                    dve.reciprocal(rs[0:ROWS[-1], 0, NT - 1:NT], rs[0:ROWS[-1], 0, NT - 1:NT])
                    dve.drain().then_inc(s_iv, 1)

                def head(h, more):
                    dve.wait_ge(s_sc, h + 1)
                    dve.wait_ge(s_rt, h + 1)
                    for rows, t0, t1 in ((P, 0, NT - 1), (ROWS[-1], NT - 1, NT)):
                        dve.tensor_tensor(sc[0:rows, t0:t1].rearrange("p t a n -> p t (a n)"), score[0:rows, t0:t1, :],
                                          rs[0:rows, 1, t0:t1].unsqueeze(2).to_broadcast([rows, t1 - t0, 2 * NKEY]), ALU.mult)
                    dve.drain().then_inc(s_sv, 1)
                    top16(dve, [(sc[0:m, t, a], sc2[0:m, t, a], val[0:m, t, a], idx[0:m, t, a])
                                for t, m in enumerate(ROWS) for a in range(2)])
                    dve.tensor_copy(idf[:], idx[:])
                    for t in range(NT):
                        dve.tensor_tensor(cand[:, t], val[:, t, 0].unsqueeze(2).to_broadcast([P, TOPK, TOPK]),
                                          val[:, t, 1].unsqueeze(1).to_broadcast([P, TOPK, TOPK]), ALU.add)
                    dve.drain()
                    if more:
                        query(h + 1)
                    top16(dve, [(cand[0:m, t].rearrange("p a b -> p (a b)"), cand2[0:m, t].rearrange("p a b -> p (a b)"),
                                 best[0:m, t], ci[0:m, t]) for t, m in enumerate(ROWS)])
                    dve.tensor_scalar(cab[:, 0], ci[:], 4, None, ALU.logical_shift_right)
                    dve.tensor_scalar(cab[:, 1], ci[:], 15, None, ALU.bitwise_and)
                    dve.tensor_copy(S.best[:, :, bass.ds(h, 1), :].rearrange("p t h k -> p t (h k)"), best[:])
                    dve.drain()
                    dve.tensor_copy(caf[:], cab[:])
                    dve.drain()
                    for a in range(2):
                        dve.tensor_tensor(hot[:], caf[:, a].rearrange("p t k -> p (t k)").unsqueeze(2).to_broadcast([P, NT * TOPK, TOPK]),
                                          S.iota[:, 0:TOPK].unsqueeze(1).to_broadcast([P, NT * TOPK, TOPK]), ALU.is_equal)
                        dve.drain()
                        h4 = hot[:].rearrange("p (t k) r -> p t k r", t=NT)
                        dve.tensor_tensor(h4, h4, idf[:, :, a].unsqueeze(2).to_broadcast([P, NT, TOPK, TOPK]), ALU.mult)
                        dve.drain()
                        dve.tensor_reduce(S.sel[:, a, :, bass.ds(h, 1), :].rearrange("p t h k -> p t (h k)"), h4, X, ALU.add)
                        dve.drain()

                query(0)
                with dve.Fori(0, PH - 1) as h:
                    head(h, True)
                head(PH - 1, False)


def top16(dve, lists):
    for src, rest, val, idx in lists:
        dve.max(val[:, 0:8], src)
    dve.drain()
    for src, rest, val, idx in lists:
        dve.max_index(idx[:, 0:8], val[:, 0:8], src)
        dve.match_replace(rest, val[:, 0:8], src, GONE)
    dve.drain()
    for src, rest, val, idx in lists:
        dve.max(val[:, 8:16], rest)
    dve.drain()
    for src, rest, val, idx in lists:
        dve.max_index(idx[:, 8:16], val[:, 8:16], rest)
    dve.drain()


def peer_gates(nc, S):
    with ExitStack() as ctx:
        s1 = sb(nc, ctx, "pg_sum", [P, NT * PH])
        s_df = nc.alloc_semaphore("pg_shifted")
        s_ex = nc.alloc_semaphore("pg_exp_ready")
        s_gt = nc.alloc_semaphore("pg_gates_ready")
        s_tr = nc.alloc_semaphore("pg_block_transposed")
        s_ev = nc.alloc_semaphore("pg_block_moved")
        b3 = S.best[:].rearrange("p t h k -> p (t h) k")
        srcs = [S.sel[:, 0], S.sel[:, 1], S.best[:]]
        with nc.Block() as block:
            @block.vector
            def _(dve):
                dve.tensor_tensor(S.gate16[:], b3, b3[:, :, 0:1].to_broadcast([P, NT * PH, TOPK]), ALU.subtract).then_inc(s_df, 1)
                dve.wait_ge(s_ex, 1)
                dve.tensor_reduce(s1[:], S.gate16[:], X, ALU.add)
                dve.drain()
                dve.reciprocal(s1[:], s1[:])
                dve.drain()
                dve.tensor_tensor(b3, S.gate16[:], s1[:].unsqueeze(2).to_broadcast([P, NT * PH, TOPK]), ALU.mult).then_inc(s_gt, 1)
                for i in range(3):
                    dve.wait_ge(s_tr, i + 1)
                    dve.tensor_copy(S.selT[:, i, :], S.ps2[:, i, 0:NTOK]).then_inc(s_ev, 1)

            @block.scalar
            def _(act):
                act.wait_ge(s_df, 1)
                act.activation(S.gate16[:], S.gate16[:], ACT.Exp).then_inc(s_ex, 1)

            @block.tensor
            def _(pe):
                pe.wait_ge(s_gt, 1)
                for i, src in enumerate(srcs):
                    for t in range(NT):
                        tr = pe.transpose(S.ps2[:, i, t * P:(t + 1) * P], src[:, t].rearrange("p h k -> p (h k)"), S.ident[:])
                    tr.then_inc(s_tr, 1)


NBLK = 64
BLOCKS = NTOK // NBLK


def peer_gate_matrix(nc, S):
    STEP = 8
    ITS = NBLK // (2 * STEP)
    with ExitStack() as ctx:
        o1 = sb(nc, ctx, "gm_one_hot1", [P, 2, STEP, NKEY])
        o2 = sb(nc, ctx, "gm_gated_hot2", [P, 2, STEP, NKEY])
        gt = sb(nc, ctx, "gm_block", [P, 3, NKEY, NBLK])
        s_o1 = nc.alloc_semaphore("gm_one_hot1_ready")
        s_o2 = nc.alloc_semaphore("gm_gated_hot2_ready")
        s_mm = nc.alloc_semaphore("gm_bank_ready")
        s_ev = nc.alloc_semaphore("gm_bank_moved")
        s_st = [nc.alloc_semaphore(f"gm_block{i}_stored") for i in range(3)]
        with nc.Block() as block:
            @block.vector
            def _(dve):
                dve.sem_inc(s_mm, 4)
                with dve.Fori(0, NTOK // (2 * STEP)) as i:
                    for par in range(2):
                        m = i * 2 + par
                        dve.wait_ge(s_mm, m * 2 + 2)
                        dve.tensor_tensor(o1[:, par], S.selT[:, 0, bass.ds(m * STEP, STEP)].unsqueeze(2).to_broadcast([P, STEP, NKEY]),
                                          S.iota[:].unsqueeze(1).to_broadcast([P, STEP, NKEY]), ALU.is_equal).then_inc(s_o1, 1)
                        for j in range(STEP):
                            n = m * STEP + j
                            dve.tensor_scalar(o2[:, par, j], S.iota[:], S.selT[:, 1, bass.ds(n, 1)],
                                              S.selT[:, 2, bass.ds(n, 1)], ALU.is_equal, ALU.mult).then_inc(s_o2, 1)

            @block.tensor
            def _(pe):
                with pe.Fori(0, NTOK // (2 * STEP)) as i:
                    for par in range(2):
                        m = i * 2 + par
                        pe.wait_ge(s_o1, m + 1)
                        for half in range(2):
                            pe.wait_ge(s_o2, m * STEP + half * 4 + 4)
                            pe.wait_ge(s_ev, m * 2 + half + 1)
                            for j in range(4):
                                mm = pe.matmul(S.ps[:, par * 2 + half, j * P:(j + 1) * P], o1[:, par, half * 4 + j],
                                               o2[:, par, half * 4 + j], start=True, stop=True)
                            mm.then_inc(s_mm, 1)

            @block.scalar
            def _(act):
                act.sem_inc(s_ev, 4)
                with act.Fori(0, BLOCKS // 3) as b:
                    for part in range(3):
                        act.wait_ge(s_st[part], b * 16 + 16)
                        with act.Fori(0, ITS) as i:
                            for q in range(4):
                                act.wait_ge(s_mm, (b * 3 + part) * 4 * ITS + i * 4 + q + 5)
                                act.activation(gt[:, part, :, bass.ds(i * 2 * STEP + q * 4, 4)],
                                               S.ps[:, q, :].rearrange("p (j n) -> p n j", j=4), ACT.Copy).then_inc(s_ev, 1)

            @block.sync
            def _(sp):
                for part in range(3):
                    sp.sem_inc(s_st[part], 16)
                with sp.Fori(0, BLOCKS // 3) as b:
                    for part in range(3):
                        sp.wait_ge(s_ev, (b * 3 + part) * 4 * ITS + 4 * ITS + 4)
                        sp.dma_start(S.gm_dram[bass.ds(b * 3 + part, 1)].rearrange("a p i n -> p (a i n)"),
                                     gt[:, part].rearrange("p i n -> p (i n)")).then_inc(s_st[part], 16)
                for part in range(3):
                    sp.wait_ge(s_st[part], 16 * (BLOCKS // 3 + 1))


def peer_experts(nc, S):
    GS = 2
    NG = NKEY // GS
    HALF = NTOK // 2
    PASSES = [(0, 0), (0, 1), (1, 0)]
    with ExitStack() as ctx:
        hs = sb(nc, ctx, "pe_h_parts", [P, 2, KD, NTOK], F32R)
        free = S.mix[:].rearrange("p t d -> p (t d)")
        u = free[:, 0:2 * GS * D].rearrange("p (g s d) -> p g s d", g=2, s=GS)
        w = free[:, 2 * GS * D:2 * GS * D + NTOK]
        v = sb(nc, ctx, "pe_v", [P, 2, GS, D])
        g = sb(nc, ctx, "pe_g", [P, 2, BLOCKS, GS, NBLK])
        uT = sb(nc, ctx, "pe_uT_parts", [P, 2, 2, KD, P], F32R)
        vs = sb(nc, ctx, "pe_v_parts", [P, 2, 2, GS, D], F32R)
        act_ = sb(nc, ctx, "pe_act", [P, 2, NTOK])
        ws = sb(nc, ctx, "pe_w_parts", [P, 2, 2, GS, NTOK], F32R)
        s_u = [nc.alloc_semaphore(f"pe_u_and_gates{i}_loaded") for i in range(2)]
        s_v = [nc.alloc_semaphore(f"pe_v{i}_loaded") for i in range(2)]
        s_hh = nc.alloc_semaphore("pe_h_high_ready")
        s_hl = nc.alloc_semaphore("pe_h_low_ready")
        s_tr = nc.alloc_semaphore("pe_half_turned")
        s_uh = nc.alloc_semaphore("pe_uT_high_ready")
        s_ul = nc.alloc_semaphore("pe_uT_low_ready")
        s_vh = nc.alloc_semaphore("pe_v_high_ready")
        s_vl = nc.alloc_semaphore("pe_v_low_ready")
        s_h = nc.alloc_semaphore("pe_products_summed")
        s_ge = nc.alloc_semaphore("pe_gelu_ready")
        s_wg = nc.alloc_semaphore("pe_gates_applied")
        s_w = nc.alloc_semaphore("pe_weights_ready")
        s_y = nc.alloc_semaphore("pe_output_summed")
        s_ya = nc.alloc_semaphore("pe_output_added")
        units = [(t, c) for t in range(NT) for c in range(2)]
        NU = len(units)
        share = [range(0, NU // 2), range(NU // 2, NU)]
        out_bank = lambda i, par: 4 + (i + par * NU) % 4
        u_v = S.peer_u.rearrange("(p s) d -> p s d", p=P)
        v_v = S.peer_v.rearrange("(p s) d -> p s d", p=P)

        with nc.Block() as block:
            @block.sync
            def _(sp):
                def load(gr, par):
                    sp.dma_start(u[:, par], u_v[:, bass.ds(gr * GS, GS), :]).then_inc(s_u[par], 16)
                    sp.dma_start(g[:, par].rearrange("p b s n -> p b (s n)"),
                                 S.gm_dram[:, :, bass.ds(gr * GS, GS), :].rearrange("b p s n -> p b (s n)")).then_inc(s_u[par], 16)
                    sp.dma_start(v[:, par], v_v[:, bass.ds(gr * GS, GS), :]).then_inc(s_v[par], 16)

                def refill(gr, par):
                    sp.wait_ge(s_tr, (gr - 1) * 2 * GS)
                    sp.wait_ge(s_wg, (gr - 1) * GS)
                    sp.wait_ge(s_vl, (gr - 1) * GS)
                    load(gr, par)

                load(0, 0)
                load(1, 1)
                with sp.Fori(0, NG // 2 - 1) as it:
                    refill(it * 2 + 2, 0)
                    refill(it * 2 + 3, 1)
                sp.wait_ge(s_ya, NG * NU + 4)
                sp.dma_start(S.y_prompt[0].rearrange("(t p) d -> p t d", p=P), S.x1[:, 0:NT - 1, :]).then_inc(S.s_out, 16)
                sp.dma_start(S.y_sample.rearrange("b t d -> (b t) d"), S.x1[0:64, NT - 1, :]).then_inc(S.s_out, 16)
                sp.wait_ge(S.s_out, 16 * (S.n_out + 2))

            @block.tensor
            def _(pe):
                def turn(n, par, s):
                    pe.wait_ge(s_ul, n * 2 + 1)
                    for k in range(KD):
                        tr = pe.transpose(S.ps[:, k // 4, (k % 4) * P:(k % 4 + 1) * P], u[:, par, s, k * P:(k + 1) * P], S.ident[:])
                        if k % 4 == 3:
                            tr.then_inc(s_tr, 1)

                def products(n, s):
                    pe.wait_ge(s_ul, n * 2 + 3)
                    pe.wait_ge(s_ge, n + 1)
                    for half in range(2):
                        out = S.ps[:, 2 + half, 0:HALF]
                        for k in range(KD):
                            for a, b in PASSES:
                                mm = pe.matmul(out, uT[:, s, a, k, :], hs[:, b, k, half * HALF:(half + 1) * HALF],
                                               start=(k == 0 and a == b), stop=(k == KD - 1 and a == 1))
                    mm.then_inc(s_h, 1)

                def output(gr, par, picks):
                    for i in picks:
                        t, c = units[i]
                        m = ROWS[t]
                        pe.wait_ge(s_ya, gr * NU + i + 1)
                        for s in range(GS):
                            for a, b in PASSES:
                                mm = pe.matmul(S.ps[0:m, out_bank(i, par), :], ws[:, par, a, s, t * P:t * P + m],
                                               vs[:, par, b, s, c * 512:(c + 1) * 512],
                                               start=(s == 0 and a == b), stop=(s == GS - 1 and a == 1))
                        mm.then_inc(s_y, 1)

                def group(gr, par, fills, prev, last=False):
                    for s in range(GS):
                        n = gr * GS + s
                        if s < GS - 1:
                            turn(n + 1, par, s + 1)
                        elif not last:
                            pe.wait_ge(s_u[1 - par], fills * 32)
                            turn(n + 1, 1 - par, 0)
                        products(n, s)
                        if prev is not None:
                            if s == 0:
                                pe.wait_ge(s_w, gr * GS)
                                pe.wait_ge(s_vl, gr * GS)
                            output(prev, 1 - par, share[s])

                pe.wait_ge(s_hl, 1)
                pe.wait_ge(s_u[0], 32)
                turn(0, 0, 0)
                group(0, 0, 1, None)
                with pe.Fori(0, NG // 2 - 1) as it:
                    group(it * 2 + 1, 1, it + 2, it * 2)
                    group(it * 2 + 2, 0, it + 2, it * 2 + 1)
                group(NG - 1, 1, 0, NG - 2, last=True)
                pe.wait_ge(s_w, NG * GS)
                pe.wait_ge(s_vl, NG * GS)
                output(NG - 1, 1, range(NU))

            @block.scalar
            def _(act):
                def high(n, slot):
                    for half in range(2):
                        act.wait_ge(s_tr, n * 2 + half + 1)
                        act.activation(uT[:, slot, 0, half * 4:half * 4 + 4, :].rearrange("p k n -> p (k n)"),
                                       S.ps[:, half, :], ACT.Copy).then_inc(s_uh, 1)

                def group(gr, par, fills, free, last=False):
                    for s in range(GS):
                        n = gr * GS + s
                        if not (last and s == GS - 1):
                            high(n + 1, 1 - s)
                        act.wait_ge(s_h, n + 1)
                        if free:
                            act.wait_ge(s_wg, n - 1)
                        act.activation(act_[:, s, :].rearrange("p (h n) -> p h n", h=2),
                                       S.ps[:, 2:4, 0:HALF], ACT.Gelu).then_inc(s_ge, 1)
                        if s == 0:
                            act.wait_ge(s_v[par], fills * 16)
                            if free:
                                act.wait_ge(s_ya, (gr - 1) * NU + 4)
                        act.activation(vs[:, par, 0, s, :], v[:, par, s, :], ACT.Copy).then_inc(s_vh, 1)

                act.sem_inc(s_ge, 1)
                act.activation(hs[:, 0], S.h2T[:, :, 0:NTOK], ACT.Copy).then_inc(s_hh, 1)
                high(0, 0)
                group(0, 0, 1, False)
                with act.Fori(0, NG // 2 - 1) as it:
                    group(it * 2 + 1, 1, it + 1, True)
                    group(it * 2 + 2, 0, it + 2, True)
                group(NG - 1, 1, NG // 2, True, last=True)

            @block.gpsimd
            def _(pool):
                def group(gr, par):
                    for s in range(GS):
                        pool.wait_ge(s_vh, gr * GS + s + 1)
                        pool.tensor_tensor(vs[:, par, 1, s, :], v[:, par, s, :], vs[:, par, 0, s, :].bitcast(F32), ALU.subtract).then_inc(s_vl, 1)

                with pool.Fori(0, NG // 2) as it:
                    group(it * 2, 0)
                    group(it * 2 + 1, 1)

            @block.vector
            def _(dve):
                def low(n, slot):
                    for half in range(2):
                        dve.wait_ge(s_uh, n * 2 + half + 1)
                        dve.tensor_tensor(uT[:, slot, 1, half * 4:half * 4 + 4, :].rearrange("p k n -> p (k n)"), S.ps[:, half, :],
                                          uT[:, slot, 0, half * 4:half * 4 + 4, :].rearrange("p k n -> p (k n)").bitcast(F32),
                                          ALU.subtract).then_inc(s_ul, 1)

                def add(gr, par, picks):
                    for i in picks:
                        t, c = units[i]
                        m = ROWS[t]
                        dve.wait_ge(s_y, gr * NU + i + 1)
                        x = S.x1[0:m, t, c * 512:(c + 1) * 512]
                        dve.tensor_tensor(x, S.ps[0:m, out_bank(i, par), :], x, ALU.add).then_inc(s_ya, 1)

                def group(gr, par, fills, prev, last=False):
                    for s in range(GS):
                        n = gr * GS + s
                        if not (last and s == GS - 1):
                            low(n + 1, 1 - s)
                        if s == 0:
                            dve.wait_ge(s_u[par], fills * 32)
                        dve.wait_ge(s_ge, n + 2)
                        dve.tensor_tensor(w.rearrange("p (b n) -> p b n", b=BLOCKS),
                                          act_[:, s, :].rearrange("p (b n) -> p b n", b=BLOCKS),
                                          g[:, par, :, s, :], ALU.mult)
                        dve.drain().then_inc(s_wg, 1)
                        dve.tensor_copy(ws[:, par, 0, s, :], w)
                        dve.drain()
                        dve.tensor_tensor(ws[:, par, 1, s, :], w, ws[:, par, 0, s, :].bitcast(F32), ALU.subtract)
                        dve.drain().then_inc(s_w, 1)
                        if prev is not None:
                            add(prev, 1 - par, share[s])

                dve.sem_inc(s_ul, 1)
                dve.sem_inc(s_ya, 4)
                dve.wait_ge(s_hh, 1)
                dve.tensor_tensor(hs[:, 1], S.h2T[:, :, 0:NTOK], hs[:, 0].bitcast(F32), ALU.subtract).then_inc(s_hl, 1)
                low(0, 0)
                group(0, 0, 1, None)
                with dve.Fori(0, NG // 2 - 1) as it:
                    group(it * 2 + 1, 1, it + 1, it * 2)
                    group(it * 2 + 2, 0, it + 2, it * 2 + 1)
                group(NG - 1, 1, NG // 2, NG - 2, last=True)
                add(NG - 1, 1, range(NU))


def constants():
    d = DMAX - np.arange(LVEC)
    n = np.maximum(d, 0)
    exact = NB // 2
    nf = np.maximum(n, exact).astype(np.float32)
    large = exact + (np.log(nf / np.float32(exact)) / np.float32(np.log(MAXD / exact)) * np.float32(NB - exact)).astype(np.int32)
    bucket = np.where(n < exact, n, np.minimum(large, NB - 1))
    oh = np.zeros((NB + 1, LVEC), np.float32)
    oh[bucket, np.arange(LVEC)] = 1.0
    oh[:NB, d < 0] = 0.0
    oh[NB, d < 0] = 1.0
    tok = np.arange(P)
    rows = (tok // 32) * 8 + tok % 8
    misc = np.zeros((P, 40), np.float32)
    misc[:, 0] = tok >= 2 * STRIDE - 1
    misc[:, 1:9] = np.where(np.arange(8)[None] <= (tok % 8)[:, None], NEG, 0.0)
    misc[:, 16:33] = np.arange(17)
    at = np.arange(TOK)
    reset = np.where(at < SEQ, at % P, at % DEC_T) > 0
    causal = tok[:, None] <= tok[None]
    gmask = np.stack([causal, causal & (tok[:, None] // DEC_T == tok[None] // DEC_T)])
    seqof = tok[:, None] // DEC_T == np.arange(DEC_B)[None]
    flips = np.stack([np.eye(P)[::-1], np.kron(np.eye(P // 8), np.eye(8)[::-1])]).astype(np.float32)
    return {"c_reset": reset.astype(np.float32), "c_gmask": gmask.astype(np.float32),
            "c_seqof": seqof.astype(np.float32), "c_flips": flips, "c_ident": np.eye(P, dtype=np.float32), "c_bucket": oh,
            "c_sub": (tok[:, None] // STRIDE == np.arange(NSUB)[None]).astype(np.float32),
            "c_group": (rows[:, None] == rows[None]).astype(np.float32), "c_misc": misc,
            "c_iota": np.tile(np.arange(NKEY, dtype=np.float32), (P, 1))}


INPUTS = ["x_prompt", "x_sample", "cache_kv", "cache_win", "state_gla", "page_table", "norm1_g", "w_in", "qn_g",
          "kn_cmp_g", "kn_slc_g", "kn_win_g", "cmp_w_pos", "cmp_proj", "rel_bias", "nsa_gate_b", "nsa_out_g",
          "gla_a_up", "gla_a_b", "gla_out_g", "w_out", "norm2_g", "peer_wq", "peer_qn_g", "peer_k1", "peer_k2",
          "peer_u", "peer_v"]
CONSTANTS = ["c_reset", "c_gmask", "c_seqof", "c_flips", "c_ident", "c_bucket", "c_sub", "c_group", "c_misc", "c_iota"]
OUTPUTS = [("y_prompt", (1, SEQ, D)), ("y_sample", (DEC_B, DEC_T, D)), ("kv_prompt", (1, SEQ, 4, G, DK)),
           ("kv_sample", (DEC_B, DEC_T, 4, G, DK)), ("win_prompt", (1, WIN, 2, G, DK)),
           ("win_sample", (DEC_B, WIN, 2, G, DK)), ("gla_prompt", (1, HG, DKG, DVG)),
           ("gla_sample", (DEC_B, HG, DKG, DVG))]
SCRATCH = [("rv", (H, LVEC)), ("gate", (DEC_B * DEC_T, 3 * H)), ("gm", (BLOCKS, P, NKEY, NBLK)), ("osa", (DEC_B, DEC_T, H, DK))]


def program(nc, S):
    with ExitStack() as ctx:
        S.ident = sb(nc, ctx, "ident", [P, P])
        S.ones = sb(nc, ctx, "ones", [P, 1])
        S.gains = sb(nc, ctx, "gains", [P, 4, DK])
        S.gates = sb(nc, ctx, "gates", [P, NT, 3 * H])
        S.ps = ctx.enter_context(nc.psum_tensor("ps", [P, 8, 512], F32))
        S.ps2 = S.ps[:].rearrange("p (a b) n -> p a (b n)", b=2)
        S.mix = sb(nc, ctx, "mix", [P, NT, D])
        S.onsa, S.ogla = S.mix[:, :, 0:H * DK], S.mix[:, :, H * DK:D]
        S.x = S.mix
        with ExitStack() as c0:
            token_mixers(nc, S, c0)
        S.iota = sb(nc, ctx, "iota", [P, NKEY])
        S.x1 = sb(nc, ctx, "x1", [P, NT, D])
        mix_out(nc, S)
        S.h2T = sb(nc, ctx, "h2T", [P, KD, TOK])
        norm_transposed(nc, S, "norm2", S.x1, S.mix, S.norm2_g, S.h2T)
        with ExitStack() as c0:
            S.selT = sb(nc, c0, "selT", [P, 3, NTOK])
            with ExitStack() as c1:
                S.best = sb(nc, c1, "best", [P, NT, PH, TOPK])
                S.sel = sb(nc, c1, "sel", [P, 2, NT, PH, TOPK])
                S.gate16 = sb(nc, c1, "gate16", [P, NT * PH, TOPK])
                peer_select(nc, S)
                peer_gates(nc, S)
            peer_gate_matrix(nc, S)
        peer_experts(nc, S)


def token_mixers(nc, S, ctx):
    S.pj = sb(nc, ctx, "pj", [P, NT, D_IN])
    load_start(nc, S)
    project_in(nc, S)
    with ExitStack() as c2:
        S.qT = sb(nc, c2, "qT", [P, 4, TOK])
        S.ksT = sb(nc, c2, "ksT", [P, TOK])
        S.kwT = sb(nc, c2, "kwT", [P, TOK])
        S.cproj = sb(nc, c2, "cproj", [P, 2, DK])
        S.grp = sb(nc, c2, "grp", [P, P])
        S.misc = sb(nc, c2, "misc", [P, 40])
        S.w16 = sb(nc, c2, "w16", [P, 4, 2, NSUB])
        S.sbias = sb(nc, c2, "sbias", [P, PAST + DEC_T])
        S.grow = sb(nc, c2, "grow", [P, 4, 3])
        with ExitStack() as c3:
            S.toep = sb(nc, c3, "toep", [P, H, 512])
            S.vc = sb(nc, c3, "vc", [32, P])
            S.kcT = sb(nc, c3, "kcT", [P, 32])
            with ExitStack() as c4:
                S.qp = sb(nc, c4, "qp", [P, NT, H * DK])
                S.gate_hj = sb(nc, c4, "gate_hj", [P, 3 * H])
                setup_buffers(nc, S, c4)
                head_norms(nc, S)
                attention_setup(nc, S)
            load_pages(nc, S, c3)
            prompt_compress(nc, S)
            prompt_attention(nc, S)
            sample_attention(nc, S)
    with ExitStack() as c2:
        S.gq = sb(nc, c2, "gq", [P, 2, TOK])
        S.gk = sb(nc, c2, "gk", [P, 2, TOK])
        S.gb = sb(nc, c2, "gb", [P, 2, TOK])
        S.gs = sb(nc, c2, "gs", [P, 2, DEC_B, DVG])
        S.gmask = sb(nc, c2, "gmask", [P, 2, P])
        S.seqof = sb(nc, c2, "seqof", [P, DEC_B])
        gla_inputs(nc, S)
        gla_chunks(nc, S)
    gla_finish(nc, S)


def kernel(**inputs):
    import numpy as _np
    import concourse.bacc as _bacc
    from concourse.bass_utils import run_bass_kernel_spmd as _run

    nc = _bacc.Bacc("TRN2", target_bir_lowering=False, num_devices=1)
    arrays = {name: _np.ascontiguousarray(inputs[name]) for name in INPUTS}
    arrays.update(constants())
    dram = {name: nc.dram_tensor("in_" + name, a.shape, mybir.dt.from_np(a.dtype), kind="ExternalInput").ap()
            for name, a in arrays.items()}
    S = Shared()
    (S.x_prompt, S.x_sample, S.cache_kv, S.cache_win, S.state_gla, S.page_table, S.norm1_g, S.w_in, S.qn_g,
     S.kn_cmp_g, S.kn_slc_g, S.kn_win_g, S.cmp_w_pos, S.cmp_proj, S.rel_bias, S.nsa_gate_b, S.nsa_out_g,
     S.gla_a_up, S.gla_a_b, S.gla_out_g, S.w_out, S.norm2_g, S.peer_wq, S.peer_qn_g, S.peer_k1, S.peer_k2,
     S.peer_u, S.peer_v) = (dram[n] for n in INPUTS)
    (S.c_reset, S.c_gmask, S.c_seqof, S.c_flips, S.c_ident, S.c_bucket, S.c_sub, S.c_group, S.c_misc, S.c_iota) = (dram[n] for n in CONSTANTS)
    (S.y_prompt, S.y_sample, S.kv_prompt, S.kv_sample, S.win_prompt, S.win_sample, S.gla_prompt, S.gla_sample) = (nc.dram_tensor("out_" + n, shape, F32, kind="ExternalOutput").ap() for n, shape in OUTPUTS)
    (S.rv_t, S.gate_t, S.gm_t, S.osa_t) = (nc.dram_tensor(n, shape, F32, kind="Internal") for n, shape in SCRATCH)
    S.rv_dram = S.rv_t.ap()
    S.gate_dram = S.gate_t.ap()
    S.gm_dram = S.gm_t.ap()
    S.osa_dram = S.osa_t.ap()
    program(nc, S)
    r = _run(nc, [{"in_" + name: a for name, a in arrays.items()}], core_ids=[0])
    return tuple(r.results[0]["out_" + name] for name, _ in OUTPUTS)
```
